# Optimizing a Trainium2 kernel written in Bass

```python
import math
import jax, jax.numpy as jnp
from jax import lax
import numpy as np

D_MODEL = 1024
BATCH = 1
SEQ = 2048
DEPTH = 1

CHUNK = 64
Q_BLOCK = 128
EPS = 1e-6
FOX_HEADS = 8
FOX_HD = 64
FOX_W = FOX_HEADS * FOX_HD
MLA_HEADS = 8
MLA_NOPE = 64
MLA_ROPE = 32
MLA_V = 64
Q_LORA = 256
KV_LORA = 128
ROPE_THETA = 10000.0
MLA_W = MLA_HEADS * MLA_V
MIX_W = FOX_W + MLA_W
IN_SIZES = (FOX_W, FOX_W, FOX_W, FOX_HEADS, Q_LORA, KV_LORA, MLA_ROPE)
IN_COLS = int(sum(IN_SIZES))
IN_SPLITS = [int(s) for s in np.cumsum(IN_SIZES)[:-1]]
D_FF = 4 * D_MODEL

kernel_name = "hymba_fox_mla_sqrelu_block"

def _rmsnorm(x, g):
    xf = x.astype(jnp.float32)
    y = xf * lax.rsqrt(jnp.mean(xf * xf, axis=-1, keepdims=True) + EPS)
    return (y * g.astype(jnp.float32)).astype(x.dtype)

def _rope(x, pos):
    half = x.shape[-1] // 2
    inv = ROPE_THETA ** (-jnp.arange(half, dtype=jnp.float32) / half)
    ang = pos.astype(jnp.float32)[:, None] * inv[None, :]
    cos = jnp.cos(ang).astype(x.dtype)
    sin = jnp.sin(ang).astype(x.dtype)
    x1, x2 = x[..., :half], x[..., half:]
    return jnp.concatenate([x1 * cos - x2 * sin, x2 * cos + x1 * sin], axis=-1)

def _block_sweep(q, k, v, block_bias, scale):
    b, h, s, dk = q.shape
    nb = s // Q_BLOCK
    qb = q.reshape(b, h, nb, Q_BLOCK, dk).transpose(2, 0, 1, 3, 4)

    def one(args):
        i, qi = args
        logits = jnp.einsum('bhqd,bhkd->bhqk', qi, k).astype(jnp.float32) * scale
        probs = jax.nn.softmax(logits + block_bias(i), axis=-1)
        return jnp.einsum('bhqk,bhkd->bhqd', probs.astype(v.dtype), v)

    out = lax.map(one, (jnp.arange(nb), qb))
    return out.transpose(1, 2, 0, 3, 4).reshape(b, h, s, v.shape[-1])

def _hybrid_mixer(h, pos, w_in, b_f, g_q, w_q_up, g_kv, w_kv_up, w_o):
    b, s, _ = h.shape
    p = jnp.einsum('bsd,dc->bsc', h, w_in)
    fq, fk, fv, f_logit, q_lat, kv_lat, k_rope_raw = jnp.split(p, IN_SPLITS, axis=-1)
    kpos = jnp.arange(s)

    def heads(t, nh):
        return t.reshape(b, s, nh, -1).transpose(0, 2, 1, 3)
    fq, fk, fv = heads(fq, FOX_HEADS), heads(fk, FOX_HEADS), heads(fv, FOX_HEADS)
    log_f = jax.nn.log_sigmoid((f_logit + b_f).astype(jnp.float32))
    logcum = jnp.cumsum(log_f, axis=1).transpose(0, 2, 1)

    def fox_bias(i):
        start = i * Q_BLOCK
        cq = lax.dynamic_slice_in_dim(logcum, start, Q_BLOCK, axis=2)
        qpos = start + jnp.arange(Q_BLOCK)
        mask = kpos[None, :] <= qpos[:, None]
        return jnp.where(mask, cq[..., None] - logcum[:, :, None, :], -jnp.inf)

    o_fox = _block_sweep(fq, fk, fv, fox_bias, 1.0 / math.sqrt(FOX_HD))

    cq = jnp.einsum('bsr,rc->bsc', _rmsnorm(q_lat, g_q), w_q_up)
    cq = heads(cq, MLA_HEADS)
    q_mla = jnp.concatenate([cq[..., :MLA_NOPE], _rope(cq[..., MLA_NOPE:], pos)], axis=-1)
    ckv = jnp.einsum('bsr,rc->bsc', _rmsnorm(kv_lat, g_kv), w_kv_up)
    ckv = heads(ckv, MLA_HEADS)
    k_nope, v_mla = ckv[..., :MLA_NOPE], ckv[..., MLA_NOPE:]
    k_rope = _rope(k_rope_raw, pos)[:, None]
    k_mla = jnp.concatenate(
        [k_nope, jnp.broadcast_to(k_rope, (b, MLA_HEADS, s, MLA_ROPE))], axis=-1)

    def chunk_bias(i):
        qpos = i * Q_BLOCK + jnp.arange(Q_BLOCK)
        mask = (kpos // CHUNK)[None, :] <= (qpos // CHUNK)[:, None]
        return jnp.where(mask, jnp.float32(0.0), jnp.float32(-jnp.inf))[None, None]

    o_mla = _block_sweep(q_mla, k_mla, v_mla, chunk_bias,
                         1.0 / math.sqrt(MLA_NOPE + MLA_ROPE))

    o = jnp.concatenate([o_fox, o_mla], axis=1)
    o = o.transpose(0, 2, 1, 3).reshape(b, s, MIX_W)
    return jnp.einsum('bsc,cd->bsd', o, w_o)

def setup_inputs(seed: int = 0) -> dict:
    key = jax.random.key(seed)
    ks = jax.random.split(key, 16)
    L = DEPTH

    def w(k, shape, fan_in):
        return jax.random.normal(k, shape, jnp.float32) * fan_in ** -0.5

    def gain(k, shape):
        return 1.0 + 0.05 * jax.random.normal(k, shape, jnp.float32)

    return {
        "x": jax.random.normal(ks[0], (BATCH, SEQ, D_MODEL), jnp.float32),
        "g_mix": gain(ks[1], (L, D_MODEL)),
        "w_in": w(ks[2], (L, D_MODEL, IN_COLS), D_MODEL),
        "b_f": 3.0 + 0.5 * jax.random.normal(ks[3], (L, FOX_HEADS), jnp.float32),
        "g_q": gain(ks[4], (L, Q_LORA)),
        "w_q_up": w(ks[5], (L, Q_LORA, MLA_HEADS * (MLA_NOPE + MLA_ROPE)), Q_LORA),
        "g_kv": gain(ks[6], (L, KV_LORA)),
        "w_kv_up": w(ks[7], (L, KV_LORA, MLA_HEADS * (MLA_NOPE + MLA_V)), KV_LORA),
        "w_o": w(ks[8], (L, MIX_W, D_MODEL), MIX_W),
        "g_mlp": gain(ks[9], (L, D_MODEL)),
        "w_ff1": w(ks[10], (L, D_MODEL, D_FF), D_MODEL),
        "w_ff2": w(ks[11], (L, D_FF, D_MODEL), D_FF),
        "g_final": gain(ks[12], (D_MODEL,)),
    }

def reference(x, g_mix, w_in, b_f, g_q, w_q_up, g_kv, w_kv_up, w_o,
              g_mlp, w_ff1, w_ff2, g_final):
    pos = jnp.arange(x.shape[1])
    for l in range(DEPTH):
        h = _rmsnorm(x, g_mix[l])
        x = x + _hybrid_mixer(h, pos, w_in[l], b_f[l], g_q[l], w_q_up[l],
                              g_kv[l], w_kv_up[l], w_o[l])
        h2 = _rmsnorm(x, g_mlp[l])
        u = jnp.einsum('bsd,df->bsf', h2, w_ff1[l])
        x = x + jnp.einsum('bsf,fd->bsd', jnp.square(jax.nn.relu(u)), w_ff2[l])
    return _rmsnorm(x, g_final)


_drawn_inputs = setup_inputs


def setup_inputs(seed=0):
    import zlib

    import numpy as np

    out = dict(_drawn_inputs(seed))
    spreads = {}
    factors = {'g_mix': 2.825, 'g_q': 8.0, 'g_kv': 8.0, 'g_mlp': 4.827}
    for name, (base, spread) in spreads.items():
        noise = np.random.default_rng([zlib.crc32(name.encode()), seed]).standard_normal(out[name].shape)
        drawn = base * np.exp(spread * noise) if base else spread * noise
        out[name] = __import__('jax').numpy.asarray(drawn.astype(out[name].dtype))
    for name, factor in factors.items():
        out[name] = (out[name] * factor).astype(out[name].dtype)
    return out
```

```python
from contextlib import ExitStack

import numpy as np
import concourse.bass as bass
from concourse import mybir

F32 = mybir.dt.float32
F32R = mybir.dt.float32r
BF16 = mybir.dt.bfloat16
ALU = mybir.AluOpType
ACT = mybir.ActivationFunctionType
AX_X = mybir.AxisListType.X

P = 128
SEQ, D_MODEL, D_FF = 2048, 1024, 4096
HEADS, HD = 8, 64
ROPE = 32
MLA_K = HD + ROPE
CHUNK = 64
EPS = 1e-6
ROPE_THETA = 10000.0
Q_LORA, KV_LORA = 256, 128

KC = D_MODEL // P
BT = 1024
NB = SEQ // BT
HALF = 512
TT = BT // P
LATS = (Q_LORA + KV_LORA) // P
RAW = 2
RING = 4
AHEAD = 1

ROW_Q, ROW_K = 0, HEADS * HD
ROW_QN, ROW_KN = 2 * HEADS * HD, 3 * HEADS * HD
ROW_QR1 = 4 * HEADS * HD
ROW_QR2 = ROW_QR1 + HEADS * ROPE // 2
ROW_KR1 = ROW_QR2 + HEADS * ROPE // 2
ROW_KR2 = ROW_KR1 + ROPE // 2
ROWS = ROW_KR2 + ROPE // 2
AUG = 4
MISC_KR1, MISC_KR2 = 32, 64

PROJ_TILES = 19
GROUP = 4
GROUPS = D_FF // P // GROUP
WO_TILES = D_MODEL // P
GROUP_TILES = 2 * GROUP
FIN_TILES = WO_TILES + GROUPS * GROUP_TILES


class Chain:

    def __init__(self, eng, sem, base, total):
        self.eng, self.sem, self.base, self.total, self.n = eng, sem, base, total, 0

    def __call__(self, instruction):
        self.n += 1
        instruction.then_inc(self.sem, 1)
        self.eng.wait_ge(self.sem, self.base + self.n)

    def close(self):
        assert self.n == self.total, (self.n, self.total)


def half(n):
    return slice(n * HALF, (n + 1) * HALF)


def project(nc, x_t, wproj, gains, lat_gains, gate_bias, cos_t, sin_t, ident, signs,
            feat, v_fox, v_mla, aug_q, aug_k):
    with ExitStack() as ctx:
        def sb(name, shape, dt=F32):
            return ctx.enter_context(nc.sbuf_tensor("p_" + name, shape, dt))

        def ps(name, shape):
            return ctx.enter_context(nc.psum_tensor("p_" + name, shape, F32))

        def sem(name):
            return ctx.enter_context(nc.semaphore("p_" + name))

        XRING = 4
        x_sb = sb("x", [P, XRING, BT])
        act_hi, act_lo = sb("act_hi", [P, KC, BT], F32R), sb("act_lo", [P, KC, BT], F32R)
        w_raw = sb("w_raw", [P, RAW, BT])
        w_hi, w_lo = sb("w_hi", [P, RING, BT], F32R), sb("w_lo", [P, RING, BT], F32R)
        stage = sb("stage", [P, 2, BT])
        rstd = sb("rstd", [P, 2, BT])
        RSTD_OF = {"x": 0, "q": 1, "kv": 0}
        lat = sb("lat", [P, LATS, BT])
        lat_hi, lat_lo = sb("lat_hi", [P, LATS, BT], F32R), sb("lat_lo", [P, LATS, BT], F32R)
        trig = sb("trig", [P, 2, BT])
        square, sumsq, diag = sb("square", [P, BT]), sb("sumsq", [P, BT]), sb("diag", [P, BT])
        misc = sb("misc", [P, 3, BT])
        gate, rot = misc[0:HEADS], misc[MISC_KR1:MISC_KR1 + ROPE // 2]
        small = sb("small", [P, 4, TT])
        rstd_t = sb("rstd_t", [P, 3, TT])
        carry = sb("carry", [HEADS, 1])
        ones = sb("ones", [P, P])
        ident_sb = sb("ident", [P, P])
        gains_sb, lat_gains_sb = sb("gains", [P, KC]), sb("lat_gains", [P, LATS])
        bias_sb, scale_sb = sb("bias", [HEADS, 1]), sb("scale", [P, 2])

        pairs = ps("pairs", [P, 2, 2, HALF])
        ps_sum = ps("sum", [P, HALF])
        ps_row = ps("row", [P, 2, HALF])

        const_landed, consts_set = sem("const_landed"), sem("consts_set")
        x_landed = [sem(f"x_landed{i}") for i in range(XRING)]
        w_landed = [sem(f"w_landed{i}") for i in range(RAW)]
        trig_landed = sem("trig_landed")
        x_split, square_done, sumsq_step = sem("x_split"), sem("square_done"), sem("sumsq_step")
        act_ready = sem("act_ready")
        w_half, w_ready = sem("w_half"), sem("w_ready")
        pair_done, pair_read = sem("pair_done"), sem("pair_read")
        sums_done, var_done, dev_done = sem("sums_done"), sem("var_done"), sem("dev_done")
        diag_done, row_done, rstd_done = sem("diag_done"), sem("row_done"), sem("rstd_done")
        lat_split, lat_ready = sem("lat_split"), sem("lat_ready")
        gate_in, gate_log, gate_done, rope_done = sem("gate_in"), sem("gate_log"), sem("gate_done"), sem("rope_done")
        act_step, dve_step = sem("act_step"), sem("dve_step")
        stored = [sem(f"stored{i}") for i in range(2)]
        misc_stored, ones_stored, q_rope_stored = sem("misc_stored"), sem("ones_stored"), sem("q_rope_stored")

        V_PAIRS = TT // 2
        QN_PAIRS, KN_PAIRS = HEADS * HD // P, HEADS * HD // P
        N_PAIRS = 4 + 8 + V_PAIRS + QN_PAIRS + 2 + KN_PAIRS + V_PAIRS
        N_STAGED = N_PAIRS - 4 - 2
        N_SQUARES = KC + LATS
        V_DONE = 12 + V_PAIRS
        USED = {i: i + 1 for i in range(12)} | {i: V_DONE for i in range(12, 16)}
        USED |= {12: 14, 13: 14, 16: V_DONE + QN_PAIRS, 17: V_DONE + QN_PAIRS + 2, 18: N_PAIRS}
        SLOT_LOADS = [len(range(s, PROJ_TILES, RAW)) for s in range(RAW)]
        NORMS = ("x", "q", "kv")

        with nc.Block() as block:
            @block.sync
            def _(sp):
                for count in (*stored, q_rope_stored, misc_stored):
                    sp.sem_inc(count, AHEAD)
                def load_w(b, i, j=0):
                    sp.wait_ge(w_ready, AHEAD + b * PROJ_TILES + (j * 4 + (i - RAW + 1) if i >= RAW else 0))
                    slot = i % RAW
                    src = wproj[i] if isinstance(j, int) else wproj[bass.ds(j * 4 + i, 1)].rearrange("o p c -> p (o c)")
                    sp.dma_start(w_raw[:, slot, :], src).then_inc(w_landed[slot], 16)

                def store(b, n, dst, j=0, tokens=0):
                    read = n + 4 if n < 8 + V_PAIRS + QN_PAIRS else n + 6
                    sp.wait_ge(pair_read, AHEAD + b * N_PAIRS + j * 4 + read + 1)
                    src = stage[:, n % 2, :]
                    src = src.rearrange("p (t c) -> p t c", t=tokens) if tokens else src
                    sp.dma_start(dst, src).then_inc(stored[n % 2], 16)

                for dst, src in ((ident_sb[:, :], ident), (gains_sb[:, :], gains), (lat_gains_sb[:, :], lat_gains),
                                 (bias_sb[:, :], gate_bias), (scale_sb[:, :], signs["scale"])):
                    sp.dma_start(dst, src).then_inc(const_landed, 16)
                for h in range(HEADS):
                    sp.dma_start(aug_q[h, 2:4, :], signs["minus"]).then_inc(ones_stored, 16)
                    sp.dma_start(aug_k[h, 0:2, :], signs["plus"]).then_inc(ones_stored, 16)
                with sp.Fori(0, NB) as b:
                    tok = bass.ds(b * BT, BT)
                    for c in range(KC):
                        sp.wait_ge(sumsq_step, AHEAD + b * N_SQUARES + max(c - XRING + 1, 0))
                        sp.dma_start(x_sb[:, c % XRING, :], x_t[c * P:(c + 1) * P, tok]).then_inc(x_landed[c % XRING], 16)
                        if c < RAW:
                            load_w(b, c)
                    sp.wait_ge(rope_done, AHEAD + b * 2)
                    sp.dma_start(trig[:, 0, :], cos_t[:, tok]).then_inc(trig_landed, 16)
                    sp.dma_start(trig[:, 1, :], sin_t[:, tok]).then_inc(trig_landed, 16)
                    for i in range(RAW, 4 + RAW):
                        load_w(b, i)
                    with sp.Fori(0, 2) as j:
                        for s in range(4):
                            load_w(b, 4 + RAW + s, j)
                            store(b, s, feat[bass.ds(j * (4 * P) + s * P, P), tok], j)
                    for i in range(14, 18):
                        load_w(b, i)
                    sp.wait_ge(gate_done, b + 1)
                    for n, plane in enumerate((2, 0)):
                        sp.dma_start(aug_q[:, n, tok], gate[:, plane, :]).then_inc(misc_stored, 16)
                        sp.dma_start(aug_k[:, 2 + n, tok], gate[:, plane, :]).then_inc(misc_stored, 16)
                    sp.wait_ge(rope_done, AHEAD + b * 2 + 1)
                    sp.dma_start(feat[ROW_KR1:ROW_KR1 + ROPE // 2, tok], rot[:, 2, :]).then_inc(misc_stored, 16)
                    sp.dma_start(feat[ROW_KR2:ROW_KR2 + ROPE // 2, tok], rot[:, 0, :]).then_inc(misc_stored, 16)
                    n = 8
                    for m in range(V_PAIRS):
                        cols = slice(m // 2 * 2 * P, (m // 2 + 1) * 2 * P)
                        store(b, n, v_fox[bass.ds(b * TT + m % 2 * 4, 4), :, cols].rearrange("t p c -> p t c"), tokens=4)
                        n += 1
                    load_w(b, 18)
                    for m in range(QN_PAIRS):
                        store(b, n, feat[ROW_QN + m * P:ROW_QN + (m + 1) * P, tok])
                        n += 1
                    for m in range(KN_PAIRS):
                        store(b, n, feat[ROW_KN + m * P:ROW_KN + (m + 1) * P, tok])
                        n += 1
                    for m in range(V_PAIRS):
                        store(b, n, v_mla[bass.ds(b * TT + 2 * m, 2)].rearrange("t p c -> p t c"), tokens=2)
                        n += 1
                    sp.wait_ge(rope_done, AHEAD + b * 2 + 2)
                    sp.dma_start(feat[ROW_QR1:ROW_QR1 + P, tok], lat[:, 2, :]).then_inc(q_rope_stored, 16)
                    sp.dma_start(feat[ROW_QR2:ROW_QR2 + P, tok], lat[:, 0, :]).then_inc(q_rope_stored, 16)
                for s in range(2):
                    sp.wait_ge(stored[s], AHEAD + 16 * NB * (N_STAGED // 2))
                sp.wait_ge(misc_stored, AHEAD + 16 * 6 * NB)
                sp.wait_ge(q_rope_stored, AHEAD + 16 * 2 * NB)
                sp.wait_ge(ones_stored, 16 * 2 * HEADS)

            @block.gpsimd
            def _(pool):
                for count in (w_ready,):
                    pool.sem_inc(count, AHEAD)
                pool.wait_ge(consts_set, 1)
                with pool.Fori(0, NB) as b:
                    for i in range(PROJ_TILES):
                        raw, slot = i % RAW, i % RING
                        pool.wait_ge(w_landed[raw], b * (16 * SLOT_LOADS[raw]) + 16 * (i // RAW + 1))
                        pool.wait_ge(pair_done, AHEAD + b * N_PAIRS + (USED[i - RING] if i >= RING else 0))
                        nc.gpsimd.tensor_tensor(w_hi[:, slot, :], w_raw[:, raw, :], ones[:, 0:1].to_broadcast([P, BT]),
                                                ALU.mult).then_inc(w_half, 1)
                        pool.wait_ge(w_half, b * PROJ_TILES + i + 1)
                        nc.gpsimd.tensor_tensor(w_lo[:, slot, :], w_raw[:, raw, :], w_hi[:, slot, :].bitcast(F32),
                                                ALU.subtract).then_inc(w_ready, 1)

            @block.scalar
            def _(act):
                for count in (rstd_done,):
                    act.sem_inc(count, AHEAD)
                def deviation(b, norm):
                    n = NORMS.index(norm)
                    act.wait_ge(var_done, b * 3 + n + 1)
                    nc.scalar.activation(small[:, 1, :], small[:, 0, :], ACT.Sqrt).then_inc(dev_done, 1)
                    act.wait_ge(row_done, AHEAD + b * 3 + n + 1)
                    nc.scalar.activation(rstd[:, RSTD_OF[norm], :], ps_row[:, :, :].rearrange("p a c -> p (a c)"),
                                         ACT.Copy).then_inc(rstd_done, 1)

                def squared(b, n, src):
                    act.wait_ge(sumsq_step, AHEAD + b * N_SQUARES + n)
                    nc.scalar.activation(square[:, :], src, ACT.Square).then_inc(square_done, 1)

                act.wait_ge(const_landed, 16 * 5)
                with act.Fori(0, NB) as b:
                    act.wait_ge(pair_done, AHEAD + b * N_PAIRS)
                    for c in range(KC):
                        act.wait_ge(x_landed[c % XRING], b * (16 * KC // XRING) + 16 * (c // XRING + 1))
                        nc.scalar.activation(act_hi[:, c, :], x_sb[:, c % XRING, :], ACT.Identity,
                                             scale=gains_sb[:, c:c + 1]).then_inc(x_split, 1)
                        squared(b, c, x_sb[:, c % XRING, :])
                    deviation(b, "x")
                    for i in range(LATS):
                        act.wait_ge(pair_read, AHEAD + b * N_PAIRS + i + 1)
                        nc.scalar.activation(lat_hi[:, i, :], lat[:, i, :], ACT.Identity,
                                             scale=lat_gains_sb[:, i:i + 1]).then_inc(lat_split, 1)
                        squared(b, KC + i, lat[:, i, :])
                    act.wait_ge(gate_in, b + 1)
                    nc.scalar.activation(gate[:, 1, :], gate[:, 1, :], ACT.Exp).then_inc(act_step, 1)
                    act.wait_ge(act_step, b + 1)
                    nc.scalar.activation(gate[:, 1, :], gate[:, 1, :], ACT.Ln, bias=1.0).then_inc(gate_log, 1)
                    deviation(b, "q")
                    deviation(b, "kv")

            @block.vector
            def _(dve):
                for count in (sumsq_step, rope_done, pair_read):
                    dve.sem_inc(count, AHEAD)
                STEPS = 3 * 5 + 1 + 2 * 3 + 3
                dve.wait_ge(const_landed, 16 * 5)
                nc.vector.memset(carry[:, :], 0.0)
                nc.vector.memset(ones[:, :], 1.0).then_inc(consts_set, 1)
                dve.wait_ge(consts_set, 1)
                with dve.Fori(0, NB) as b:
                    link = Chain(dve, dve_step, b * STEPS, STEPS)

                    def add_square(n, first):
                        dve.wait_ge(square_done, b * N_SQUARES + n + 1)
                        if first:
                            op = nc.vector.tensor_copy(sumsq[:, :], square[:, :])
                        else:
                            dve.wait_ge(sumsq_step, AHEAD + b * N_SQUARES + n)
                            op = nc.vector.tensor_tensor(sumsq[:, :], sumsq[:, :], square[:, :], ALU.add)
                        op.then_inc(sumsq_step, 1)

                    def reciprocal_root(norm, width):
                        n = NORMS.index(norm)
                        dve.wait_ge(sums_done, b * 3 + n + 1)
                        var, dev, a = small[:, 0, :], small[:, 1, :], small[:, 2, :]
                        nc.vector.tensor_scalar(var, ps_sum[:, n * TT:(n + 1) * TT], 1.0 / width, EPS,
                                                ALU.mult, ALU.add).then_inc(var_done, 1)
                        dve.wait_ge(dev_done, b * 3 + n + 1)
                        r = rstd_t[:, n, :]
                        link(nc.vector.reciprocal(r, dev))
                        link(nc.vector.tensor_tensor(a, r, r, ALU.mult))
                        link(nc.vector.tensor_tensor(a, a, var, ALU.mult))
                        link(nc.vector.tensor_scalar(a, a, -0.5, 1.5, ALU.mult, ALU.add))
                        link(nc.vector.tensor_tensor(r, r, a, ALU.mult))
                        dve.wait_ge(row_done, AHEAD + b * 3 + n)
                        nc.vector.tensor_tensor(
                            diag[:, :].rearrange("p (t c) -> p t c", t=TT),
                            ident_sb[:, :].unsqueeze(1).to_broadcast([P, TT, P]),
                            r.unsqueeze(2).to_broadcast([P, TT, P]), ALU.mult).then_inc(diag_done, 1)

                    def pair(n, j=0):
                        dve.wait_ge(pair_done, AHEAD + b * N_PAIRS + j * 4 + n + 1)
                        return pairs[:, n % 2, :, :].rearrange("p a c -> p (a c)")

                    def free_stage(n, j=0):
                        dve.wait_ge(stored[n % 2], AHEAD + b * (16 * N_STAGED // 2) + j * 32 + 16 * (n // 2))

                    for c in range(KC):
                        dve.wait_ge(x_split, b * KC + c + 1)
                        nc.vector.scalar_tensor_tensor(act_lo[:, c, :], x_sb[:, c % XRING, :], gains_sb[:, c:c + 1],
                                                       act_hi[:, c, :].bitcast(F32), ALU.mult,
                                                       ALU.subtract).then_inc(act_ready, 1)
                        add_square(c, c == 0)
                    reciprocal_root("x", D_MODEL)
                    dve.wait_ge(rstd_done, AHEAD + b * 3 + 1)
                    dve.wait_ge(q_rope_stored, AHEAD + b * 32)
                    dve.wait_ge(misc_stored, AHEAD + b * 96)
                    for i in range(LATS):
                        src = pair(i)
                        nc.vector.tensor_tensor(lat[:, i, :], src, rstd[:, 0, :], ALU.mult).then_inc(pair_read, 1)
                    src = pair(LATS)
                    nc.vector.tensor_tensor(gate[:, 0, :], src[0:HEADS], rstd[0:HEADS, 0, :], ALU.mult)
                    for plane, row in enumerate((MISC_KR1, MISC_KR2)):
                        end = row + ROPE // 2
                        last = nc.vector.tensor_tensor(rot[:, plane, :], src[row:end], rstd[row:end, 0, :], ALU.mult)
                    last.then_inc(pair_read, 1)
                    dve.wait_ge(pair_read, AHEAD + b * N_PAIRS + 4)
                    for i in range(LATS):
                        dve.wait_ge(lat_split, b * LATS + i + 1)
                        nc.vector.scalar_tensor_tensor(lat_lo[:, i, :], lat[:, i, :], lat_gains_sb[:, i:i + 1],
                                                       lat_hi[:, i, :].bitcast(F32), ALU.mult,
                                                       ALU.subtract).then_inc(lat_ready, 1)
                        if i < 2:
                            add_square(KC + i, i == 0)
                    link(nc.vector.tensor_scalar(gate[:, 0, :], gate[:, 0, :], bias_sb[:, 0:1], None, ALU.add))
                    nc.vector.scalar_tensor_tensor(gate[:, 1, :], gate[:, 0, :], -1.0, gate[:, 0, :], ALU.mult,
                                                   ALU.min).then_inc(gate_in, 1)
                    dve.wait_ge(trig_landed, b * 32 + 32)

                    def rotate(x1, x2, out, tmp, cos, sin):
                        nc.vector.tensor_tensor(out, x1, cos, ALU.mult)
                        link(nc.vector.tensor_tensor(tmp, x2, sin, ALU.mult))
                        link(nc.vector.tensor_tensor(out, out, tmp, ALU.subtract))
                        nc.vector.tensor_tensor(tmp, x2, cos, ALU.mult)
                        link(nc.vector.tensor_tensor(x1, x1, sin, ALU.mult))
                        nc.vector.tensor_tensor(x1, x1, tmp, ALU.add).then_inc(rope_done, 1)

                    kr = slice(MISC_KR1, MISC_KR1 + ROPE // 2)
                    rotate(rot[:, 0, :], rot[:, 1, :], rot[:, 2, :], diag[kr, :], trig[kr, 0, :], trig[kr, 1, :])
                    dve.wait_ge(gate_log, b + 1)
                    link(nc.vector.scalar_tensor_tensor(gate[:, 0, :], gate[:, 0, :], 0.0, gate[:, 1, :], ALU.min,
                                                        ALU.subtract))
                    link(nc.vector.tensor_tensor_scan(gate[:, 1, :], gate[:, 0, :], gate[:, 0, :], carry[:, 0:1],
                                                      ALU.add, ALU.bypass))
                    nc.vector.tensor_copy(carry[:, :], gate[:, 1, BT - 1:BT])
                    link(nc.vector.tensor_copy(gate[:, 2, :].bitcast(F32R), gate[:, 1, :]))
                    nc.vector.tensor_tensor(gate[:, 0, :], gate[:, 1, :], gate[:, 2, :],
                                            ALU.subtract).then_inc(gate_done, 1)

                    with dve.Fori(0, 2) as j:
                        for s in range(4):
                            src = pair(4 + s, j)
                            free_stage(s, j)
                            nc.vector.scalar_tensor_tensor(stage[:, s % 2, :], src, scale_sb[:, bass.ds(j, 1)],
                                                           rstd[:, 0, :], ALU.mult, ALU.mult).then_inc(pair_read, 1)

                    def values(n, norm, m):
                        src = pair(n)
                        staged = n - 4 if norm == 0 else n - 6
                        free_stage(staged)
                        first, tiles = (4 * (m % 2), 4) if norm == 0 else (2 * m, 2)
                        src = src.rearrange("p (t c) -> p t c", t=tiles)
                        dst = stage[:, staged % 2, :].rearrange("p (t c) -> p t c", t=tiles)
                        for h in range(tiles):
                            last = nc.vector.tensor_scalar(dst[:, h, :], src[:, h, :],
                                                           rstd_t[:, norm, first + h:first + h + 1], None, ALU.mult)
                        last.then_inc(pair_read, 1)

                    reciprocal_root("q", Q_LORA)
                    n = 12
                    for m in range(V_PAIRS):
                        if m == 1:
                            add_square(KC + 2, True)
                        if m == 2:
                            reciprocal_root("kv", KV_LORA)
                        values(n, 0, m)
                        n += 1
                    dve.wait_ge(rstd_done, AHEAD + b * 3 + 2)
                    for m in range(QN_PAIRS + 2):
                        src = pair(n)
                        if m < QN_PAIRS:
                            free_stage(n - 4)
                            dst = stage[:, n % 2, :]
                        else:
                            dst = lat[:, m - QN_PAIRS, :]
                        nc.vector.scalar_tensor_tensor(dst, src, MLA_K ** -0.5, rstd[:, 1, :], ALU.mult,
                                                       ALU.mult).then_inc(pair_read, 1)
                        n += 1
                    dve.wait_ge(rstd_done, AHEAD + b * 3 + 3)
                    for m in range(KN_PAIRS):
                        src = pair(n)
                        free_stage(n - 6)
                        nc.vector.tensor_tensor(stage[:, n % 2, :], src, rstd[:, 0, :], ALU.mult).then_inc(pair_read, 1)
                        n += 1
                    for m in range(V_PAIRS):
                        values(n, 2, m)
                        n += 1
                    assert n == N_PAIRS
                    rotate(lat[:, 0, :], lat[:, 1, :], lat[:, 2, :], diag[:, :], trig[:, 0, :], trig[:, 1, :])
                    link.close()

            @block.tensor
            def _(pe):
                for count in (pair_done, row_done):
                    pe.sem_inc(count, AHEAD)
                def tile_product(out, w_slot, w_cols, hi, lo, chunks, paced=None):
                    for c in range(chunks):
                        if paced is not None:
                            pe.wait_ge(act_ready, paced + c + 1)
                        cols = w_cols(c)
                        for n in range(2):
                            for k, (w, a) in enumerate(((w_hi, hi), (w_hi, lo), (w_lo, hi))):
                                last = nc.tensor.matmul(out[:, n, :], w[:, w_slot, cols], a[:, c, half(n)],
                                                        start=c == 0 and k == 0, stop=c == chunks - 1 and k == 2)
                    return last

                def by_chunk(c):
                    return slice(c * P, (c + 1) * P)

                pe.wait_ge(const_landed, 16 * 5)
                pe.wait_ge(consts_set, 1)
                with pe.Fori(0, NB) as b:
                    def wait_w(i, j=0):
                        pe.wait_ge(w_ready, AHEAD + b * PROJ_TILES + j * 4 + i + 1)

                    def out(n, j=0):
                        pe.wait_ge(pair_read, AHEAD + b * N_PAIRS + (j * 4 + n - 1 if n >= 2 else 0))
                        return pairs[:, n % 2, :, :]

                    def sums(norm):
                        n = NORMS.index(norm)
                        pe.wait_ge(sumsq_step, AHEAD + b * N_SQUARES + (KC, KC + 2, KC + 3)[n])
                        for t in range(TT):
                            last = nc.tensor.matmul(ps_sum[:, n * TT + t:n * TT + t + 1], sumsq[:, t * P:(t + 1) * P],
                                                    ones[:, 0:1], start=True, stop=True)
                        last.then_inc(sums_done, 1)

                    def row(norm):
                        n = NORMS.index(norm)
                        pe.wait_ge(diag_done, b * 3 + n + 1)
                        pe.wait_ge(rstd_done, AHEAD + b * 3 + n)
                        for h in range(2):
                            last = nc.tensor.matmul(ps_row[:, h, :], ones[:, :], diag[:, half(h)], start=True, stop=True)
                        last.then_inc(row_done, 1)

                    for i in range(4):
                        wait_w(i)
                        last = tile_product(out(i), i, by_chunk, act_hi, act_lo, KC, paced=b * KC if i == 0 else None)
                        last.then_inc(pair_done, 1)
                        if i == 0:
                            sums("x")
                        if i == 1:
                            row("x")
                    with pe.Fori(0, 2) as j:
                        for s in range(4):
                            wait_w(4 + s, j)
                            tile_product(out(4 + s, j), s, by_chunk, act_hi, act_lo, KC).then_inc(pair_done, 1)
                    sums("q")
                    n = 12
                    for m in range(V_PAIRS):
                        s = 2 * (m // 2)
                        if m % 2 == 0:
                            wait_w(12 + s + 1)
                        banks = out(n)
                        for q in range(4):
                            tokens = slice((4 * (m % 2) + q) * P, (4 * (m % 2) + q + 1) * P)
                            for c in range(KC):
                                for k, (w, a) in enumerate(((w_hi, act_hi), (w_hi, act_lo), (w_lo, act_hi))):
                                    last = nc.tensor.matmul(banks[:, q // 2, q % 2 * 2 * P:(q % 2 + 1) * 2 * P],
                                                            a[:, c, tokens], w[:, s:s + 2, by_chunk(c)],
                                                            start=c == 0 and k == 0, stop=c == KC - 1 and k == 2)
                        last.then_inc(pair_done, 1)
                        n += 1
                        if m == 0:
                            row("q")
                        if m == 1:
                            sums("kv")
                        if m == 2:
                            row("kv")
                    pe.wait_ge(lat_ready, b * LATS + LATS)
                    for m in range(QN_PAIRS + 2):
                        i, at = (16, m) if m < QN_PAIRS else (17, m - QN_PAIRS)
                        if at == 0:
                            wait_w(i)
                        last = tile_product(out(n), i % RING, lambda c: slice((2 * at + c) * P, (2 * at + c + 1) * P),
                                            lat_hi, lat_lo, 2)
                        last.then_inc(pair_done, 1)
                        n += 1
                    wait_w(18)
                    for m in range(KN_PAIRS):
                        last = tile_product(out(n), 18 % RING, lambda c: slice(m * P, (m + 1) * P),
                                            lat_hi[:, 2:3, :], lat_lo[:, 2:3, :], 1)
                        last.then_inc(pair_done, 1)
                        n += 1
                    for m in range(V_PAIRS):
                        banks = out(n)
                        for h in range(2):
                            tokens = slice((2 * m + h) * P, (2 * m + h + 1) * P)
                            for k, (w, a) in enumerate(((w_hi, lat_hi), (w_hi, lat_lo), (w_lo, lat_hi))):
                                last = nc.tensor.matmul(banks[:, h, :], a[:, 2, tokens], w[:, 18 % RING, HALF:],
                                                        start=k == 0, stop=k == 2)
                        last.then_inc(pair_done, 1)
                        n += 1


def attend(nc, ident, ident_b, masks, feat, v_fox, v_mla, aug_q, aug_k, o_t):
    with ExitStack() as ctx:
        def sb(name, shape, dt=F32):
            return ctx.enter_context(nc.sbuf_tensor("a_" + name, shape, dt))

        def ps(name, shape):
            return ctx.enter_context(nc.psum_tensor("a_" + name, shape, F32))

        def sem(name):
            return ctx.enter_context(nc.semaphore("a_" + name))

        QT = SEQ // P
        KB = HALF // P
        TURNS = HEADS // 2
        TILES = [(0, i) for i in range(QT)] + [(1, i) for i in reversed(range(QT))]
        NT = len(TILES)
        CHUNKS = [i // KB + 1 for _, i in TILES]
        BEFORE = [sum(CHUNKS[:t]) for t in range(NT + 1)]
        NCH = BEFORE[-1]
        S_BANKS, T_BANKS, PT_SLOTS = 4, 2, 8
        MAX_CHUNKS = QT // KB
        O_GROUP = 4
        GROUPS_O = NT // O_GROUP
        STEPS = NT + 4

        def width(t, c):
            return min(HALF, (TILES[t][1] + 1) * P - c * HALF)

        def chunks(t):
            return CHUNKS[t] if 0 <= t < NT else 0

        qa, qb = sb("qa", [P, 2, SEQ], F32R), sb("qb", [P, 2, SEQ], F32R)
        ka, kb = sb("ka", [P, 2, SEQ], F32R), sb("kb", [P, 2, SEQ], F32R)
        q_raw, k_raw = sb("q_raw", [P, SEQ]), sb("k_raw", [P, SEQ])
        v_raw = sb("v_raw", [P, QT, HD])
        v = sb("v", [P, 2, QT, 2, HD], F32R)
        probs = sb("probs", [P, 2, SEQ])
        pt_hi, pt_lo = sb("pt_hi", [P, PT_SLOTS, KB, P], F32R), sb("pt_lo", [P, PT_SLOTS, KB, P], F32R)
        o_pair = sb("o_pair", [P, QT, 2 * HD])
        o_feat = sb("o_feat", [P, SEQ])
        part_max, neg_max = sb("part_max", [P, 2, MAX_CHUNKS]), sb("neg_max", [P, 4])
        row_sum = sb("row_sum", [P, 2, QT, MAX_CHUNKS])
        weight = sb("weight", [P, 2, O_GROUP])
        o_sum = sb("o_sum", [P, O_GROUP, HD])
        ident_sb, ident_b_sb = sb("ident", [P, P]), sb("ident_b", [P, P], BF16)
        masks_sb = sb("masks", [P, 2, P], BF16)
        ones = sb("ones", [P, 1])

        s_ps = ps("s", [P, S_BANKS, HALF])
        t_ps = ps("t", [P, T_BANKS, HALF])
        o_ps = ps("o", [P, 2, O_GROUP, 2 * HD])

        const_landed, consts_set = sem("const_landed"), sem("consts_set")
        head_landed, gates_landed = sem("head_landed"), [sem(f"gates_landed{p}") for p in range(2)]
        q_split, k_hi_done, head_split = sem("q_split"), sem("k_hi_done"), sem("head_split")
        k_copied = [sem(f"k_copied{p}") for p in range(2)]
        k_lo_done, q_lo_done, v_half = sem("k_lo_done"), sem("q_lo_done"), sem("v_half")
        scored, tile_max, exped = sem("scored"), sem("tile_max"), sem("exped")
        turned, hi_done, lo_done, weighed = sem("turned"), sem("hi_done"), sem("lo_done"), sem("weighed")
        o_read, o_turned, o_out, o_stored = sem("o_read"), sem("o_turned"), sem("o_out"), sem("o_stored")
        max_step, o_step = sem("max_step"), sem("o_step")

        with nc.Block() as block:
            @block.sync
            def _(sp):
                for dst, src in ((ident_sb[:, :], ident), (ident_b_sb[:, :], ident_b), (masks_sb[:, :, :], masks)):
                    sp.dma_start(dst, src).then_inc(const_landed, 16)

                def rows(dst, row, h, size):
                    sp.dma_start(dst, feat[bass.ds(h * size + row, size), :]).then_inc(head_landed, 16)

                with sp.Fori(0, TURNS) as it:
                    for par in range(2):
                        h = it * 2 + par
                        sp.wait_ge(head_split, AHEAD + it * 2 + par)
                        for part in range(2):
                            rows(q_raw[part * HD:(part + 1) * HD, :], ROW_Q, h, HD)
                            rows(k_raw[part * HD:(part + 1) * HD, :], ROW_K, h, HD)
                        sp.dma_start(v_raw[:, :, :], v_fox[:, :, bass.ds(h * HD, HD)].rearrange("t p d -> p t d")
                                     ).then_inc(head_landed, 16)
                        sp.wait_ge(scored, it * NCH + (NCH // 2 if par == 0 else NCH))
                        for dst, src in ((qb, aug_q), (kb, aug_k)):
                            sp.dma_start(dst[HD:HD + AUG, par, :].bitcast(F32),
                                         src[bass.ds(h, 1)].rearrange("o r n -> (o r) n")).then_inc(gates_landed[par], 16)
                        sp.wait_ge(k_hi_done, it * 2 + par + 1)
                        sp.dma_start(kb[0:HD, par, :].bitcast(F32), ka[0:HD, par, :].bitcast(F32)).then_inc(k_copied[par], 16)
                with sp.Fori(0, TURNS) as it:
                    for par in range(2):
                        h = it * 2 + par
                        sp.wait_ge(head_split, AHEAD + it * 2 + HEADS + par)
                        rows(q_raw[0:HD, :], ROW_QN, h, HD)
                        rows(q_raw[HD:HD + 16, :], ROW_QR1, h, 16)
                        rows(q_raw[HD + 16:MLA_K, :], ROW_QR2, h, 16)
                        rows(k_raw[0:HD, :], ROW_KN, h, HD)
                        sp.dma_start(k_raw[HD:MLA_K, :], feat[ROW_KR1:ROW_KR1 + ROPE, :]).then_inc(head_landed, 16)
                        sp.dma_start(v_raw[:, :, :], v_mla[:, :, bass.ds(h * HD, HD)].rearrange("t p d -> p t d")
                                     ).then_inc(head_landed, 16)

            @block.gpsimd
            def _(pool):
                for count in (head_split,):
                    pool.sem_inc(count, AHEAD)
                pool.wait_ge(consts_set, 1)

                def fox(it, par):
                    n = it * 2 + par
                    pool.wait_ge(head_landed, n * 80 + 80)
                    pool.wait_ge(scored, it * NCH + (NCH // 2 if par == 0 else NCH))
                    nc.gpsimd.tensor_tensor(ka[:, par, :], k_raw[:, :], ones[:, 0:1].to_broadcast([P, SEQ]),
                                            ALU.mult).then_inc(k_hi_done, 1)
                    nc.gpsimd.tensor_tensor(qa[:, par, :], q_raw[:, :], ones[:, 0:1].to_broadcast([P, SEQ]),
                                            ALU.mult).then_inc(q_split, 1)
                    pool.wait_ge(q_split, n + 1)
                    nc.gpsimd.tensor_tensor(ka[HD:P, par, :], k_raw[HD:P, :], ka[HD:P, par, :].bitcast(F32),
                                            ALU.subtract).then_inc(k_lo_done, 1)
                    pool.wait_ge(k_lo_done, n + 1)
                    nc.gpsimd.tensor_tensor(qb[0:HD, par, :], q_raw[0:HD, :], qa[0:HD, par, :].bitcast(F32),
                                            ALU.subtract).then_inc(q_lo_done, 1)
                    pool.wait_ge(q_lo_done, n + 1)
                    values(it, par, 0)

                def mla(it, par):
                    n = it * 2 + par
                    pool.wait_ge(head_landed, n * 96 + (HEADS * 80 + 96))
                    pool.wait_ge(scored, it * NCH + (TURNS * NCH + (NCH // 2 if par == 0 else NCH)))
                    nc.gpsimd.tensor_tensor(ka[0:MLA_K, par, :], k_raw[0:MLA_K, :],
                                            ones[0:MLA_K, 0:1].to_broadcast([MLA_K, SEQ]), ALU.mult).then_inc(k_hi_done, 1)
                    nc.gpsimd.tensor_tensor(qa[0:MLA_K, par, :], q_raw[0:MLA_K, :],
                                            ones[0:MLA_K, 0:1].to_broadcast([MLA_K, SEQ]), ALU.mult).then_inc(q_split, 1)
                    pool.wait_ge(q_split, n + (HEADS + 1))
                    nc.gpsimd.tensor_tensor(kb[0:MLA_K, par, :], k_raw[0:MLA_K, :], ka[0:MLA_K, par, :].bitcast(F32),
                                            ALU.subtract)
                    nc.gpsimd.tensor_tensor(qb[0:MLA_K, par, :], q_raw[0:MLA_K, :], qa[0:MLA_K, par, :].bitcast(F32),
                                            ALU.subtract).then_inc(q_lo_done, 1)
                    pool.wait_ge(q_lo_done, n + (HEADS + 1))
                    values(it, par, TURNS)

                def values(it, par, turn0):
                    pool.wait_ge(weighed, it * NCH + (turn0 * NCH + (NCH // 2 if par == 0 else NCH)))
                    nc.gpsimd.tensor_tensor(v[:, par, :, 0, :], v_raw[:, :, :],
                                            ones[:, 0:1].unsqueeze(2).to_broadcast([P, QT, HD]), ALU.mult).then_inc(v_half, 1)
                    pool.wait_ge(v_half, it * 2 + (turn0 * 2 + par + 1))
                    nc.gpsimd.tensor_tensor(v[:, par, :, 1, :], v_raw[:, :, :], v[:, par, :, 0, :].bitcast(F32),
                                            ALU.subtract).then_inc(head_split, 1)

                with pool.Fori(0, TURNS) as it:
                    fox(it, 0)
                    fox(it, 1)
                with pool.Fori(0, TURNS) as it:
                    mla(it, 0)
                    mla(it, 1)

            def exp_program(act, it, turn0):
                at = turn0 * NCH

                def exponentials(t, c):
                    if c == 0:
                        act.wait_ge(tile_max, it * NT + (turn0 * NT + t + 1))
                        act.wait_ge(turned, AHEAD + it * NCH + (at + BEFORE[max(t - 1, 0)]))
                    w = width(t, c)
                    nc.scalar.activation(probs[:, t % 2, c * HALF:c * HALF + w], s_ps[:, (BEFORE[t] + c) % S_BANKS, 0:w],
                                         ACT.Exp, bias=neg_max[:, t % 4:t % 4 + 1],
                                         accum_out=row_sum[:, TILES[t][0], TILES[t][1], c:c + 1]).then_inc(exped, 1)

                def high(t, c):
                    n = BEFORE[t] + c
                    act.wait_ge(turned, AHEAD + it * NCH + (at + n + 1))
                    act.wait_ge(weighed, it * NCH + (at + NCH + max(n - PT_SLOTS + 1, 0)))
                    w = width(t, c)
                    nc.scalar.activation(pt_hi[:, n % PT_SLOTS, :, :].rearrange("p a b -> p (a b)")[:, 0:w],
                                         t_ps[:, n % T_BANKS, 0:w], ACT.Copy).then_inc(hi_done, 1)

                for k in range(STEPS):
                    e, h = chunks(k - 1), chunks(k - 2)
                    order = [("e", 0), ("h", 0), ("e", 1), ("e", 2), ("h", 1), ("e", 3), ("h", 2), ("h", 3)]
                    for what, c in order:
                        if what == "e" and c < e:
                            exponentials(k - 1, c)
                        if what == "h" and c < h:
                            high(k - 2, c)
                for n in range(S_BANKS):
                    act.wait_ge(o_turned, AHEAD + it * S_BANKS + (turn0 * S_BANKS + n + 1))
                    if n == 0:
                        act.wait_ge(o_stored, AHEAD + it * 16 + turn0 * 16)
                    nc.scalar.activation(o_feat[:, half(n)], s_ps[:, n, :], ACT.Copy).then_inc(o_out, 1)
                act.wait_ge(o_out, AHEAD + it * S_BANKS + (turn0 + 1) * S_BANKS)
                act.dma_start(o_t[bass.ds(it * P + turn0 * P, P), :], o_feat[:, :]).then_inc(o_stored, 16)

            @block.scalar
            def _(act):
                for count in (o_out, o_stored):
                    act.sem_inc(count, AHEAD)
                nc.scalar.preload_act_table(ACT.Exp)
                with act.Fori(0, TURNS) as it:
                    exp_program(act, it, 0)
                with act.Fori(0, TURNS) as it:
                    exp_program(act, it, TURNS)
                act.wait_ge(o_stored, AHEAD + 16 * 2 * TURNS)

            N_MAX_STEPS = sum(c for c in CHUNKS if c > 1)

            def max_program(dve, it, turn0):
                at = turn0 * NCH
                link = Chain(dve, o_step, it * (2 * GROUPS_O) + turn0 * (2 * GROUPS_O), 2 * GROUPS_O)
                part_steps = [0]

                def maximum(t, c):
                    dve.wait_ge(scored, it * NCH + (at + NCH + BEFORE[t] + c + 1))
                    w = width(t, c)
                    src = s_ps[:, (BEFORE[t] + c) % S_BANKS, 0:w]
                    if CHUNKS[t] == 1:
                        nc.vector.tensor_reduce(neg_max[:, t % 4:t % 4 + 1], src, AX_X, ALU.max,
                                                negate=True).then_inc(tile_max, 1)
                        return
                    nc.vector.tensor_reduce(part_max[:, t % 2, c:c + 1], src, AX_X, ALU.max).then_inc(max_step, 1)
                    part_steps[0] += 1
                    if c == CHUNKS[t] - 1:
                        dve.wait_ge(max_step, it * N_MAX_STEPS + (turn0 * N_MAX_STEPS + part_steps[0]))
                        nc.vector.tensor_reduce(neg_max[:, t % 4:t % 4 + 1], part_max[:, t % 2, 0:CHUNKS[t]], AX_X,
                                                ALU.max, negate=True).then_inc(tile_max, 1)

                def low(t, c):
                    n = BEFORE[t] + c
                    dve.wait_ge(hi_done, it * NCH + (at + n + 1))
                    w = width(t, c)
                    nc.vector.tensor_tensor(pt_lo[:, n % PT_SLOTS, :, :].rearrange("p a b -> p (a b)")[:, 0:w],
                                            t_ps[:, n % T_BANKS, 0:w],
                                            pt_hi[:, n % PT_SLOTS, :, :].rearrange("p a b -> p (a b)")[:, 0:w].bitcast(F32),
                                            ALU.subtract).then_inc(lo_done, 1)

                def outputs(g):
                    dve.wait_ge(weighed, it * NCH + (at + NCH + BEFORE[(g + 1) * O_GROUP]))
                    t0, par = g * O_GROUP, g // (GROUPS_O // 2)
                    q0 = min(TILES[t][1] for t in range(t0, t0 + O_GROUP))
                    sums, inv = weight[:, 0, :], weight[:, 1, :]
                    nc.vector.tensor_reduce(sums, row_sum[:, par, q0:q0 + O_GROUP, :], AX_X, ALU.add)
                    link(nc.vector.tensor_reduce(o_sum[:, :, :],
                                                 o_ps[:, g % 2, :, :].rearrange("p g (l d) -> p g d l", l=2), AX_X, ALU.add))
                    link(nc.vector.reciprocal(inv, sums))
                    nc.vector.tensor_tensor(o_pair[:, q0:q0 + O_GROUP, par * HD:(par + 1) * HD], o_sum[:, :, :], inv.unsqueeze(2).to_broadcast([P, O_GROUP, HD]),
                                            ALU.mult).then_inc(o_read, 1)

                for k in range(STEPS):
                    if k - 4 >= 0 and (k - 4) % O_GROUP == O_GROUP - 1:
                        if k - 4 == O_GROUP - 1:
                            dve.wait_ge(o_turned, AHEAD + it * S_BANKS + turn0 * S_BANKS)
                        outputs((k - 4) // O_GROUP)
                    m, l = chunks(k), chunks(k - 2)
                    order = [("m", 0), ("l", 0), ("m", 1), ("m", 2), ("l", 1), ("m", 3), ("l", 2), ("l", 3)]
                    for what, c in order:
                        if what == "m" and c < m:
                            maximum(k, c)
                        if what == "l" and c < l:
                            low(k - 2, c)
                link.close()

            @block.vector
            def _(dve):
                for count in (lo_done, o_read):
                    dve.sem_inc(count, AHEAD)
                nc.vector.memset(row_sum[:, :, :], 0.0)
                nc.vector.memset(ones[:, :], 1.0).then_inc(consts_set, 1)
                dve.wait_ge(consts_set, 1)
                with dve.Fori(0, TURNS) as it:
                    max_program(dve, it, 0)
                with dve.Fori(0, TURNS) as it:
                    max_program(dve, it, TURNS)

            def product_program(pe, it, turn0):
                at, latent = turn0 * NCH, turn0 > 0

                def scores(t, c):
                    par, i = TILES[t]
                    n = BEFORE[t] + c
                    if n in (0, NCH // 2) and c == 0:
                        pe.wait_ge(head_split, AHEAD + it * 2 + (turn0 * 2 + par + 1))
                        if not latent:
                            pe.wait_ge(gates_landed[par], it * 32 + 32)
                            pe.wait_ge(k_copied[par], it * 16 + 16)
                    if n < S_BANKS:
                        pe.wait_ge(o_out, AHEAD + it * S_BANKS + turn0 * S_BANKS)
                    else:
                        pe.wait_ge(exped, it * NCH + (at + n - S_BANKS + 1))
                    w = width(t, c)
                    dst = s_ps[:, n % S_BANKS, 0:w]
                    queries, keys = slice(i * P, (i + 1) * P), slice(c * HALF, c * HALF + w)
                    if latent:
                        pairs = [(qa[0:MLA_K], ka[0:MLA_K]), (qb[0:MLA_K], ka[0:MLA_K]), (qa[0:MLA_K], kb[0:MLA_K])]
                    else:
                        pairs = [(qa, ka), (qb[0:HD + AUG], kb[0:HD + AUG])]
                    diagonal = c == CHUNKS[t] - 1
                    for m, (q, k) in enumerate(pairs):
                        last = nc.tensor.matmul(dst, q[:, par, queries], k[:, par, keys], start=m == 0,
                                                stop=m == len(pairs) - 1 and not diagonal)
                    if diagonal:
                        last = nc.tensor.matmul(dst[:, w - P:w], ident_b_sb[:, :], masks_sb[:, int(latent), :],
                                                start=False, stop=True)
                    last.then_inc(scored, 1)

                def turn_over(t, c):
                    n = BEFORE[t] + c
                    pe.wait_ge(exped, it * NCH + (at + n + 1))
                    pe.wait_ge(lo_done, AHEAD + it * NCH + (at + max(n - T_BANKS + 1, 0)))
                    for b in range(width(t, c) // P):
                        cols = slice(b * P, (b + 1) * P)
                        last = nc.tensor.transpose(t_ps[:, n % T_BANKS, cols],
                                                   probs[:, t % 2, c * HALF + b * P:c * HALF + (b + 1) * P], ident_sb[:, :])
                    last.then_inc(turned, 1)

                def weigh(t, c):
                    par, i = TILES[t]
                    n, g = BEFORE[t] + c, t // O_GROUP
                    if t % O_GROUP == 0 and c == 0:
                        pe.wait_ge(o_read, AHEAD + it * GROUPS_O + (turn0 * GROUPS_O + max(g - 1, 0)))
                    pe.wait_ge(lo_done, AHEAD + it * NCH + (at + n + 1))
                    dst = o_ps[:, g % 2, i % O_GROUP, :]
                    for b in range(width(t, c) // P):
                        j = c * KB + b
                        nc.tensor.matmul(dst, pt_hi[:, n % PT_SLOTS, b, :], v[:, par, j, :, :], start=j == 0, stop=False)
                        last = nc.tensor.matmul(dst[:, 0:HD], pt_lo[:, n % PT_SLOTS, b, :], v[:, par, j, 0, :],
                                                start=False, stop=j == i)
                    last.then_inc(weighed, 1)

                for k in range(STEPS):
                    for c in range(2):
                        if c < chunks(k - 2):
                            turn_over(k - 2, c)
                    for c in range(MAX_CHUNKS):
                        if c < chunks(k):
                            scores(k, c)
                        if c < chunks(k - 3):
                            weigh(k - 3, c)
                    for c in range(2, MAX_CHUNKS):
                        if c < chunks(k - 2):
                            turn_over(k - 2, c)
                pe.wait_ge(o_read, AHEAD + it * GROUPS_O + (turn0 + 1) * GROUPS_O)
                pe.wait_ge(exped, it * NCH + (at + NCH))
                for n in range(S_BANKS):
                    for b in range(KB):
                        last = nc.tensor.transpose(s_ps[:, n, b * P:(b + 1) * P], o_pair[:, n * KB + b, :], ident_sb[:, :])
                    last.then_inc(o_turned, 1)

            @block.tensor
            def _(pe):
                for count in (turned, o_turned):
                    pe.sem_inc(count, AHEAD)
                pe.sem_inc(scored, NCH)
                pe.sem_inc(weighed, NCH)
                pe.wait_ge(const_landed, 16 * 3)
                with pe.Fori(0, TURNS) as it:
                    product_program(pe, it, 0)
                with pe.Fori(0, TURNS) as it:
                    product_program(pe, it, TURNS)


def finish(nc, x_t, o_t, wfin, gains, ident, out_t):
    with ExitStack() as ctx:
        def sb(name, shape, dt=F32):
            return ctx.enter_context(nc.sbuf_tensor("f_" + name, shape, dt))

        def ps(name, shape):
            return ctx.enter_context(nc.psum_tensor("f_" + name, shape, F32))

        def sem(name):
            return ctx.enter_context(nc.semaphore("f_" + name))

        x_sb = sb("x", [P, KC, BT])
        act_hi, act_lo = sb("act_hi", [P, KC, BT], F32R), sb("act_lo", [P, KC, BT], F32R)
        w_raw = sb("w_raw", [P, RAW, BT])
        w_hi, w_lo = sb("w_hi", [P, RING, BT], F32R), sb("w_lo", [P, RING, BT], F32R)
        r_hi, r_lo = sb("r_hi", [P, GROUP, BT], F32R), sb("r_lo", [P, GROUP, BT], F32R)
        o_raw = sb("o_raw", [P, 2, BT])
        hidden = o_raw
        rstd = sb("rstd", [P, BT])
        square, sumsq, diag = sb("square", [P, BT]), sb("sumsq", [P, BT]), sb("diag", [P, BT])
        small = sb("small", [P, 4, TT])
        ones, ident_sb = sb("ones", [P, P]), sb("ident", [P, P])
        gains_sb = sb("gains", [P, 2, KC])

        pairs = ps("pairs", [P, 2, 2, HALF])
        ps_sum = ps("sum", [P, HALF])
        ps_row = ps("row", [P, 2, HALF])

        const_landed, consts_set = sem("const_landed"), sem("consts_set")
        x_landed = sem("x_landed")
        o_landed = [sem(f"o_landed{i}") for i in range(2)]
        w_landed = [sem(f"w_landed{i}") for i in range(RAW)]
        w_half, w_ready = sem("w_half"), sem("w_ready")
        act_split, act_ready = sem("act_split"), sem("act_ready")
        square_done, sumsq_step = sem("square_done"), sem("sumsq_step")
        pair_done, pair_read = sem("pair_done"), sem("pair_read")
        sums_done, var_done, dev_done = sem("sums_done"), sem("var_done"), sem("dev_done")
        diag_done, row_done, rstd_done = sem("diag_done"), sem("row_done"), sem("rstd_done")
        hidden_squared, hidden_hi, hidden_ready = sem("hidden_squared"), sem("hidden_hi"), sem("hidden_ready")
        scaled, dve_step = sem("scaled"), sem("dve_step")
        stored = sem("stored")

        TILES = FIN_TILES
        G_PAIRS = GROUP + KC
        N_PAIRS = KC + GROUPS * G_PAIRS
        NORMS = 2

        def used(i):
            if i < WO_TILES:
                return i + 1
            g, k = divmod(i - WO_TILES, GROUP_TILES)
            return KC + g * G_PAIRS + (k + 1 if k < GROUP else GROUP + 2 * (k - GROUP + 1))

        with nc.Block() as block:
            @block.sync
            def _(sp):
                for count in (stored,):
                    sp.sem_inc(count, AHEAD)
                def load_w(b, i, g=0):
                    sp.wait_ge(w_ready, AHEAD + b * TILES + (g * GROUP_TILES + (i - RAW + 1) if i >= RAW else 0))
                    slot = i % RAW
                    src = wfin[i] if isinstance(g, int) else wfin[bass.ds(g * GROUP_TILES + i, 1)].rearrange("o p c -> p (o c)")
                    sp.dma_start(w_raw[:, slot, :], src).then_inc(w_landed[slot], 16)

                for dst, src in ((ident_sb[:, :], ident), (gains_sb[:, :, :], gains)):
                    sp.dma_start(dst, src).then_inc(const_landed, 16)
                with sp.Fori(0, NB) as b:
                    tok = bass.ds(b * BT, BT)
                    for c in range(KC):
                        if c == 0:
                            sp.wait_ge(hidden_ready, AHEAD + b * (GROUPS * GROUP))
                        elif c >= 2:
                            sp.wait_ge(act_ready, b * (2 * KC) + c - 1)
                        sp.dma_start(o_raw[:, c % 2, :], o_t[c * P:(c + 1) * P, tok]).then_inc(o_landed[c % 2], 16)
                        if c < RAW:
                            load_w(b, c)
                    sp.wait_ge(stored, AHEAD + b * (16 * KC))
                    sp.dma_start(x_sb[:, :, :], x_t[:, tok].rearrange("(c p) n -> p c n", p=P)).then_inc(x_landed, 16)
                    for i in range(RAW, WO_TILES + RAW):
                        load_w(b, i)
                    with sp.Fori(0, GROUPS - 1) as g:
                        for k in range(GROUP_TILES):
                            load_w(b, WO_TILES + RAW + k, g)
                    for i in range(TILES - GROUP_TILES + RAW, TILES):
                        load_w(b, i)
                    for c in range(KC):
                        sp.wait_ge(scaled, b * KC + c + 1)
                        sp.dma_start(out_t[c * P:(c + 1) * P, tok], x_sb[:, c, :]).then_inc(stored, 16)
                sp.wait_ge(stored, AHEAD + NB * 16 * KC)

            @block.gpsimd
            def _(pool):
                for count in (w_ready,):
                    pool.sem_inc(count, AHEAD)
                pool.wait_ge(consts_set, 1)

                def split(b, i, g=0):
                    raw, slot = i % RAW, i % RING
                    pool.wait_ge(w_landed[raw], b * (16 * TILES // RAW) + g * (16 * GROUP_TILES // RAW) + 16 * (i // RAW + 1))
                    pool.wait_ge(pair_done, AHEAD + b * N_PAIRS + g * G_PAIRS + (used(i - RING) if i >= RING else 0))
                    nc.gpsimd.tensor_tensor(w_hi[:, slot, :], w_raw[:, raw, :], ones[:, 0:1].to_broadcast([P, BT]),
                                            ALU.mult).then_inc(w_half, 1)
                    pool.wait_ge(w_half, b * TILES + g * GROUP_TILES + i + 1)
                    nc.gpsimd.tensor_tensor(w_lo[:, slot, :], w_raw[:, raw, :], w_hi[:, slot, :].bitcast(F32),
                                            ALU.subtract).then_inc(w_ready, 1)

                with pool.Fori(0, NB) as b:
                    for i in range(WO_TILES + RING):
                        split(b, i)
                    with pool.Fori(0, GROUPS - 1) as g:
                        for k in range(GROUP_TILES):
                            split(b, WO_TILES + RING + k, g)
                    for i in range(TILES - RING, TILES):
                        split(b, i)

            @block.scalar
            def _(act):
                for count in (rstd_done,):
                    act.sem_inc(count, AHEAD)
                def squared(b, n, src):
                    act.wait_ge(sumsq_step, AHEAD + b * (NORMS * KC) + n)
                    nc.scalar.activation(square[:, :], src, ACT.Square).then_inc(square_done, 1)

                def deviation(b, n):
                    act.wait_ge(var_done, b * NORMS + n + 1)
                    nc.scalar.activation(small[:, 1, :], small[:, 0, :], ACT.Sqrt).then_inc(dev_done, 1)
                    act.wait_ge(row_done, AHEAD + b * NORMS + n + 1)
                    nc.scalar.activation(rstd[:, :], ps_row[:, :, :].rearrange("p a c -> p (a c)"),
                                         ACT.Copy).then_inc(rstd_done, 1)

                def square_hidden(b, f, g=0):
                    act.wait_ge(pair_read, AHEAD + b * N_PAIRS + g * G_PAIRS + (KC + f + 1))
                    nc.scalar.activation(hidden[:, f % 2, :], hidden[:, f % 2, :], ACT.Square).then_inc(hidden_squared, 1)
                    act.wait_ge(hidden_squared, b * (GROUPS * GROUP) + g * GROUP + f + 1)
                    nc.scalar.activation(r_hi[:, f, :], hidden[:, f % 2, :], ACT.Copy).then_inc(hidden_hi, 1)

                act.wait_ge(const_landed, 32)
                with act.Fori(0, NB) as b:
                    act.wait_ge(pair_done, AHEAD + b * N_PAIRS)
                    for c in range(KC):
                        act.wait_ge(o_landed[c % 2], b * (16 * KC // 2) + 16 * (c // 2 + 1))
                        nc.scalar.activation(act_hi[:, c, :], o_raw[:, c % 2, :], ACT.Copy).then_inc(act_split, 1)
                    for c in range(KC):
                        act.wait_ge(pair_read, AHEAD + b * N_PAIRS + c + 1)
                        squared(b, c, x_sb[:, c, :])
                    act.wait_ge(pair_done, AHEAD + b * N_PAIRS + KC)
                    for c in range(KC):
                        nc.scalar.activation(act_hi[:, c, :], x_sb[:, c, :], ACT.Identity,
                                             scale=gains_sb[:, 0, c:c + 1]).then_inc(act_split, 1)
                    deviation(b, 0)
                    with act.Fori(0, GROUPS) as g:
                        act.wait_ge(pair_done, AHEAD + b * N_PAIRS + g * G_PAIRS + KC)
                        for f in range(GROUP):
                            square_hidden(b, f, g)
                    for c in range(KC):
                        act.wait_ge(pair_read, AHEAD + b * N_PAIRS + (N_PAIRS - KC + c + 1))
                        squared(b, KC + c, x_sb[:, c, :])
                    deviation(b, 1)

            @block.vector
            def _(dve):
                for count in (hidden_ready, sumsq_step, pair_read):
                    dve.sem_inc(count, AHEAD)
                dve.wait_ge(const_landed, 32)
                nc.vector.memset(ones[:, :], 1.0).then_inc(consts_set, 1)
                dve.wait_ge(consts_set, 1)
                with dve.Fori(0, NB) as b:
                    link = Chain(dve, dve_step, b * (5 * NORMS), 5 * NORMS)

                    def add_square(n, first):
                        dve.wait_ge(square_done, b * (NORMS * KC) + n + 1)
                        if first:
                            op = nc.vector.tensor_copy(sumsq[:, :], square[:, :])
                        else:
                            dve.wait_ge(sumsq_step, AHEAD + b * (NORMS * KC) + n)
                            op = nc.vector.tensor_tensor(sumsq[:, :], sumsq[:, :], square[:, :], ALU.add)
                        op.then_inc(sumsq_step, 1)

                    def reciprocal_root(n):
                        dve.wait_ge(sums_done, b * NORMS + n + 1)
                        var, dev, a, r = (small[:, k, :] for k in range(4))
                        nc.vector.tensor_scalar(var, ps_sum[:, n * TT:(n + 1) * TT], 1.0 / D_MODEL, EPS,
                                                ALU.mult, ALU.add).then_inc(var_done, 1)
                        dve.wait_ge(dev_done, b * NORMS + n + 1)
                        link(nc.vector.reciprocal(r, dev))
                        link(nc.vector.tensor_tensor(a, r, r, ALU.mult))
                        link(nc.vector.tensor_tensor(a, a, var, ALU.mult))
                        link(nc.vector.tensor_scalar(a, a, -0.5, 1.5, ALU.mult, ALU.add))
                        link(nc.vector.tensor_tensor(r, r, a, ALU.mult))
                        dve.wait_ge(row_done, AHEAD + b * NORMS + n)
                        nc.vector.tensor_tensor(
                            diag[:, :].rearrange("p (t c) -> p t c", t=TT),
                            ident_sb[:, :].unsqueeze(1).to_broadcast([P, TT, P]),
                            r.unsqueeze(2).to_broadcast([P, TT, P]), ALU.mult).then_inc(diag_done, 1)

                    def pair(n, g=0):
                        dve.wait_ge(pair_done, AHEAD + b * N_PAIRS + g * G_PAIRS + n + 1)
                        return pairs[:, n % 2, :, :].rearrange("p a c -> p (a c)")

                    def add_residual(n, c, g=0):
                        src = pair(n, g)
                        nc.vector.tensor_tensor(x_sb[:, c, :], x_sb[:, c, :], src, ALU.add).then_inc(pair_read, 1)

                    for c in range(KC):
                        dve.wait_ge(act_split, b * (2 * KC) + c + 1)
                        nc.vector.tensor_tensor(act_lo[:, c, :], o_raw[:, c % 2, :], act_hi[:, c, :].bitcast(F32),
                                                ALU.subtract).then_inc(act_ready, 1)
                    dve.wait_ge(x_landed, b * 16 + 16)
                    for c in range(KC):
                        add_residual(c, c)
                        if c > 0:
                            add_square(c - 1, c == 1)
                    add_square(KC - 1, False)
                    for c in range(KC):
                        dve.wait_ge(act_split, b * (2 * KC) + KC + c + 1)
                        nc.vector.scalar_tensor_tensor(act_lo[:, c, :], x_sb[:, c, :], gains_sb[:, 0, c:c + 1],
                                                       act_hi[:, c, :].bitcast(F32), ALU.mult,
                                                       ALU.subtract).then_inc(act_ready, 1)
                    reciprocal_root(0)
                    with dve.Fori(0, GROUPS) as g:
                        dve.wait_ge(rstd_done, AHEAD + b * NORMS + 1)
                        for f in range(GROUP):
                            n = b * (GROUPS * GROUP) + g * GROUP + f
                            src = pair(KC + f, g)
                            nc.vector.scalar_tensor_tensor(hidden[:, f % 2, :], src, 0.0, rstd[:, :], ALU.max,
                                                           ALU.mult).then_inc(pair_read, 1)
                            dve.wait_ge(hidden_hi, n + 1)
                            nc.vector.tensor_tensor(r_lo[:, f, :], hidden[:, f % 2, :], r_hi[:, f, :].bitcast(F32),
                                                    ALU.subtract).then_inc(hidden_ready, 1)
                        for c in range(KC):
                            add_residual(KC + GROUP + c, c, g)
                    for c in range(KC):
                        add_square(KC + c, c == 0)
                    reciprocal_root(1)
                    dve.wait_ge(rstd_done, AHEAD + b * NORMS + 2)
                    for c in range(KC):
                        nc.vector.scalar_tensor_tensor(x_sb[:, c, :], x_sb[:, c, :], gains_sb[:, 1, c:c + 1], rstd[:, :],
                                                       ALU.mult, ALU.mult).then_inc(scaled, 1)
                    link.close()

            @block.tensor
            def _(pe):
                for count in (pair_done, row_done):
                    pe.sem_inc(count, AHEAD)
                pe.wait_ge(const_landed, 32)
                pe.wait_ge(consts_set, 1)
                with pe.Fori(0, NB) as b:
                    def wait_w(i, g=0):
                        pe.wait_ge(w_ready, AHEAD + b * TILES + g * GROUP_TILES + i + 1)

                    def out(n, g=0):
                        pe.wait_ge(pair_read, AHEAD + b * N_PAIRS + g * G_PAIRS + (n - 1 if n >= 2 else 0))
                        return pairs[:, n % 2, :, :]

                    def tile_product(banks, slot, paced=None):
                        for c in range(KC):
                            if paced is not None:
                                pe.wait_ge(act_ready, paced + c + 1)
                            for n in range(2):
                                for k, (w, a) in enumerate(((w_hi, act_hi), (w_hi, act_lo), (w_lo, act_hi))):
                                    last = nc.tensor.matmul(banks[:, n, :], w[:, slot, c * P:(c + 1) * P], a[:, c, half(n)],
                                                            start=c == 0 and k == 0, stop=c == KC - 1 and k == 2)
                        last.then_inc(pair_done, 1)

                    def hidden_product(banks, slot, d, tiles):
                        for f in tiles:
                            cols = slice((f * 2 + d) * P, (f * 2 + d + 1) * P)
                            for n in range(2):
                                for k, (w, a) in enumerate(((w_hi, r_hi), (w_hi, r_lo), (w_lo, r_hi))):
                                    last = nc.tensor.matmul(banks[:, n, :], w[:, slot, cols], a[:, f, half(n)],
                                                            start=f == 0 and k == 0, stop=f == GROUP - 1 and k == 2)
                        return last

                    def norm(n):
                        pe.wait_ge(sumsq_step, AHEAD + b * (NORMS * KC) + (n + 1) * KC)
                        for t in range(TT):
                            last = nc.tensor.matmul(ps_sum[:, n * TT + t:n * TT + t + 1], sumsq[:, t * P:(t + 1) * P],
                                                    ones[:, 0:1], start=True, stop=True)
                        last.then_inc(sums_done, 1)
                        pe.wait_ge(diag_done, b * NORMS + n + 1)
                        pe.wait_ge(rstd_done, AHEAD + b * NORMS + n)
                        for h in range(2):
                            last = nc.tensor.matmul(ps_row[:, h, :], ones[:, :], diag[:, half(h)], start=True, stop=True)
                        last.then_inc(row_done, 1)

                    for i in range(WO_TILES):
                        wait_w(i)
                        tile_product(out(i), i % RING, paced=b * (2 * KC) if i == 0 else None)
                    pe.wait_ge(act_ready, b * (2 * KC) + 2 * KC)
                    norm(0)
                    with pe.Fori(0, GROUPS) as g:
                        for f in range(GROUP):
                            wait_w(WO_TILES + f, g)
                            tile_product(out(KC + f, g), f)
                        for m in range(GROUP):
                            wait_w(WO_TILES + GROUP + m, g)
                            ready = b * (GROUPS * GROUP) + g * GROUP
                            if m == 0:
                                pe.wait_ge(hidden_ready, AHEAD + ready + GROUP - 1)
                            n = KC + GROUP + 2 * m
                            banks = [out(n, g), None]
                            hidden_product(banks[0], m, 0, range(GROUP - 1))
                            banks[1] = out(n + 1, g)
                            hidden_product(banks[1], m, 1, range(GROUP - 1))
                            if m == 0:
                                pe.wait_ge(hidden_ready, AHEAD + ready + GROUP)
                            for d in range(2):
                                hidden_product(banks[d], m, d, [GROUP - 1]).then_inc(pair_done, 1)
                    norm(1)


def weight_tile(w, cols):
    rows = w.shape[0] // P
    tile = w[:, cols].reshape(rows, P, len(cols)).transpose(1, 0, 2).reshape(P, -1)
    return np.pad(tile, ((0, 0), (0, BT - tile.shape[1])))


def projection_stream(w_in, w_q_up, w_kv_up):
    w = HEADS * HD
    gate0 = 3 * w
    lat0 = gate0 + HEADS
    kr0 = lat0 + Q_LORA + KV_LORA
    padded = np.pad(w_in, ((0, 0), (0, 1)))
    pad = w_in.shape[1]
    misc = np.full(P, pad)
    misc[0:HEADS] = gate0 + np.arange(HEADS)
    misc[MISC_KR1:MISC_KR1 + 16] = kr0 + np.arange(16)
    misc[MISC_KR2:MISC_KR2 + 16] = kr0 + 16 + np.arange(16)
    tiles = [weight_tile(padded, lat0 + i * P + np.arange(P)) for i in range(LATS)]
    tiles.append(weight_tile(padded, misc))
    for i in range(12):
        tiles.append(weight_tile(padded, i * P + np.arange(P)))
    heads = np.arange(HEADS)[:, None] * MLA_K
    plain = (heads + np.arange(HD)).reshape(-1, P)
    r1 = (heads + HD + np.arange(16)).reshape(-1)
    r2 = (heads + HD + 16 + np.arange(16)).reshape(-1)
    parts = [weight_tile(w_q_up, c)[:, :2 * P] for c in (*plain, r1, r2)]
    tiles.append(np.concatenate(parts[0:4], axis=1))
    tiles.append(np.pad(np.concatenate(parts[4:6], axis=1), ((0, 0), (0, BT - 4 * P))))
    heads = np.arange(HEADS)[:, None] * 2 * HD
    tiles.append(w_kv_up[:, np.concatenate([(heads + np.arange(HD)).reshape(-1), (heads + HD + np.arange(HD)).reshape(-1)])])
    return np.ascontiguousarray(np.stack(tiles))


def finish_stream(w_o, w_ff1, w_ff2):
    tiles = [weight_tile(w_o, i * P + np.arange(P)) for i in range(WO_TILES)]
    for g in range(GROUPS):
        tiles += [weight_tile(w_ff1, (g * GROUP + f) * P + np.arange(P)) for f in range(GROUP)]
        rows = w_ff2[g * GROUP * P:(g + 1) * GROUP * P]
        tiles += [weight_tile(rows, m * 2 * P + np.arange(2 * P)) for m in range(GROUP)]
    return np.ascontiguousarray(np.stack(tiles))


def program(nc, x_t, wproj, wfin, gain_mix, gain_lat, gains_fin, gate_bias, cos_t, sin_t, ident, ident_b, masks,
            scale, minus, plus, out_t):
    feat = nc.dram_tensor("feat", [ROWS, SEQ], F32).ap()
    v_fox = nc.dram_tensor("v_fox", [SEQ // P, P, HEADS * HD], F32).ap()
    v_mla = nc.dram_tensor("v_mla", [SEQ // P, P, HEADS * HD], F32).ap()
    aug_q = nc.dram_tensor("aug_q", [HEADS, AUG, SEQ], F32).ap()
    aug_k = nc.dram_tensor("aug_k", [HEADS, AUG, SEQ], F32).ap()
    o_t = nc.dram_tensor("o_t", [D_MODEL, SEQ], F32).ap()
    project(nc, x_t, wproj, gain_mix, gain_lat, gate_bias, cos_t, sin_t, ident,
            {"scale": scale, "minus": minus, "plus": plus}, feat, v_fox, v_mla, aug_q, aug_k)
    attend(nc, ident, ident_b, masks, feat, v_fox, v_mla, aug_q, aug_k, o_t)
    finish(nc, x_t, o_t, wfin, gains_fin, ident, out_t)


def shape_constants():
    bf16 = np.dtype(mybir.dt.np(BF16))
    half_rope = ROPE // 2
    inv = (np.float32(ROPE_THETA) ** (-np.arange(half_rope, dtype=np.float32) / np.float32(half_rope))).astype(np.float32)
    ang = inv[:, None] * np.arange(SEQ, dtype=np.float32)[None, :]
    i = np.arange(P)
    causal = i[None, :] <= i[:, None]
    chunked = (i // CHUNK)[None, :] <= (i // CHUNK)[:, None]
    masks = np.stack([np.where(m, 0.0, -1e30) for m in (causal, chunked)], axis=1)
    return {
        "cos_t": np.tile(np.cos(ang), (HEADS, 1)).astype(np.float32),
        "sin_t": np.tile(np.sin(ang), (HEADS, 1)).astype(np.float32),
        "ident": np.eye(P, dtype=np.float32),
        "ident_b": np.eye(P).astype(bf16),
        "masks": masks.astype(bf16),
        "scale": np.tile(np.array([[HD ** -0.5, 1.0]], np.float32), (P, 1)),
        "minus": -np.ones((2, SEQ), np.float32),
        "plus": np.ones((2, SEQ), np.float32),
    }


def kernel(**inputs):
    import concourse.bacc as bacc
    from concourse.bass_utils import run_bass_kernel_spmd

    a = {k: np.asarray(v) for k, v in inputs.items()}
    arrays = {
        "x_t": a["x"][0].T,
        "wproj": projection_stream(a["w_in"][0], a["w_q_up"][0], a["w_kv_up"][0]),
        "wfin": finish_stream(a["w_o"][0], a["w_ff1"][0], a["w_ff2"][0]),
        "gain_mix": a["g_mix"][0].reshape(KC, P).T,
        "gain_lat": np.concatenate([a["g_q"][0], a["g_kv"][0]]).reshape(LATS, P).T,
        "gains_fin": np.stack([a["g_mlp"][0].reshape(KC, P), a["g_final"].reshape(KC, P)]).transpose(2, 0, 1),
        "gate_bias": a["b_f"][0][:, None],
        **shape_constants(),
    }
    arrays = {k: np.ascontiguousarray(v) for k, v in arrays.items()}
    nc = bacc.Bacc("TRN2", target_bir_lowering=False, num_devices=1)
    args = {k: nc.dram_tensor(k, v.shape, mybir.dt.from_np(v.dtype), kind="ExternalInput").ap() for k, v in arrays.items()}
    out_t = nc.dram_tensor("out_t", [D_MODEL, SEQ], F32, kind="ExternalOutput").ap()
    program(nc, **args, out_t=out_t)
    got = run_bass_kernel_spmd(nc, [arrays], core_ids=[0]).results[0]["out_t"]
    return np.ascontiguousarray(got.T)[None]
```

```python
from contextlib import ExitStack

import numpy as np
import concourse.bass as bass
from concourse import mybir

F32 = mybir.dt.float32
F32R = mybir.dt.float32r
BF16 = mybir.dt.bfloat16
ALU = mybir.AluOpType
ACT = mybir.ActivationFunctionType
AX_X = mybir.AxisListType.X

P = 128
SEQ, D_MODEL, D_FF = 2048, 1024, 4096
HEADS, HD = 8, 64
ROPE = 32
MLA_K = HD + ROPE
CHUNK = 64
EPS = 1e-6
ROPE_THETA = 10000.0
Q_LORA, KV_LORA = 256, 128

KC = D_MODEL // P
BT = 1024
NB = SEQ // BT
HALF = 512
TT = BT // P
LATS = (Q_LORA + KV_LORA) // P
RAW = 2
RING = 4
AHEAD = 1

ROW_Q, ROW_K = 0, HEADS * HD
ROW_QN, ROW_KN = 2 * HEADS * HD, 3 * HEADS * HD
ROW_QR1 = 4 * HEADS * HD
ROW_QR2 = ROW_QR1 + HEADS * ROPE // 2
ROW_KR1 = ROW_QR2 + HEADS * ROPE // 2
ROW_KR2 = ROW_KR1 + ROPE // 2
ROWS = ROW_KR2 + ROPE // 2
AUG = 4
MISC_KR1, MISC_KR2 = 32, 64

PROJ_TILES = 19
GROUP = 4
GROUPS = D_FF // P // GROUP
WO_TILES = D_MODEL // P
GROUP_TILES = 2 * GROUP
FIN_TILES = WO_TILES + GROUPS * GROUP_TILES


class Chain:

    def __init__(self, eng, sem, base, total):
        self.eng, self.sem, self.base, self.total, self.n = eng, sem, base, total, 0

    def __call__(self, instruction):
        self.n += 1
        instruction.then_inc(self.sem, 1)
        self.eng.wait_ge(self.sem, self.base + self.n)

    def close(self):
        assert self.n == self.total, (self.n, self.total)


def half(n):
    return slice(n * HALF, (n + 1) * HALF)


def project(nc, x_t, wproj, gains, lat_gains, gate_bias, cos_t, sin_t, ident, signs,
            feat, v_fox, v_mla, aug_q, aug_k):
    with ExitStack() as ctx:
        def sb(name, shape, dt=F32):
            return ctx.enter_context(nc.sbuf_tensor("p_" + name, shape, dt))

        def ps(name, shape):
            return ctx.enter_context(nc.psum_tensor("p_" + name, shape, F32))

        def sem(name):
            return ctx.enter_context(nc.semaphore("p_" + name))

        XRING = 4
        x_sb = sb("x", [P, XRING, BT])
        act_hi, act_lo = sb("act_hi", [P, KC, BT], F32R), sb("act_lo", [P, KC, BT], F32R)
        w_raw = sb("w_raw", [P, RAW, BT])
        w_hi, w_lo = sb("w_hi", [P, RING, BT], F32R), sb("w_lo", [P, RING, BT], F32R)
        stage = sb("stage", [P, 2, BT])
        rstd = sb("rstd", [P, 2, BT])
        RSTD_OF = {"x": 0, "q": 1, "kv": 0}
        lat = sb("lat", [P, LATS, BT])
        lat_hi, lat_lo = sb("lat_hi", [P, LATS, BT], F32R), sb("lat_lo", [P, LATS, BT], F32R)
        trig = sb("trig", [P, 2, BT])
        square, sumsq, diag = sb("square", [P, BT]), sb("sumsq", [P, BT]), sb("diag", [P, BT])
        misc = sb("misc", [P, 3, BT])
        gate, rot = misc[0:HEADS], misc[MISC_KR1:MISC_KR1 + ROPE // 2]
        small = sb("small", [P, 4, TT])
        rstd_t = sb("rstd_t", [P, 3, TT])
        carry = sb("carry", [HEADS, 1])
        ones = sb("ones", [P, P])
        ident_sb = sb("ident", [P, P])
        gains_sb, lat_gains_sb = sb("gains", [P, KC]), sb("lat_gains", [P, LATS])
        bias_sb, scale_sb = sb("bias", [HEADS, 1]), sb("scale", [P, 2])

        pairs = ps("pairs", [P, 2, 2, HALF])
        ps_sum = ps("sum", [P, HALF])
        ps_row = ps("row", [P, 2, HALF])

        const_landed, consts_set = sem("const_landed"), sem("consts_set")
        x_landed = [sem(f"x_landed{i}") for i in range(XRING)]
        w_landed = [sem(f"w_landed{i}") for i in range(RAW)]
        trig_landed = sem("trig_landed")
        x_split, square_done, sumsq_step = sem("x_split"), sem("square_done"), sem("sumsq_step")
        act_ready = sem("act_ready")
        w_half, w_ready = sem("w_half"), sem("w_ready")
        pair_done, pair_read = sem("pair_done"), sem("pair_read")
        sums_done, var_done, dev_done = sem("sums_done"), sem("var_done"), sem("dev_done")
        diag_done, row_done, rstd_done = sem("diag_done"), sem("row_done"), sem("rstd_done")
        lat_split, lat_ready = sem("lat_split"), sem("lat_ready")
        gate_in, gate_log, gate_done, rope_done = sem("gate_in"), sem("gate_log"), sem("gate_done"), sem("rope_done")
        act_step, dve_step = sem("act_step"), sem("dve_step")
        stored = [sem(f"stored{i}") for i in range(2)]
        misc_stored, ones_stored, q_rope_stored = sem("misc_stored"), sem("ones_stored"), sem("q_rope_stored")

        V_PAIRS = TT // 2
        QN_PAIRS, KN_PAIRS = HEADS * HD // P, HEADS * HD // P
        N_PAIRS = 4 + 8 + V_PAIRS + QN_PAIRS + 2 + KN_PAIRS + V_PAIRS
        N_STAGED = N_PAIRS - 4 - 2
        N_SQUARES = KC + LATS
        V_DONE = 12 + V_PAIRS
        USED = {i: i + 1 for i in range(12)} | {i: V_DONE for i in range(12, 16)}
        USED |= {12: 14, 13: 14, 16: V_DONE + QN_PAIRS, 17: V_DONE + QN_PAIRS + 2, 18: N_PAIRS}
        SLOT_LOADS = [len(range(s, PROJ_TILES, RAW)) for s in range(RAW)]
        NORMS = ("x", "q", "kv")

        with nc.Block() as block:
            @block.sync
            def _(sp):
                for count in (*stored, q_rope_stored, misc_stored):
                    sp.sem_inc(count, AHEAD)
                def load_w(b, i, j=0):
                    sp.wait_ge(w_ready, AHEAD + b * PROJ_TILES + (j * 4 + (i - RAW + 1) if i >= RAW else 0))
                    slot = i % RAW
                    src = wproj[i] if isinstance(j, int) else wproj[bass.ds(j * 4 + i, 1)].rearrange("o p c -> p (o c)")
                    sp.dma_start(w_raw[:, slot, :], src).then_inc(w_landed[slot], 16)

                def store(b, n, dst, j=0, tokens=0):
                    read = n + 4 if n < 8 + V_PAIRS + QN_PAIRS else n + 6
                    sp.wait_ge(pair_read, AHEAD + b * N_PAIRS + j * 4 + read + 1)
                    src = stage[:, n % 2, :]
                    src = src.rearrange("p (t c) -> p t c", t=tokens) if tokens else src
                    sp.dma_start(dst, src).then_inc(stored[n % 2], 16)

                for dst, src in ((ident_sb[:, :], ident), (gains_sb[:, :], gains), (lat_gains_sb[:, :], lat_gains),
                                 (bias_sb[:, :], gate_bias), (scale_sb[:, :], signs["scale"])):
                    sp.dma_start(dst, src).then_inc(const_landed, 16)
                for h in range(HEADS):
                    sp.dma_start(aug_q[h, 2:4, :], signs["minus"]).then_inc(ones_stored, 16)
                    sp.dma_start(aug_k[h, 0:2, :], signs["plus"]).then_inc(ones_stored, 16)
                with sp.Fori(0, NB) as b:
                    tok = bass.ds(b * BT, BT)
                    for c in range(KC):
                        sp.wait_ge(sumsq_step, AHEAD + b * N_SQUARES + max(c - XRING + 1, 0))
                        sp.dma_start(x_sb[:, c % XRING, :], x_t[c * P:(c + 1) * P, tok]).then_inc(x_landed[c % XRING], 16)
                        if c < RAW:
                            load_w(b, c)
                    sp.wait_ge(rope_done, AHEAD + b * 2)
                    sp.dma_start(trig[:, 0, :], cos_t[:, tok]).then_inc(trig_landed, 16)
                    sp.dma_start(trig[:, 1, :], sin_t[:, tok]).then_inc(trig_landed, 16)
                    for i in range(RAW, 4 + RAW):
                        load_w(b, i)
                    with sp.Fori(0, 2) as j:
                        for s in range(4):
                            load_w(b, 4 + RAW + s, j)
                            store(b, s, feat[bass.ds(j * (4 * P) + s * P, P), tok], j)
                    for i in range(14, 18):
                        load_w(b, i)
                    sp.wait_ge(gate_done, b + 1)
                    for n, plane in enumerate((2, 0)):
                        sp.dma_start(aug_q[:, n, tok], gate[:, plane, :]).then_inc(misc_stored, 16)
                        sp.dma_start(aug_k[:, 2 + n, tok], gate[:, plane, :]).then_inc(misc_stored, 16)
                    sp.wait_ge(rope_done, AHEAD + b * 2 + 1)
                    sp.dma_start(feat[ROW_KR1:ROW_KR1 + ROPE // 2, tok], rot[:, 2, :]).then_inc(misc_stored, 16)
                    sp.dma_start(feat[ROW_KR2:ROW_KR2 + ROPE // 2, tok], rot[:, 0, :]).then_inc(misc_stored, 16)
                    n = 8
                    for m in range(V_PAIRS):
                        cols = slice(m // 2 * 2 * P, (m // 2 + 1) * 2 * P)
                        store(b, n, v_fox[bass.ds(b * TT + m % 2 * 4, 4), :, cols].rearrange("t p c -> p t c"), tokens=4)
                        n += 1
                    load_w(b, 18)
                    for m in range(QN_PAIRS):
                        store(b, n, feat[ROW_QN + m * P:ROW_QN + (m + 1) * P, tok])
                        n += 1
                    for m in range(KN_PAIRS):
                        store(b, n, feat[ROW_KN + m * P:ROW_KN + (m + 1) * P, tok])
                        n += 1
                    for m in range(V_PAIRS):
                        store(b, n, v_mla[bass.ds(b * TT + 2 * m, 2)].rearrange("t p c -> p t c"), tokens=2)
                        n += 1
                    sp.wait_ge(rope_done, AHEAD + b * 2 + 2)
                    sp.dma_start(feat[ROW_QR1:ROW_QR1 + P, tok], lat[:, 2, :]).then_inc(q_rope_stored, 16)
                    sp.dma_start(feat[ROW_QR2:ROW_QR2 + P, tok], lat[:, 0, :]).then_inc(q_rope_stored, 16)
                for s in range(2):
                    sp.wait_ge(stored[s], AHEAD + 16 * NB * (N_STAGED // 2))
                sp.wait_ge(misc_stored, AHEAD + 16 * 6 * NB)
                sp.wait_ge(q_rope_stored, AHEAD + 16 * 2 * NB)
                sp.wait_ge(ones_stored, 16 * 2 * HEADS)

            @block.gpsimd
            def _(pool):
                for count in (w_ready,):
                    pool.sem_inc(count, AHEAD)
                pool.wait_ge(consts_set, 1)
                with pool.Fori(0, NB) as b:
                    for i in range(PROJ_TILES):
                        raw, slot = i % RAW, i % RING
                        pool.wait_ge(w_landed[raw], b * (16 * SLOT_LOADS[raw]) + 16 * (i // RAW + 1))
                        pool.wait_ge(pair_done, AHEAD + b * N_PAIRS + (USED[i - RING] if i >= RING else 0))
                        nc.gpsimd.tensor_tensor(w_hi[:, slot, :], w_raw[:, raw, :], ones[:, 0:1].to_broadcast([P, BT]),
                                                ALU.mult).then_inc(w_half, 1)
                        pool.wait_ge(w_half, b * PROJ_TILES + i + 1)
                        nc.gpsimd.tensor_tensor(w_lo[:, slot, :], w_raw[:, raw, :], w_hi[:, slot, :].bitcast(F32),
                                                ALU.subtract).then_inc(w_ready, 1)

            @block.scalar
            def _(act):
                for count in (rstd_done,):
                    act.sem_inc(count, AHEAD)
                def deviation(b, norm):
                    n = NORMS.index(norm)
                    act.wait_ge(var_done, b * 3 + n + 1)
                    nc.scalar.activation(small[:, 1, :], small[:, 0, :], ACT.Sqrt).then_inc(dev_done, 1)
                    act.wait_ge(row_done, AHEAD + b * 3 + n + 1)
                    nc.scalar.activation(rstd[:, RSTD_OF[norm], :], ps_row[:, :, :].rearrange("p a c -> p (a c)"),
                                         ACT.Copy).then_inc(rstd_done, 1)

                def squared(b, n, src):
                    act.wait_ge(sumsq_step, AHEAD + b * N_SQUARES + n)
                    nc.scalar.activation(square[:, :], src, ACT.Square).then_inc(square_done, 1)

                act.wait_ge(const_landed, 16 * 5)
                with act.Fori(0, NB) as b:
                    act.wait_ge(pair_done, AHEAD + b * N_PAIRS)
                    for c in range(KC):
                        act.wait_ge(x_landed[c % XRING], b * (16 * KC // XRING) + 16 * (c // XRING + 1))
                        nc.scalar.activation(act_hi[:, c, :], x_sb[:, c % XRING, :], ACT.Identity,
                                             scale=gains_sb[:, c:c + 1]).then_inc(x_split, 1)
                        squared(b, c, x_sb[:, c % XRING, :])
                    deviation(b, "x")
                    for i in range(LATS):
                        act.wait_ge(pair_read, AHEAD + b * N_PAIRS + i + 1)
                        nc.scalar.activation(lat_hi[:, i, :], lat[:, i, :], ACT.Identity,
                                             scale=lat_gains_sb[:, i:i + 1]).then_inc(lat_split, 1)
                        squared(b, KC + i, lat[:, i, :])
                    act.wait_ge(gate_in, b + 1)
                    nc.scalar.activation(gate[:, 1, :], gate[:, 1, :], ACT.Exp).then_inc(act_step, 1)
                    act.wait_ge(act_step, b + 1)
                    nc.scalar.activation(gate[:, 1, :], gate[:, 1, :], ACT.Ln, bias=1.0).then_inc(gate_log, 1)
                    deviation(b, "q")
                    deviation(b, "kv")

            @block.vector
            def _(dve):
                for count in (sumsq_step, rope_done, pair_read):
                    dve.sem_inc(count, AHEAD)
                STEPS = 3 * 5 + 1 + 2 * 3 + 3
                dve.wait_ge(const_landed, 16 * 5)
                nc.vector.memset(carry[:, :], 0.0)
                nc.vector.memset(ones[:, :], 1.0).then_inc(consts_set, 1)
                dve.wait_ge(consts_set, 1)
                with dve.Fori(0, NB) as b:
                    link = Chain(dve, dve_step, b * STEPS, STEPS)

                    def add_square(n, first):
                        dve.wait_ge(square_done, b * N_SQUARES + n + 1)
                        if first:
                            op = nc.vector.tensor_copy(sumsq[:, :], square[:, :])
                        else:
                            dve.wait_ge(sumsq_step, AHEAD + b * N_SQUARES + n)
                            op = nc.vector.tensor_tensor(sumsq[:, :], sumsq[:, :], square[:, :], ALU.add)
                        op.then_inc(sumsq_step, 1)

                    def reciprocal_root(norm, width):
                        n = NORMS.index(norm)
                        dve.wait_ge(sums_done, b * 3 + n + 1)
                        var, dev, a = small[:, 0, :], small[:, 1, :], small[:, 2, :]
                        nc.vector.tensor_scalar(var, ps_sum[:, n * TT:(n + 1) * TT], 1.0 / width, EPS,
                                                ALU.mult, ALU.add).then_inc(var_done, 1)
                        dve.wait_ge(dev_done, b * 3 + n + 1)
                        r = rstd_t[:, n, :]
                        link(nc.vector.reciprocal(r, dev))
                        link(nc.vector.tensor_tensor(a, r, r, ALU.mult))
                        link(nc.vector.tensor_tensor(a, a, var, ALU.mult))
                        link(nc.vector.tensor_scalar(a, a, -0.5, 1.5, ALU.mult, ALU.add))
                        link(nc.vector.tensor_tensor(r, r, a, ALU.mult))
                        dve.wait_ge(row_done, AHEAD + b * 3 + n)
                        nc.vector.tensor_tensor(
                            diag[:, :].rearrange("p (t c) -> p t c", t=TT),
                            ident_sb[:, :].unsqueeze(1).to_broadcast([P, TT, P]),
                            r.unsqueeze(2).to_broadcast([P, TT, P]), ALU.mult).then_inc(diag_done, 1)

                    def pair(n, j=0):
                        dve.wait_ge(pair_done, AHEAD + b * N_PAIRS + j * 4 + n + 1)
                        return pairs[:, n % 2, :, :].rearrange("p a c -> p (a c)")

                    def free_stage(n, j=0):
                        dve.wait_ge(stored[n % 2], AHEAD + b * (16 * N_STAGED // 2) + j * 32 + 16 * (n // 2))

                    for c in range(KC):
                        dve.wait_ge(x_split, b * KC + c + 1)
                        nc.vector.scalar_tensor_tensor(act_lo[:, c, :], x_sb[:, c % XRING, :], gains_sb[:, c:c + 1],
                                                       act_hi[:, c, :].bitcast(F32), ALU.mult,
                                                       ALU.subtract).then_inc(act_ready, 1)
                        add_square(c, c == 0)
                    reciprocal_root("x", D_MODEL)
                    dve.wait_ge(rstd_done, AHEAD + b * 3 + 1)
                    dve.wait_ge(q_rope_stored, AHEAD + b * 32)
                    dve.wait_ge(misc_stored, AHEAD + b * 96)
                    for i in range(LATS):
                        src = pair(i)
                        nc.vector.tensor_tensor(lat[:, i, :], src, rstd[:, 0, :], ALU.mult).then_inc(pair_read, 1)
                    src = pair(LATS)
                    nc.vector.tensor_tensor(gate[:, 0, :], src[0:HEADS], rstd[0:HEADS, 0, :], ALU.mult)
                    for plane, row in enumerate((MISC_KR1, MISC_KR2)):
                        end = row + ROPE // 2
                        last = nc.vector.tensor_tensor(rot[:, plane, :], src[row:end], rstd[row:end, 0, :], ALU.mult)
                    last.then_inc(pair_read, 1)
                    dve.wait_ge(pair_read, AHEAD + b * N_PAIRS + 4)
                    for i in range(LATS):
                        dve.wait_ge(lat_split, b * LATS + i + 1)
                        nc.vector.scalar_tensor_tensor(lat_lo[:, i, :], lat[:, i, :], lat_gains_sb[:, i:i + 1],
                                                       lat_hi[:, i, :].bitcast(F32), ALU.mult,
                                                       ALU.subtract).then_inc(lat_ready, 1)
                        if i < 2:
                            add_square(KC + i, i == 0)
                    link(nc.vector.tensor_scalar(gate[:, 0, :], gate[:, 0, :], bias_sb[:, 0:1], None, ALU.add))
                    nc.vector.scalar_tensor_tensor(gate[:, 1, :], gate[:, 0, :], -1.0, gate[:, 0, :], ALU.mult,
                                                   ALU.min).then_inc(gate_in, 1)
                    dve.wait_ge(trig_landed, b * 32 + 32)

                    def rotate(x1, x2, out, tmp, cos, sin):
                        nc.vector.tensor_tensor(out, x1, cos, ALU.mult)
                        link(nc.vector.tensor_tensor(tmp, x2, sin, ALU.mult))
                        link(nc.vector.tensor_tensor(out, out, tmp, ALU.subtract))
                        nc.vector.tensor_tensor(tmp, x2, cos, ALU.mult)
                        link(nc.vector.tensor_tensor(x1, x1, sin, ALU.mult))
                        nc.vector.tensor_tensor(x1, x1, tmp, ALU.add).then_inc(rope_done, 1)

                    kr = slice(MISC_KR1, MISC_KR1 + ROPE // 2)
                    rotate(rot[:, 0, :], rot[:, 1, :], rot[:, 2, :], diag[kr, :], trig[kr, 0, :], trig[kr, 1, :])
                    dve.wait_ge(gate_log, b + 1)
                    link(nc.vector.scalar_tensor_tensor(gate[:, 0, :], gate[:, 0, :], 0.0, gate[:, 1, :], ALU.min,
                                                        ALU.subtract))
                    link(nc.vector.tensor_tensor_scan(gate[:, 1, :], gate[:, 0, :], gate[:, 0, :], carry[:, 0:1],
                                                      ALU.add, ALU.bypass))
                    nc.vector.tensor_copy(carry[:, :], gate[:, 1, BT - 1:BT])
                    link(nc.vector.tensor_copy(gate[:, 2, :].bitcast(F32R), gate[:, 1, :]))
                    nc.vector.tensor_tensor(gate[:, 0, :], gate[:, 1, :], gate[:, 2, :],
                                            ALU.subtract).then_inc(gate_done, 1)

                    with dve.Fori(0, 2) as j:
                        for s in range(4):
                            src = pair(4 + s, j)
                            free_stage(s, j)
                            nc.vector.scalar_tensor_tensor(stage[:, s % 2, :], src, scale_sb[:, bass.ds(j, 1)],
                                                           rstd[:, 0, :], ALU.mult, ALU.mult).then_inc(pair_read, 1)

                    def values(n, norm, m):
                        src = pair(n)
                        staged = n - 4 if norm == 0 else n - 6
                        free_stage(staged)
                        first, tiles = (4 * (m % 2), 4) if norm == 0 else (2 * m, 2)
                        src = src.rearrange("p (t c) -> p t c", t=tiles)
                        dst = stage[:, staged % 2, :].rearrange("p (t c) -> p t c", t=tiles)
                        for h in range(tiles):
                            last = nc.vector.tensor_scalar(dst[:, h, :], src[:, h, :],
                                                           rstd_t[:, norm, first + h:first + h + 1], None, ALU.mult)
                        last.then_inc(pair_read, 1)

                    reciprocal_root("q", Q_LORA)
                    n = 12
                    for m in range(V_PAIRS):
                        if m == 1:
                            add_square(KC + 2, True)
                        if m == 2:
                            reciprocal_root("kv", KV_LORA)
                        values(n, 0, m)
                        n += 1
                    dve.wait_ge(rstd_done, AHEAD + b * 3 + 2)
                    for m in range(QN_PAIRS + 2):
                        src = pair(n)
                        if m < QN_PAIRS:
                            free_stage(n - 4)
                            dst = stage[:, n % 2, :]
                        else:
                            dst = lat[:, m - QN_PAIRS, :]
                        nc.vector.scalar_tensor_tensor(dst, src, MLA_K ** -0.5, rstd[:, 1, :], ALU.mult,
                                                       ALU.mult).then_inc(pair_read, 1)
                        n += 1
                    dve.wait_ge(rstd_done, AHEAD + b * 3 + 3)
                    for m in range(KN_PAIRS):
                        src = pair(n)
                        free_stage(n - 6)
                        nc.vector.tensor_tensor(stage[:, n % 2, :], src, rstd[:, 0, :], ALU.mult).then_inc(pair_read, 1)
                        n += 1
                    for m in range(V_PAIRS):
                        values(n, 2, m)
                        n += 1
                    assert n == N_PAIRS
                    rotate(lat[:, 0, :], lat[:, 1, :], lat[:, 2, :], diag[:, :], trig[:, 0, :], trig[:, 1, :])
                    link.close()

            @block.tensor
            def _(pe):
                for count in (pair_done, row_done):
                    pe.sem_inc(count, AHEAD)
                def tile_product(out, w_slot, w_cols, hi, lo, chunks, paced=None):
                    for c in range(chunks):
                        if paced is not None:
                            pe.wait_ge(act_ready, paced + c + 1)
                        cols = w_cols(c)
                        for n in range(2):
                            for k, (w, a) in enumerate(((w_hi, hi), (w_hi, lo), (w_lo, hi))):
                                last = nc.tensor.matmul(out[:, n, :], w[:, w_slot, cols], a[:, c, half(n)],
                                                        start=c == 0 and k == 0, stop=c == chunks - 1 and k == 2)
                    return last

                def by_chunk(c):
                    return slice(c * P, (c + 1) * P)

                pe.wait_ge(const_landed, 16 * 5)
                pe.wait_ge(consts_set, 1)
                with pe.Fori(0, NB) as b:
                    def wait_w(i, j=0):
                        pe.wait_ge(w_ready, AHEAD + b * PROJ_TILES + j * 4 + i + 1)

                    def out(n, j=0):
                        pe.wait_ge(pair_read, AHEAD + b * N_PAIRS + (j * 4 + n - 1 if n >= 2 else 0))
                        return pairs[:, n % 2, :, :]

                    def sums(norm):
                        n = NORMS.index(norm)
                        pe.wait_ge(sumsq_step, AHEAD + b * N_SQUARES + (KC, KC + 2, KC + 3)[n])
                        for t in range(TT):
                            last = nc.tensor.matmul(ps_sum[:, n * TT + t:n * TT + t + 1], sumsq[:, t * P:(t + 1) * P],
                                                    ones[:, 0:1], start=True, stop=True)
                        last.then_inc(sums_done, 1)

                    def row(norm):
                        n = NORMS.index(norm)
                        pe.wait_ge(diag_done, b * 3 + n + 1)
                        pe.wait_ge(rstd_done, AHEAD + b * 3 + n)
                        for h in range(2):
                            last = nc.tensor.matmul(ps_row[:, h, :], ones[:, :], diag[:, half(h)], start=True, stop=True)
                        last.then_inc(row_done, 1)

                    for i in range(4):
                        wait_w(i)
                        last = tile_product(out(i), i, by_chunk, act_hi, act_lo, KC, paced=b * KC if i == 0 else None)
                        last.then_inc(pair_done, 1)
                        if i == 0:
                            sums("x")
                        if i == 1:
                            row("x")
                    with pe.Fori(0, 2) as j:
                        for s in range(4):
                            wait_w(4 + s, j)
                            tile_product(out(4 + s, j), s, by_chunk, act_hi, act_lo, KC).then_inc(pair_done, 1)
                    sums("q")
                    n = 12
                    for m in range(V_PAIRS):
                        s = 2 * (m // 2)
                        if m % 2 == 0:
                            wait_w(12 + s + 1)
                        banks = out(n)
                        for q in range(4):
                            tokens = slice((4 * (m % 2) + q) * P, (4 * (m % 2) + q + 1) * P)
                            for c in range(KC):
                                for k, (w, a) in enumerate(((w_hi, act_hi), (w_hi, act_lo), (w_lo, act_hi))):
                                    last = nc.tensor.matmul(banks[:, q // 2, q % 2 * 2 * P:(q % 2 + 1) * 2 * P],
                                                            a[:, c, tokens], w[:, s:s + 2, by_chunk(c)],
                                                            start=c == 0 and k == 0, stop=c == KC - 1 and k == 2)
                        last.then_inc(pair_done, 1)
                        n += 1
                        if m == 0:
                            row("q")
                        if m == 1:
                            sums("kv")
                        if m == 2:
                            row("kv")
                    pe.wait_ge(lat_ready, b * LATS + LATS)
                    for m in range(QN_PAIRS + 2):
                        i, at = (16, m) if m < QN_PAIRS else (17, m - QN_PAIRS)
                        if at == 0:
                            wait_w(i)
                        last = tile_product(out(n), i % RING, lambda c: slice((2 * at + c) * P, (2 * at + c + 1) * P),
                                            lat_hi, lat_lo, 2)
                        last.then_inc(pair_done, 1)
                        n += 1
                    wait_w(18)
                    for m in range(KN_PAIRS):
                        last = tile_product(out(n), 18 % RING, lambda c: slice(m * P, (m + 1) * P),
                                            lat_hi[:, 2:3, :], lat_lo[:, 2:3, :], 1)
                        last.then_inc(pair_done, 1)
                        n += 1
                    for m in range(V_PAIRS):
                        banks = out(n)
                        for h in range(2):
                            tokens = slice((2 * m + h) * P, (2 * m + h + 1) * P)
                            for k, (w, a) in enumerate(((w_hi, lat_hi), (w_hi, lat_lo), (w_lo, lat_hi))):
                                last = nc.tensor.matmul(banks[:, h, :], a[:, 2, tokens], w[:, 18 % RING, HALF:],
                                                        start=k == 0, stop=k == 2)
                        last.then_inc(pair_done, 1)
                        n += 1


def attend(nc, ident, ident_b, masks, masks_wide, feat, v_fox, v_mla, aug_q, aug_k, inv_rows, o_t):
    with ExitStack() as ctx:
        def sb(name, shape, dt=F32):
            return ctx.enter_context(nc.sbuf_tensor("a_" + name, shape, dt))

        def ps(name, shape):
            return ctx.enter_context(nc.psum_tensor("a_" + name, shape, F32))

        def sem(name):
            return ctx.enter_context(nc.semaphore("a_" + name))

        QT = SEQ // P
        KB = HALF // P
        GR = SEQ // HALF
        UNITS = [(g, 2 * j) for g in range(GR) for j in range(2 * (g + 1))]
        NU = len(UNITS)
        LAST_UNIT = [max(u for u in range(NU) if UNITS[u][0] == g) for g in range(GR)]
        CHUNKS = [(i, c) for i in range(QT) for c in range(i // KB + 1)]
        NX = len(CHUNKS) + 1
        SLOTS = 4
        LEAD = 2
        ROW_M = (HD + AUG, MLA_K)
        ROUND_STEPS, HALF_STEPS = 4, (6, 4)
        per = 3
        BESIDE = [[x for x in range(NX - 1) if x // per == u - 1] for u in range(NU)]
        NEGATE_AT, INVERT_AT = NX // per + 2, 6
        START = 64

        qa, qb = sb("qa", [P, 2, SEQ], F32R), sb("qb", [P, 2, SEQ], F32R)
        ka, kb = sb("ka", [P, 2, SEQ], F32R), sb("kb", [P, 2, SEQ], F32R)
        q_raw, k_raw = sb("q_raw", [P, SEQ]), sb("k_raw", [P, SEQ])
        v_raw = sb("v_raw", [P, QT, HD])
        v_ones = sb("v_ones", [P, 2, QT, 2, HD], F32R)
        v_lo = sb("v_lo", [P, 2, QT, HD], F32R)
        e_full = sb("e_full", [P, 2, 2, HALF])
        e_hi, e_lo = sb("e_hi", [P, SLOTS, 2, HALF], F32R), sb("e_lo", [P, SLOTS, 2, HALF], F32R)
        o_raw = sb("o_raw", [P, 2, SEQ])
        o_fin = sb("o_fin", [HD, SEQ])
        sums_t, inv_t = sb("sums_t", [P, QT]), sb("inv_t", [P, QT])
        part_max, neg_max = sb("part_max", [P, QT, GR]), sb("neg_max", [P, QT])
        m_rows = sb("m_rows", [QT, P], F32R)
        ident_sb, ident_b_sb = sb("ident", [P, P]), sb("ident_b", [P, P], BF16)
        masks_sb, wide_sb = sb("masks", [P, 2, P], BF16), sb("masks_wide", [P, 2, 2 * P], BF16)
        ones = sb("ones", [P, 1])

        s_ps = ps("s", [P, 2, 2, HALF])
        x_ps = ps("x", [P, 2, HALF])
        o_ps = ps("o", [P, 2, HALF])

        const_landed, consts_set = sem("const_landed"), sem("consts_set")
        head_landed, gates_landed, row_landed = sem("head_landed"), [sem(f"gates_landed{p}") for p in range(2)], sem("row_landed")
        rounded, halved = sem("rounded"), sem("halved")
        x_scored, x_read, max_done = sem("x_scored"), sem("x_read"), sem("max_done")
        scored, exped, split, weighed = sem("scored"), sem("exped"), sem("split"), sem("weighed")
        o_read, sums_landed, inverted = sem("o_read"), sem("sums_landed"), sem("inverted")
        inv_landed, divided, stored = sem("inv_landed"), sem("divided"), sem("stored")

        def at(n, per, plus=0):
            it, heads = n
            if it is None:
                return START + heads * per + plus
            return it * (2 * per) + (START + heads * per + plus)

        def has_before(n):
            return n[0] is not None or n[1] > 0

        def later(n, heads):
            return n[0], n[1] + heads

        def has_before(n):
            return n[0] is not None or n[1] > 0

        def later(n, heads):
            return n[0], n[1] + heads

        def every_head(eng, run):
            run((None, 0))
            with eng.Fori(0, 2) as it:
                run((it, 1))
                run((it, 2))
            for head in range(5, HEADS):
                run((None, head))
            with eng.Fori(0, 3) as it:
                run((it, HEADS))
                run((it, HEADS + 1))
            for head in range(2 * HEADS - 2, 2 * HEADS):
                run((None, head))

        def kind(n, heads=0):
            total = n[1] + heads
            if n[0] is None:
                return None if not 0 <= total < 2 * HEADS else int(total >= HEADS)
            return int(n[1] >= HEADS)

        def both(n, fox, mla, plus=0):
            return at(n, mla, HEADS * (fox - mla) + plus) if kind(n) else at(n, fox, plus)

        def of_kind(n):
            h = n[1] - HEADS * kind(n)
            return h if n[0] is None else n[0] * 2 + h

        def span(h, size, first=0):
            return slice(first + h * size, first + (h + 1) * size) if isinstance(h, int) else bass.ds(h * size + first, size)

        def group_cols(g):
            return slice(g * HALF, (g + 1) * HALF)

        def unit_cols(u):
            g, j = UNITS[u]
            return slice(HALF // 2 if j == g * KB + 2 else 0, HALF)

        with nc.Block() as block:
            @block.sync
            def _(sp):
                for count in (head_landed, *gates_landed, row_landed, sums_landed, inv_landed, stored):
                    sp.sem_inc(count, START)
                for dst, src in ((ident_sb[:, :], ident), (ident_b_sb[:, :], ident_b), (masks_sb[:, :, :], masks),
                                 (wide_sb[:, :, :], masks_wide)):
                    sp.dma_start(dst, src).then_inc(const_landed, 16)

                def rows(dst, row, h, size):
                    sp.dma_start(dst, feat[span(h, size, row), :]).then_inc(head_landed, 16)

                def load(n):
                    sp.wait_ge(halved, both(n, *HALF_STEPS))
                    h = of_kind(n)
                    if kind(n):
                        rows(q_raw[0:HD, :], ROW_QN, h, HD)
                        rows(k_raw[0:HD, :], ROW_KN, h, HD)
                        rows(q_raw[HD:HD + 16, :], ROW_QR1, h, 16)
                        rows(q_raw[HD + 16:MLA_K, :], ROW_QR2, h, 16)
                        sp.dma_start(k_raw[HD:MLA_K, :], feat[ROW_KR1:ROW_KR1 + ROPE, :]).then_inc(head_landed, 16)
                    else:
                        for part in range(2):
                            rows(q_raw[part * HD:(part + 1) * HD, :], ROW_Q, h, HD)
                            rows(k_raw[part * HD:(part + 1) * HD, :], ROW_K, h, HD)
                    sp.dma_start(v_raw[:, :, :], (v_mla if kind(n) else v_fox)[:, :, span(h, HD)].rearrange("t p d -> p t d")
                                 ).then_inc(head_landed, 16)

                def gates(n):
                    par, h = n[1] % 2, of_kind(n)
                    sp.wait_ge(scored, at(n, NU, -NU))
                    for dst, src in ((qa, aug_q), (ka, aug_k)):
                        sp.dma_start(dst[HD:HD + AUG, par, :].bitcast(F32), src[span(h, 1)].rearrange("o r n -> (o r) n")
                                     ).then_inc(gates_landed[par], 16)

                def maximum_row(n):
                    sp.wait_ge(x_read, at(n, NX, NX))
                    row = ROW_M[kind(n)]
                    sp.dma_start(qa[row:row + 1, n[1] % 2, :].bitcast(F32), m_rows[:, :].bitcast(F32)).then_inc(row_landed, 16)

                def reciprocals(n):
                    sp.wait_ge(o_read, at(n, GR, GR))
                    sp.dma_start(sums_t[:, :], o_raw[HD:HD + 1, n[1] % 2, :]).then_inc(sums_landed, 16)
                    sp.wait_ge(inverted, at(n, 1, 1))
                    row = inv_rows[span(of_kind(n), 1, HEADS * kind(n)), :]
                    sp.dma_start(row.rearrange("o (p t) -> (o p) t", p=P), inv_t[:, :]).then_inc(stored, 16)
                    sp.wait_ge(stored, at(n, 32, 16))
                    sp.dma_start(o_fin[:, :], row.to_broadcast([HD, SEQ])).then_inc(inv_landed, 16)

                def store(n):
                    sp.wait_ge(divided, at(n, 1, 1))
                    sp.dma_start(o_t[span(of_kind(n), HD, HEADS * HD * kind(n)), :], o_fin[:, :]).then_inc(stored, 16)

                def beside(n):
                    if kind(n, 1) == 0:
                        gates(later(n, 1))
                    if has_before(n):
                        reciprocals(later(n, -1))
                    if kind(n, 2) is not None:
                        load(later(n, 2))
                    if has_before(n):
                        store(later(n, -1))
                    if kind(n, 1) is not None:
                        maximum_row(later(n, 1))

                first = (None, 0)
                load(first)
                sp.wait_ge(consts_set, 1)
                gates(first)
                load(later(first, 1))
                maximum_row(first)
                every_head(sp, beside)
                last = (None, 2 * HEADS - 1)
                reciprocals(last)
                store(last)
                sp.wait_ge(stored, at(last, 32, 32))

            @block.gpsimd
            def _(pool):
                pool.sem_inc(halved, START)
                pool.sem_inc(divided, START)
                pool.wait_ge(consts_set, 1)

                def copy(dst, src, first=0):
                    one = ones[first:first + src.shape[0], 0:1]
                    one = one.to_broadcast(src.shape) if len(src.shape) == 2 else one.unsqueeze(2).to_broadcast(src.shape)
                    return nc.gpsimd.tensor_tensor(dst, src, one, ALU.mult)

                def halve(n):
                    par, steps = n[1] % 2, 0
                    pool.wait_ge(head_landed, both(n, 16 * 5, 16 * 6, 16 * (6 if kind(n) else 5)))
                    pool.wait_ge(scored, at(n, NU, -NU))
                    if kind(n):
                        pool.wait_ge(rounded, at(n, ROUND_STEPS, ROUND_STEPS))
                        nc.gpsimd.tensor_tensor(kb[0:MLA_K, par, :], k_raw[0:MLA_K, :], ka[0:MLA_K, par, :].bitcast(F32),
                                                ALU.subtract).then_inc(halved, 1)
                        nc.gpsimd.tensor_tensor(qb[0:MLA_K, par, :], q_raw[0:MLA_K, :], qa[0:MLA_K, par, :].bitcast(F32),
                                                ALU.subtract).then_inc(halved, 1)
                        steps = 2
                    else:
                        copy(kb[:, par, :], k_raw[:, :]).then_inc(halved, 1)
                        pool.wait_ge(halved, both(n, *HALF_STEPS, 1))
                        nc.gpsimd.tensor_tensor(kb[HD:P, par, :], k_raw[HD:P, :], kb[HD:P, par, :].bitcast(F32),
                                                ALU.subtract).then_inc(halved, 1)
                        copy(qb[HD:P, par, :], q_raw[HD:P, :], HD).then_inc(halved, 1)
                        pool.wait_ge(halved, both(n, *HALF_STEPS, 3))
                        pool.wait_ge(rounded, at(n, ROUND_STEPS, ROUND_STEPS))
                        nc.gpsimd.tensor_tensor(qb[0:HD, par, :], q_raw[0:HD, :], qa[0:HD, par, :].bitcast(F32),
                                                ALU.subtract).then_inc(halved, 1)
                        steps = 4
                    pool.wait_ge(halved, both(n, *HALF_STEPS, steps))
                    pool.wait_ge(weighed, at(n, NU, -NU))
                    copy(v_ones[:, par, :, 0, :], v_raw[:, :, :]).then_inc(halved, 1)
                    pool.wait_ge(halved, both(n, *HALF_STEPS, steps + 1))
                    nc.gpsimd.tensor_tensor(v_lo[:, par, :, :], v_raw[:, :, :], v_ones[:, par, :, 0, :].bitcast(F32),
                                            ALU.subtract).then_inc(halved, 1)

                def divide(n):
                    pool.wait_ge(inv_landed, at(n, 16, 16))
                    nc.gpsimd.tensor_tensor(o_fin[:, :], o_raw[0:HD, n[1] % 2, :], o_fin[:, :], ALU.mult).then_inc(divided, 1)

                def beside(n):
                    if kind(n, 1) is not None:
                        halve(later(n, 1))
                    if has_before(n):
                        divide(later(n, -1))

                halve((None, 0))
                every_head(pool, beside)
                divide((None, 2 * HEADS - 1))

            @block.scalar
            def _(act):
                for count in (rounded, exped, o_read):
                    act.sem_inc(count, START)
                nc.scalar.preload_act_table(ACT.Exp)

                def round_part(n, part):
                    width, tok = (MLA_K if kind(n) else HD), slice(part * SEQ // 2, (part + 1) * SEQ // 2)
                    if part == 0:
                        act.wait_ge(head_landed, both(n, 16 * 5, 16 * 6, 16 * (6 if kind(n) else 5)))
                        act.wait_ge(scored, at(n, NU, -NU))
                        act.wait_ge(consts_set, 1)
                    for dst, src in ((ka, k_raw), (qa, q_raw)):
                        nc.scalar.activation(dst[0:width, n[1] % 2, tok], src[0:width, tok], ACT.Copy).then_inc(rounded, 1)

                def exponentials(n, u):
                    act.wait_ge(scored, at(n, NU, u + 1))
                    act.wait_ge(weighed, at(n, NU, u + 1 - SLOTS))
                    src = s_ps[:, u % 2, :, unit_cols(u)]
                    nc.scalar.activation(e_hi[:, u % SLOTS, :, unit_cols(u)], src, ACT.Exp)
                    act.wait_ge(split, at(n, NU, u + 1 - 2))
                    nc.scalar.activation(e_full[:, u % 2, :, unit_cols(u)], src, ACT.Exp).then_inc(exped, 1)

                def read_output(n, g):
                    act.wait_ge(weighed, at(n, NU, LAST_UNIT[g] + 1))
                    if g == 0:
                        act.wait_ge(divided, at(n, 1, -1))
                    nc.scalar.activation(o_raw[:, n[1] % 2, group_cols(g)], o_ps[:, g % 2, :], ACT.Copy).then_inc(o_read, 1)

                def main(n):
                    for u in range(NU):
                        if kind(n, 1) is not None and u < 2:
                            round_part(later(n, 1), u)
                        if u + LEAD < NU:
                            exponentials(n, u + LEAD)
                        elif kind(n, 1) is not None:
                            exponentials(later(n, 1), u + LEAD - NU)
                        if u in LAST_UNIT:
                            read_output(n, UNITS[u][0])

                first = (None, 0)
                for part in range(2):
                    round_part(first, part)
                for u in range(LEAD):
                    exponentials(first, u)
                every_head(act, main)

            @block.vector
            def _(dve):
                for count in (x_read, max_done, split, inverted):
                    dve.sem_inc(count, START)
                nc.vector.memset(ka[HD:P, :, :].bitcast(F32), 1.0)
                nc.vector.memset(v_ones[:, :, :, 1, :].bitcast(F32), 1.0)
                nc.vector.memset(part_max[:, :, :], -3e38)
                nc.vector.memset(ones[:, :], 1.0).then_inc(consts_set, 1)

                def chunk_maximum(n, x):
                    i, c = CHUNKS[x]
                    w = min(HALF, (i + 1) * P - c * HALF)
                    dve.wait_ge(x_scored, at(n, NX, x + 1))
                    nc.vector.tensor_reduce(part_max[:, i, c:c + 1], x_ps[:, (n[1] + x) % 2, 0:w], AX_X, ALU.max
                                            ).then_inc(x_read, 1)

                def negate_maxima(n):
                    dve.wait_ge(x_read, at(n, NX, NX - 1))
                    nc.vector.tensor_reduce(neg_max[:, :], part_max[:, :, :], AX_X, ALU.max, negate=True).then_inc(max_done, 1)

                def maxima_rows(n):
                    dve.wait_ge(x_scored, at(n, NX, NX))
                    dve.wait_ge(row_landed, at(n, 16))
                    nc.vector.tensor_copy(m_rows[:, :], x_ps[0:QT, (n[1] + NX - 1) % 2, 0:P]).then_inc(x_read, 1)

                def low(n, u):
                    dve.wait_ge(exped, at(n, NU, u + 1))
                    cols = unit_cols(u)
                    nc.vector.tensor_tensor(e_lo[:, u % SLOTS, :, cols], e_full[:, u % 2, :, cols],
                                            e_hi[:, u % SLOTS, :, cols].bitcast(F32), ALU.subtract).then_inc(split, 1)

                def invert(n):
                    dve.wait_ge(sums_landed, at(n, 16, 16))
                    nc.vector.reciprocal(inv_t[:, :], sums_t[:, :]).then_inc(inverted, 1)

                def main(n):
                    for u in range(NU):
                        if kind(n, 1) is not None:
                            for x in BESIDE[u]:
                                chunk_maximum(later(n, 1), x)
                            if u == NEGATE_AT:
                                negate_maxima(later(n, 1))
                        if u + LEAD < NU:
                            low(n, u + LEAD)
                        elif kind(n, 1) is not None:
                            low(later(n, 1), u + LEAD - NU)
                        if kind(n, 1) is not None and u == NEGATE_AT:
                            maxima_rows(later(n, 1))
                        if u == INVERT_AT and has_before(n):
                            invert(later(n, -1))

                first = (None, 0)
                for x in range(NX - 1):
                    chunk_maximum(first, x)
                negate_maxima(first)
                maxima_rows(first)
                for u in range(LEAD):
                    low(first, u)
                every_head(dve, main)
                invert((None, 2 * HEADS - 1))

            @block.tensor
            def _(pe):
                for count in (x_scored, scored, weighed):
                    pe.sem_inc(count, START)
                pe.wait_ge(const_landed, 16 * 4)

                def chunk(n, x):
                    par, (i, c) = n[1] % 2, CHUNKS[x]
                    if x == 0:
                        if not kind(n):
                            pe.wait_ge(gates_landed[par], at(later(n, -par), 16, 32))
                        pe.wait_ge(rounded, at(n, ROUND_STEPS, ROUND_STEPS // 2))
                    if i == QT // 2 and c == 0:
                        pe.wait_ge(rounded, at(n, ROUND_STEPS, ROUND_STEPS))
                    pe.wait_ge(x_read, at(n, NX, x + 1 - 2))
                    width = MLA_K if kind(n) else HD + AUG
                    w = min(HALF, (i + 1) * P - c * HALF)
                    dst = x_ps[:, (n[1] + x) % 2, 0:w]
                    diagonal = c == i // KB
                    last = nc.tensor.matmul(dst, qa[0:width, par, i * P:(i + 1) * P], ka[0:width, par, c * HALF:c * HALF + w],
                                            start=True, stop=not diagonal)
                    if diagonal:
                        last = nc.tensor.matmul(dst[:, w - P:w], ident_b_sb[:, :], masks_sb[:, kind(n), :],
                                                start=False, stop=True)
                    last.then_inc(x_scored, 1)

                def turn_maxima(n):
                    pe.wait_ge(max_done, at(n, 1, 1))
                    nc.tensor.transpose(x_ps[0:QT, (n[1] + NX - 1) % 2, 0:P], neg_max[:, :], ident_sb[:, :]).then_inc(x_scored, 1)

                def scores(n, u):
                    par, latent, (g, j0) = n[1] % 2, kind(n), UNITS[u]
                    if u == 0:
                        pe.wait_ge(row_landed, at(n, 16, 16))
                        pe.wait_ge(halved, both(n, *HALF_STEPS, 2 if latent else 4))
                    pe.wait_ge(exped, at(n, NU, u + 1 - 2))
                    cols = unit_cols(u)
                    queries = slice(g * HALF + cols.start, (g + 1) * HALF)
                    rows = ROW_M[latent] + 1
                    terms = [(ka[0:rows], qa[0:rows])]
                    if latent:
                        terms += [(ka[0:MLA_K], qb[0:MLA_K]), (kb[0:MLA_K], qa[0:MLA_K])]
                    else:
                        terms += [(kb, qb)]
                    for b in range(2):
                        j = j0 + b
                        diagonal = j0 >= g * KB
                        for m, (k, q) in enumerate(terms):
                            last = nc.tensor.matmul(s_ps[:, u % 2, b, cols], k[:, par, j * P:(j + 1) * P], q[:, par, queries],
                                                    start=m == 0, stop=m == len(terms) - 1 and not diagonal)
                        if diagonal:
                            own = (j - g * KB) * P
                            last = nc.tensor.matmul(s_ps[:, u % 2, b, own - b * P:own + P], ident_b_sb[:, :],
                                                    wide_sb[:, latent, (1 - b) * P:2 * P], start=False, stop=True)
                    last.then_inc(scored, 1)

                def weigh(n, u, b):
                    par, (g, j0) = n[1] % 2, UNITS[u]
                    j, cols = j0 + b, unit_cols(u)
                    if b == 0:
                        if u == 0:
                            pe.wait_ge(halved, both(n, *HALF_STEPS, HALF_STEPS[kind(n)]))
                        if j == 0:
                            pe.wait_ge(o_read, at(n, GR, g + 1 - 2))
                        pe.wait_ge(split, at(n, NU, u + 1))
                    dst = o_ps[:, g % 2, cols]
                    hi, lo = e_hi[:, u % SLOTS, b, cols], e_lo[:, u % SLOTS, b, cols]
                    nc.tensor.matmul(dst, v_ones[:, par, j, :, :], hi, start=j == 0, stop=False)
                    nc.tensor.matmul(dst[0:HD], v_lo[:, par, j, :], hi, start=False, stop=False)
                    last = nc.tensor.matmul(dst, v_ones[:, par, j, :, :], lo, start=False, stop=j == (g + 1) * KB - 1)
                    if b == 1:
                        last.then_inc(weighed, 1)

                def main(n):
                    for u in range(NU):
                        if u + LEAD < NU:
                            scores(n, u + LEAD)
                        elif kind(n, 1) is not None:
                            scores(later(n, 1), u + LEAD - NU)
                        more = BESIDE[u] if kind(n, 1) is not None else []
                        for x in more[:1]:
                            chunk(later(n, 1), x)
                        weigh(n, u, 0)
                        for x in more[1:2]:
                            chunk(later(n, 1), x)
                        weigh(n, u, 1)
                        for x in more[2:]:
                            chunk(later(n, 1), x)
                        if kind(n, 1) is not None and u == NEGATE_AT:
                            turn_maxima(later(n, 1))

                first = (None, 0)
                for x in range(NX - 1):
                    chunk(first, x)
                turn_maxima(first)
                for u in range(LEAD):
                    scores(first, u)
                every_head(pe, main)


def finish(nc, x_t, o_t, wfin, gains, ident, out_t):
    with ExitStack() as ctx:
        def sb(name, shape, dt=F32):
            return ctx.enter_context(nc.sbuf_tensor("f_" + name, shape, dt))

        def ps(name, shape):
            return ctx.enter_context(nc.psum_tensor("f_" + name, shape, F32))

        def sem(name):
            return ctx.enter_context(nc.semaphore("f_" + name))

        x_sb = sb("x", [P, KC, BT])
        act_hi, act_lo = sb("act_hi", [P, KC, BT], F32R), sb("act_lo", [P, KC, BT], F32R)
        w_raw = sb("w_raw", [P, RAW, BT])
        w_hi, w_lo = sb("w_hi", [P, RING, BT], F32R), sb("w_lo", [P, RING, BT], F32R)
        r_hi, r_lo = sb("r_hi", [P, GROUP, BT], F32R), sb("r_lo", [P, GROUP, BT], F32R)
        o_raw = sb("o_raw", [P, 2, BT])
        hidden = o_raw
        rstd = sb("rstd", [P, BT])
        square, sumsq, diag = sb("square", [P, BT]), sb("sumsq", [P, BT]), sb("diag", [P, BT])
        small = sb("small", [P, 4, TT])
        ones, ident_sb = sb("ones", [P, P]), sb("ident", [P, P])
        gains_sb = sb("gains", [P, 2, KC])

        pairs = ps("pairs", [P, 2, 2, HALF])
        ps_sum = ps("sum", [P, HALF])
        ps_row = ps("row", [P, 2, HALF])

        const_landed, consts_set = sem("const_landed"), sem("consts_set")
        x_landed = sem("x_landed")
        o_landed = [sem(f"o_landed{i}") for i in range(2)]
        w_landed = [sem(f"w_landed{i}") for i in range(RAW)]
        w_half, w_ready = sem("w_half"), sem("w_ready")
        act_split, act_ready = sem("act_split"), sem("act_ready")
        square_done, sumsq_step = sem("square_done"), sem("sumsq_step")
        pair_done, pair_read = sem("pair_done"), sem("pair_read")
        sums_done, var_done, dev_done = sem("sums_done"), sem("var_done"), sem("dev_done")
        diag_done, row_done, rstd_done = sem("diag_done"), sem("row_done"), sem("rstd_done")
        hidden_squared, hidden_hi, hidden_ready = sem("hidden_squared"), sem("hidden_hi"), sem("hidden_ready")
        scaled, dve_step = sem("scaled"), sem("dve_step")
        stored = sem("stored")

        TILES = FIN_TILES
        G_PAIRS = GROUP + KC
        N_PAIRS = KC + GROUPS * G_PAIRS
        NORMS = 2

        def used(i):
            if i < WO_TILES:
                return i + 1
            g, k = divmod(i - WO_TILES, GROUP_TILES)
            return KC + g * G_PAIRS + (k + 1 if k < GROUP else GROUP + 2 * (k - GROUP + 1))

        with nc.Block() as block:
            @block.sync
            def _(sp):
                for count in (stored,):
                    sp.sem_inc(count, AHEAD)
                def load_w(b, i, g=0):
                    sp.wait_ge(w_ready, AHEAD + b * TILES + (g * GROUP_TILES + (i - RAW + 1) if i >= RAW else 0))
                    slot = i % RAW
                    src = wfin[i] if isinstance(g, int) else wfin[bass.ds(g * GROUP_TILES + i, 1)].rearrange("o p c -> p (o c)")
                    sp.dma_start(w_raw[:, slot, :], src).then_inc(w_landed[slot], 16)

                for dst, src in ((ident_sb[:, :], ident), (gains_sb[:, :, :], gains)):
                    sp.dma_start(dst, src).then_inc(const_landed, 16)
                with sp.Fori(0, NB) as b:
                    tok = bass.ds(b * BT, BT)
                    for c in range(KC):
                        if c == 0:
                            sp.wait_ge(hidden_ready, AHEAD + b * (GROUPS * GROUP))
                        elif c >= 2:
                            sp.wait_ge(act_ready, b * (2 * KC) + c - 1)
                        sp.dma_start(o_raw[:, c % 2, :], o_t[c * P:(c + 1) * P, tok]).then_inc(o_landed[c % 2], 16)
                        if c < RAW:
                            load_w(b, c)
                    sp.wait_ge(stored, AHEAD + b * (16 * KC))
                    sp.dma_start(x_sb[:, :, :], x_t[:, tok].rearrange("(c p) n -> p c n", p=P)).then_inc(x_landed, 16)
                    for i in range(RAW, WO_TILES + RAW):
                        load_w(b, i)
                    with sp.Fori(0, GROUPS - 1) as g:
                        for k in range(GROUP_TILES):
                            load_w(b, WO_TILES + RAW + k, g)
                    for i in range(TILES - GROUP_TILES + RAW, TILES):
                        load_w(b, i)
                    for c in range(KC):
                        sp.wait_ge(scaled, b * KC + c + 1)
                        sp.dma_start(out_t[c * P:(c + 1) * P, tok], x_sb[:, c, :]).then_inc(stored, 16)
                sp.wait_ge(stored, AHEAD + NB * 16 * KC)

            @block.gpsimd
            def _(pool):
                for count in (w_ready,):
                    pool.sem_inc(count, AHEAD)
                pool.wait_ge(consts_set, 1)

                def split(b, i, g=0):
                    raw, slot = i % RAW, i % RING
                    pool.wait_ge(w_landed[raw], b * (16 * TILES // RAW) + g * (16 * GROUP_TILES // RAW) + 16 * (i // RAW + 1))
                    pool.wait_ge(pair_done, AHEAD + b * N_PAIRS + g * G_PAIRS + (used(i - RING) if i >= RING else 0))
                    nc.gpsimd.tensor_tensor(w_hi[:, slot, :], w_raw[:, raw, :], ones[:, 0:1].to_broadcast([P, BT]),
                                            ALU.mult).then_inc(w_half, 1)
                    pool.wait_ge(w_half, b * TILES + g * GROUP_TILES + i + 1)
                    nc.gpsimd.tensor_tensor(w_lo[:, slot, :], w_raw[:, raw, :], w_hi[:, slot, :].bitcast(F32),
                                            ALU.subtract).then_inc(w_ready, 1)

                with pool.Fori(0, NB) as b:
                    for i in range(WO_TILES + RING):
                        split(b, i)
                    with pool.Fori(0, GROUPS - 1) as g:
                        for k in range(GROUP_TILES):
                            split(b, WO_TILES + RING + k, g)
                    for i in range(TILES - RING, TILES):
                        split(b, i)

            @block.scalar
            def _(act):
                for count in (rstd_done,):
                    act.sem_inc(count, AHEAD)
                def squared(b, n, src):
                    act.wait_ge(sumsq_step, AHEAD + b * (NORMS * KC) + n)
                    nc.scalar.activation(square[:, :], src, ACT.Square).then_inc(square_done, 1)

                def deviation(b, n):
                    act.wait_ge(var_done, b * NORMS + n + 1)
                    nc.scalar.activation(small[:, 1, :], small[:, 0, :], ACT.Sqrt).then_inc(dev_done, 1)
                    act.wait_ge(row_done, AHEAD + b * NORMS + n + 1)
                    nc.scalar.activation(rstd[:, :], ps_row[:, :, :].rearrange("p a c -> p (a c)"),
                                         ACT.Copy).then_inc(rstd_done, 1)

                def square_hidden(b, f, g=0):
                    act.wait_ge(pair_read, AHEAD + b * N_PAIRS + g * G_PAIRS + (KC + f + 1))
                    nc.scalar.activation(hidden[:, f % 2, :], hidden[:, f % 2, :], ACT.Square).then_inc(hidden_squared, 1)
                    act.wait_ge(hidden_squared, b * (GROUPS * GROUP) + g * GROUP + f + 1)
                    nc.scalar.activation(r_hi[:, f, :], hidden[:, f % 2, :], ACT.Copy).then_inc(hidden_hi, 1)

                act.wait_ge(const_landed, 32)
                with act.Fori(0, NB) as b:
                    act.wait_ge(pair_done, AHEAD + b * N_PAIRS)
                    for c in range(KC):
                        act.wait_ge(o_landed[c % 2], b * (16 * KC // 2) + 16 * (c // 2 + 1))
                        nc.scalar.activation(act_hi[:, c, :], o_raw[:, c % 2, :], ACT.Copy).then_inc(act_split, 1)
                    for c in range(KC):
                        act.wait_ge(pair_read, AHEAD + b * N_PAIRS + c + 1)
                        squared(b, c, x_sb[:, c, :])
                    act.wait_ge(pair_done, AHEAD + b * N_PAIRS + KC)
                    for c in range(KC):
                        nc.scalar.activation(act_hi[:, c, :], x_sb[:, c, :], ACT.Identity,
                                             scale=gains_sb[:, 0, c:c + 1]).then_inc(act_split, 1)
                    deviation(b, 0)
                    with act.Fori(0, GROUPS) as g:
                        act.wait_ge(pair_done, AHEAD + b * N_PAIRS + g * G_PAIRS + KC)
                        for f in range(GROUP):
                            square_hidden(b, f, g)
                    for c in range(KC):
                        act.wait_ge(pair_read, AHEAD + b * N_PAIRS + (N_PAIRS - KC + c + 1))
                        squared(b, KC + c, x_sb[:, c, :])
                    deviation(b, 1)

            @block.vector
            def _(dve):
                for count in (hidden_ready, sumsq_step, pair_read):
                    dve.sem_inc(count, AHEAD)
                dve.wait_ge(const_landed, 32)
                nc.vector.memset(ones[:, :], 1.0).then_inc(consts_set, 1)
                dve.wait_ge(consts_set, 1)
                with dve.Fori(0, NB) as b:
                    link = Chain(dve, dve_step, b * (5 * NORMS), 5 * NORMS)

                    def add_square(n, first):
                        dve.wait_ge(square_done, b * (NORMS * KC) + n + 1)
                        if first:
                            op = nc.vector.tensor_copy(sumsq[:, :], square[:, :])
                        else:
                            dve.wait_ge(sumsq_step, AHEAD + b * (NORMS * KC) + n)
                            op = nc.vector.tensor_tensor(sumsq[:, :], sumsq[:, :], square[:, :], ALU.add)
                        op.then_inc(sumsq_step, 1)

                    def reciprocal_root(n):
                        dve.wait_ge(sums_done, b * NORMS + n + 1)
                        var, dev, a, r = (small[:, k, :] for k in range(4))
                        nc.vector.tensor_scalar(var, ps_sum[:, n * TT:(n + 1) * TT], 1.0 / D_MODEL, EPS,
                                                ALU.mult, ALU.add).then_inc(var_done, 1)
                        dve.wait_ge(dev_done, b * NORMS + n + 1)
                        link(nc.vector.reciprocal(r, dev))
                        link(nc.vector.tensor_tensor(a, r, r, ALU.mult))
                        link(nc.vector.tensor_tensor(a, a, var, ALU.mult))
                        link(nc.vector.tensor_scalar(a, a, -0.5, 1.5, ALU.mult, ALU.add))
                        link(nc.vector.tensor_tensor(r, r, a, ALU.mult))
                        dve.wait_ge(row_done, AHEAD + b * NORMS + n)
                        nc.vector.tensor_tensor(
                            diag[:, :].rearrange("p (t c) -> p t c", t=TT),
                            ident_sb[:, :].unsqueeze(1).to_broadcast([P, TT, P]),
                            r.unsqueeze(2).to_broadcast([P, TT, P]), ALU.mult).then_inc(diag_done, 1)

                    def pair(n, g=0):
                        dve.wait_ge(pair_done, AHEAD + b * N_PAIRS + g * G_PAIRS + n + 1)
                        return pairs[:, n % 2, :, :].rearrange("p a c -> p (a c)")

                    def add_residual(n, c, g=0):
                        src = pair(n, g)
                        nc.vector.tensor_tensor(x_sb[:, c, :], x_sb[:, c, :], src, ALU.add).then_inc(pair_read, 1)

                    for c in range(KC):
                        dve.wait_ge(act_split, b * (2 * KC) + c + 1)
                        nc.vector.tensor_tensor(act_lo[:, c, :], o_raw[:, c % 2, :], act_hi[:, c, :].bitcast(F32),
                                                ALU.subtract).then_inc(act_ready, 1)
                    dve.wait_ge(x_landed, b * 16 + 16)
                    for c in range(KC):
                        add_residual(c, c)
                        if c > 0:
                            add_square(c - 1, c == 1)
                    add_square(KC - 1, False)
                    for c in range(KC):
                        dve.wait_ge(act_split, b * (2 * KC) + KC + c + 1)
                        nc.vector.scalar_tensor_tensor(act_lo[:, c, :], x_sb[:, c, :], gains_sb[:, 0, c:c + 1],
                                                       act_hi[:, c, :].bitcast(F32), ALU.mult,
                                                       ALU.subtract).then_inc(act_ready, 1)
                    reciprocal_root(0)
                    with dve.Fori(0, GROUPS) as g:
                        dve.wait_ge(rstd_done, AHEAD + b * NORMS + 1)
                        for f in range(GROUP):
                            n = b * (GROUPS * GROUP) + g * GROUP + f
                            src = pair(KC + f, g)
                            nc.vector.scalar_tensor_tensor(hidden[:, f % 2, :], src, 0.0, rstd[:, :], ALU.max,
                                                           ALU.mult).then_inc(pair_read, 1)
                            dve.wait_ge(hidden_hi, n + 1)
                            nc.vector.tensor_tensor(r_lo[:, f, :], hidden[:, f % 2, :], r_hi[:, f, :].bitcast(F32),
                                                    ALU.subtract).then_inc(hidden_ready, 1)
                        for c in range(KC):
                            add_residual(KC + GROUP + c, c, g)
                    for c in range(KC):
                        add_square(KC + c, c == 0)
                    reciprocal_root(1)
                    dve.wait_ge(rstd_done, AHEAD + b * NORMS + 2)
                    for c in range(KC):
                        nc.vector.scalar_tensor_tensor(x_sb[:, c, :], x_sb[:, c, :], gains_sb[:, 1, c:c + 1], rstd[:, :],
                                                       ALU.mult, ALU.mult).then_inc(scaled, 1)
                    link.close()

            @block.tensor
            def _(pe):
                for count in (pair_done, row_done):
                    pe.sem_inc(count, AHEAD)
                pe.wait_ge(const_landed, 32)
                pe.wait_ge(consts_set, 1)
                with pe.Fori(0, NB) as b:
                    def wait_w(i, g=0):
                        pe.wait_ge(w_ready, AHEAD + b * TILES + g * GROUP_TILES + i + 1)

                    def out(n, g=0):
                        pe.wait_ge(pair_read, AHEAD + b * N_PAIRS + g * G_PAIRS + (n - 1 if n >= 2 else 0))
                        return pairs[:, n % 2, :, :]

                    def tile_product(banks, slot, paced=None):
                        for c in range(KC):
                            if paced is not None:
                                pe.wait_ge(act_ready, paced + c + 1)
                            for n in range(2):
                                for k, (w, a) in enumerate(((w_hi, act_hi), (w_hi, act_lo), (w_lo, act_hi))):
                                    last = nc.tensor.matmul(banks[:, n, :], w[:, slot, c * P:(c + 1) * P], a[:, c, half(n)],
                                                            start=c == 0 and k == 0, stop=c == KC - 1 and k == 2)
                        last.then_inc(pair_done, 1)

                    def hidden_product(banks, slot, d, tiles):
                        for f in tiles:
                            cols = slice((f * 2 + d) * P, (f * 2 + d + 1) * P)
                            for n in range(2):
                                for k, (w, a) in enumerate(((w_hi, r_hi), (w_hi, r_lo), (w_lo, r_hi))):
                                    last = nc.tensor.matmul(banks[:, n, :], w[:, slot, cols], a[:, f, half(n)],
                                                            start=f == 0 and k == 0, stop=f == GROUP - 1 and k == 2)
                        return last

                    def norm(n):
                        pe.wait_ge(sumsq_step, AHEAD + b * (NORMS * KC) + (n + 1) * KC)
                        for t in range(TT):
                            last = nc.tensor.matmul(ps_sum[:, n * TT + t:n * TT + t + 1], sumsq[:, t * P:(t + 1) * P],
                                                    ones[:, 0:1], start=True, stop=True)
                        last.then_inc(sums_done, 1)
                        pe.wait_ge(diag_done, b * NORMS + n + 1)
                        pe.wait_ge(rstd_done, AHEAD + b * NORMS + n)
                        for h in range(2):
                            last = nc.tensor.matmul(ps_row[:, h, :], ones[:, :], diag[:, half(h)], start=True, stop=True)
                        last.then_inc(row_done, 1)

                    for i in range(WO_TILES):
                        wait_w(i)
                        tile_product(out(i), i % RING, paced=b * (2 * KC) if i == 0 else None)
                    pe.wait_ge(act_ready, b * (2 * KC) + 2 * KC)
                    norm(0)
                    with pe.Fori(0, GROUPS) as g:
                        for f in range(GROUP):
                            wait_w(WO_TILES + f, g)
                            tile_product(out(KC + f, g), f)
                        for m in range(GROUP):
                            wait_w(WO_TILES + GROUP + m, g)
                            ready = b * (GROUPS * GROUP) + g * GROUP
                            if m == 0:
                                pe.wait_ge(hidden_ready, AHEAD + ready + GROUP - 1)
                            n = KC + GROUP + 2 * m
                            banks = [out(n, g), None]
                            hidden_product(banks[0], m, 0, range(GROUP - 1))
                            banks[1] = out(n + 1, g)
                            hidden_product(banks[1], m, 1, range(GROUP - 1))
                            if m == 0:
                                pe.wait_ge(hidden_ready, AHEAD + ready + GROUP)
                            for d in range(2):
                                hidden_product(banks[d], m, d, [GROUP - 1]).then_inc(pair_done, 1)
                    norm(1)


def weight_tile(w, cols):
    rows = w.shape[0] // P
    tile = w[:, cols].reshape(rows, P, len(cols)).transpose(1, 0, 2).reshape(P, -1)
    return np.pad(tile, ((0, 0), (0, BT - tile.shape[1])))


def projection_stream(w_in, w_q_up, w_kv_up):
    w = HEADS * HD
    gate0 = 3 * w
    lat0 = gate0 + HEADS
    kr0 = lat0 + Q_LORA + KV_LORA
    padded = np.pad(w_in, ((0, 0), (0, 1)))
    pad = w_in.shape[1]
    misc = np.full(P, pad)
    misc[0:HEADS] = gate0 + np.arange(HEADS)
    misc[MISC_KR1:MISC_KR1 + 16] = kr0 + np.arange(16)
    misc[MISC_KR2:MISC_KR2 + 16] = kr0 + 16 + np.arange(16)
    tiles = [weight_tile(padded, lat0 + i * P + np.arange(P)) for i in range(LATS)]
    tiles.append(weight_tile(padded, misc))
    for i in range(12):
        tiles.append(weight_tile(padded, i * P + np.arange(P)))
    heads = np.arange(HEADS)[:, None] * MLA_K
    plain = (heads + np.arange(HD)).reshape(-1, P)
    r1 = (heads + HD + np.arange(16)).reshape(-1)
    r2 = (heads + HD + 16 + np.arange(16)).reshape(-1)
    parts = [weight_tile(w_q_up, c)[:, :2 * P] for c in (*plain, r1, r2)]
    tiles.append(np.concatenate(parts[0:4], axis=1))
    tiles.append(np.pad(np.concatenate(parts[4:6], axis=1), ((0, 0), (0, BT - 4 * P))))
    heads = np.arange(HEADS)[:, None] * 2 * HD
    tiles.append(w_kv_up[:, np.concatenate([(heads + np.arange(HD)).reshape(-1), (heads + HD + np.arange(HD)).reshape(-1)])])
    return np.ascontiguousarray(np.stack(tiles))


def finish_stream(w_o, w_ff1, w_ff2):
    tiles = [weight_tile(w_o, i * P + np.arange(P)) for i in range(WO_TILES)]
    for g in range(GROUPS):
        tiles += [weight_tile(w_ff1, (g * GROUP + f) * P + np.arange(P)) for f in range(GROUP)]
        rows = w_ff2[g * GROUP * P:(g + 1) * GROUP * P]
        tiles += [weight_tile(rows, m * 2 * P + np.arange(2 * P)) for m in range(GROUP)]
    return np.ascontiguousarray(np.stack(tiles))


def program(nc, x_t, wproj, wfin, gain_mix, gain_lat, gains_fin, gate_bias, cos_t, sin_t, ident, ident_b, masks,
            masks_wide, scale, minus, plus, out_t):
    feat = nc.dram_tensor("feat", [ROWS, SEQ], F32).ap()
    v_fox = nc.dram_tensor("v_fox", [SEQ // P, P, HEADS * HD], F32).ap()
    v_mla = nc.dram_tensor("v_mla", [SEQ // P, P, HEADS * HD], F32).ap()
    aug_q = nc.dram_tensor("aug_q", [HEADS, AUG, SEQ], F32).ap()
    aug_k = nc.dram_tensor("aug_k", [HEADS, AUG, SEQ], F32).ap()
    inv_rows = nc.dram_tensor("inv_rows", [2 * HEADS, SEQ], F32).ap()
    o_t = nc.dram_tensor("o_t", [D_MODEL, SEQ], F32).ap()
    project(nc, x_t, wproj, gain_mix, gain_lat, gate_bias, cos_t, sin_t, ident,
            {"scale": scale, "minus": minus, "plus": plus}, feat, v_fox, v_mla, aug_q, aug_k)
    attend(nc, ident, ident_b, masks, masks_wide, feat, v_fox, v_mla, aug_q, aug_k, inv_rows, o_t)
    finish(nc, x_t, o_t, wfin, gains_fin, ident, out_t)


def shape_constants():
    bf16 = np.dtype(mybir.dt.np(BF16))
    half_rope = ROPE // 2
    inv = (np.float32(ROPE_THETA) ** (-np.arange(half_rope, dtype=np.float32) / np.float32(half_rope))).astype(np.float32)
    ang = inv[:, None] * np.arange(SEQ, dtype=np.float32)[None, :]
    i = np.arange(P)
    causal = i[None, :] <= i[:, None]
    chunked = (i // CHUNK)[None, :] <= (i // CHUNK)[:, None]
    masks = [np.where(m, 0.0, -1e30) for m in (causal, chunked)]
    wide = [np.concatenate([np.full((P, P), -1e30), m.T], axis=1) for m in masks]
    return {
        "cos_t": np.tile(np.cos(ang), (HEADS, 1)).astype(np.float32),
        "sin_t": np.tile(np.sin(ang), (HEADS, 1)).astype(np.float32),
        "ident": np.eye(P, dtype=np.float32),
        "ident_b": np.eye(P).astype(bf16),
        "masks": np.stack(masks, axis=1).astype(bf16),
        "masks_wide": np.stack(wide, axis=1).astype(bf16),
        "scale": np.tile(np.array([[HD ** -0.5, 1.0]], np.float32), (P, 1)),
        "minus": -np.ones((2, SEQ), np.float32),
        "plus": np.ones((2, SEQ), np.float32),
    }


def kernel(**inputs):
    import concourse.bacc as bacc
    from concourse.bass_utils import run_bass_kernel_spmd

    a = {k: np.asarray(v) for k, v in inputs.items()}
    arrays = {
        "x_t": a["x"][0].T,
        "wproj": projection_stream(a["w_in"][0], a["w_q_up"][0], a["w_kv_up"][0]),
        "wfin": finish_stream(a["w_o"][0], a["w_ff1"][0], a["w_ff2"][0]),
        "gain_mix": a["g_mix"][0].reshape(KC, P).T,
        "gain_lat": np.concatenate([a["g_q"][0], a["g_kv"][0]]).reshape(LATS, P).T,
        "gains_fin": np.stack([a["g_mlp"][0].reshape(KC, P), a["g_final"].reshape(KC, P)]).transpose(2, 0, 1),
        "gate_bias": a["b_f"][0][:, None],
        **shape_constants(),
    }
    arrays = {k: np.ascontiguousarray(v) for k, v in arrays.items()}
    nc = bacc.Bacc("TRN2", target_bir_lowering=False, num_devices=1)
    args = {k: nc.dram_tensor(k, v.shape, mybir.dt.from_np(v.dtype), kind="ExternalInput").ap() for k, v in arrays.items()}
    out_t = nc.dram_tensor("out_t", [D_MODEL, SEQ], F32, kind="ExternalOutput").ap()
    program(nc, **args, out_t=out_t)
    got = run_bass_kernel_spmd(nc, [arrays], core_ids=[0]).results[0]["out_t"]
    return np.ascontiguousarray(got.T)[None]
```

```python
from contextlib import ExitStack

import numpy as np
import concourse.bass as bass
from concourse import mybir

F32 = mybir.dt.float32
F32R = mybir.dt.float32r
BF16 = mybir.dt.bfloat16
ALU = mybir.AluOpType
ACT = mybir.ActivationFunctionType
AX_X = mybir.AxisListType.X

P = 128
SEQ, D_MODEL, D_FF = 2048, 1024, 4096
HEADS, HD = 8, 64
ROPE = 32
MLA_K = HD + ROPE
CHUNK = 64
EPS = 1e-6
ROPE_THETA = 10000.0
Q_LORA, KV_LORA = 256, 128

KC = D_MODEL // P
BT = 1024
NB = SEQ // BT
HALF = 512
TT = BT // P
LATS = (Q_LORA + KV_LORA) // P
RAW = 2
RING = 4
AHEAD = 64

ROW_Q, ROW_K = 0, HEADS * HD
ROW_QN, ROW_KN = 2 * HEADS * HD, 3 * HEADS * HD
ROW_QR1 = 4 * HEADS * HD
ROW_QR2 = ROW_QR1 + HEADS * ROPE // 2
ROW_KR1 = ROW_QR2 + HEADS * ROPE // 2
ROW_KR2 = ROW_KR1 + ROPE // 2
ROWS = ROW_KR2 + ROPE // 2
AUG = 4
MISC_KR1, MISC_KR2 = 32, 64

PROJ_TILES = 19
GROUP = 4
GROUPS = D_FF // P // GROUP
WO_TILES = D_MODEL // P
GROUP_TILES = 2 * GROUP
FIN_TILES = WO_TILES + GROUPS * GROUP_TILES


class Chain:

    def __init__(self, eng, sem, base, total):
        self.eng, self.sem, self.base, self.total, self.n = eng, sem, base, total, 0

    def __call__(self, instruction):
        self.n += 1
        instruction.then_inc(self.sem, 1)
        self.eng.wait_ge(self.sem, self.base + self.n)

    def close(self):
        assert self.n == self.total, (self.n, self.total)


def half(n):
    return slice(n * HALF, (n + 1) * HALF)


def project(nc, x_t, wproj, gains, lat_gains, gate_bias, cos_t, sin_t, ident, signs,
            feat, v_fox, v_mla, aug_q, aug_k):
    with ExitStack() as ctx:
        def sb(name, shape, dt=F32):
            return ctx.enter_context(nc.sbuf_tensor("p_" + name, shape, dt))

        def ps(name, shape):
            return ctx.enter_context(nc.psum_tensor("p_" + name, shape, F32))

        def sem(name):
            return ctx.enter_context(nc.semaphore("p_" + name))

        XRING = 4
        x_sb = sb("x", [P, XRING, BT])
        act_hi, act_lo = sb("act_hi", [P, KC, BT], F32R), sb("act_lo", [P, KC, BT], F32R)
        w_raw = sb("w_raw", [P, RAW, BT])
        w_hi, w_lo = sb("w_hi", [P, RING, BT], F32R), sb("w_lo", [P, RING, BT], F32R)
        stage = sb("stage", [P, 2, BT])
        rstd = sb("rstd", [P, 2, BT])
        RSTD_OF = {"x": 0, "q": 1, "kv": 0}
        lat = sb("lat", [P, LATS, BT])
        lat_hi, lat_lo = sb("lat_hi", [P, LATS, BT], F32R), sb("lat_lo", [P, LATS, BT], F32R)
        trig = sb("trig", [P, 2, BT])
        square, sumsq, diag = sb("square", [P, BT]), sb("sumsq", [P, BT]), sb("diag", [P, BT])
        misc = sb("misc", [P, 3, BT])
        gate, rot = misc[0:HEADS], misc[MISC_KR1:MISC_KR1 + ROPE // 2]
        small = sb("small", [P, 4, TT])
        rstd_t = sb("rstd_t", [P, 3, TT])
        carry = sb("carry", [HEADS, 1])
        ones = sb("ones", [P, P])
        ident_sb = sb("ident", [P, P])
        gains_sb, lat_gains_sb = sb("gains", [P, KC]), sb("lat_gains", [P, LATS])
        bias_sb, scale_sb = sb("bias", [HEADS, 1]), sb("scale", [P, 2])

        pairs = ps("pairs", [P, 2, 2, HALF])
        ps_sum = ps("sum", [P, HALF])
        ps_row = ps("row", [P, 2, HALF])

        gains_landed, const_landed, consts_set = sem("gains_landed"), sem("const_landed"), sem("consts_set")
        x_landed = [sem(f"x_landed{i}") for i in range(XRING)]
        w_landed = [sem(f"w_landed{i}") for i in range(RAW)]
        trig_landed = sem("trig_landed")
        x_split, square_done, sumsq_step = sem("x_split"), sem("square_done"), sem("sumsq_step")
        act_ready = sem("act_ready")
        w_half, w_ready = sem("w_half"), sem("w_ready")
        pair_done, pair_read = sem("pair_done"), sem("pair_read")
        sums_done, var_done, dev_done = sem("sums_done"), sem("var_done"), sem("dev_done")
        diag_done, row_done, rstd_done = sem("diag_done"), sem("row_done"), sem("rstd_done")
        lat_split, lat_ready = sem("lat_split"), sem("lat_ready")
        gate_in, gate_log, gate_done = sem("gate_in"), sem("gate_log"), sem("gate_done")
        rope_done, q_rope_done, pool_step = sem("rope_done"), sem("q_rope_done"), sem("pool_step")
        act_step, dve_step = sem("act_step"), sem("dve_step")
        stored = [sem(f"stored{i}") for i in range(2)]
        misc_stored, ones_stored, q_rope_stored = sem("misc_stored"), sem("ones_stored"), sem("q_rope_stored")

        V_PAIRS = TT // 2
        QN_PAIRS, KN_PAIRS = HEADS * HD // P, HEADS * HD // P
        N_PAIRS = 4 + 8 + V_PAIRS + QN_PAIRS + 2 + KN_PAIRS + V_PAIRS
        N_STAGED = N_PAIRS - 4 - 2
        N_SQUARES = KC + LATS
        V_DONE = 12 + V_PAIRS
        USED = {i: i + 1 for i in range(12)} | {i: V_DONE for i in range(12, 16)}
        USED |= {12: 14, 13: 14, 16: V_DONE + QN_PAIRS, 17: V_DONE + QN_PAIRS + 2, 18: N_PAIRS}
        LEFT = {i % RING: USED[i] for i in range(PROJ_TILES - RING, PROJ_TILES)}
        SLOT_LOADS = [len(range(s, PROJ_TILES, RAW)) for s in range(RAW)]
        NORMS = ("x", "q", "kv")

        with nc.Block() as block:
            @block.sync
            def _(sp):
                for count in (*stored, q_rope_stored, misc_stored):
                    sp.sem_inc(count, AHEAD)
                def load_w(b, i, j=0):
                    sp.wait_ge(w_ready, AHEAD + b * PROJ_TILES + j * 4 + i - RAW + 1)
                    slot = i % RAW
                    src = wproj[i] if isinstance(j, int) else wproj[bass.ds(j * 4 + i, 1)].rearrange("o p c -> p (o c)")
                    sp.dma_start(w_raw[:, slot, :], src).then_inc(w_landed[slot], 16)

                def store(b, n, dst, j=0, tokens=0):
                    read = n + 4 if n < 8 + V_PAIRS + QN_PAIRS else n + 6
                    sp.wait_ge(pair_read, AHEAD + b * N_PAIRS + j * 4 + read + 1)
                    src = stage[:, n % 2, :]
                    src = src.rearrange("p (t c) -> p t c", t=tokens) if tokens else src
                    sp.dma_start(dst, src).then_inc(stored[n % 2], 16)

                sp.dma_start(gains_sb[:, :], gains).then_inc(gains_landed, 16)
                for dst, src in ((ident_sb[:, :], ident), (lat_gains_sb[:, :], lat_gains),
                                 (bias_sb[:, :], gate_bias), (scale_sb[:, :], signs["scale"])):
                    sp.dma_start(dst, src).then_inc(const_landed, 16)
                with sp.Fori(0, NB) as b:
                    tok = bass.ds(b * BT, BT)
                    sp.wait_ge(q_rope_done, AHEAD + b)
                    sp.dma_start(trig[:, 0, :], cos_t[:, tok]).then_inc(trig_landed, 16)
                    sp.dma_start(trig[:, 1, :], sin_t[:, tok]).then_inc(trig_landed, 16)
                    for i in range(RAW, 4 + RAW):
                        load_w(b, i)
                    with sp.Fori(0, 2) as j:
                        for s in range(4):
                            load_w(b, 4 + RAW + s, j)
                            store(b, s, feat[bass.ds(j * (4 * P) + s * P, P), tok], j)
                    for i in range(14, 18):
                        load_w(b, i)
                    sp.wait_ge(gate_done, b + 1)
                    for n, plane in enumerate((2, 0)):
                        sp.dma_start(aug_q[:, n, tok], gate[:, plane, :]).then_inc(misc_stored, 16)
                        sp.dma_start(aug_k[:, 2 + n, tok], gate[:, plane, :]).then_inc(misc_stored, 16)
                    sp.wait_ge(rope_done, b + 1)
                    sp.dma_start(feat[ROW_KR1:ROW_KR1 + ROPE // 2, tok], rot[:, 2, :]).then_inc(misc_stored, 16)
                    sp.dma_start(feat[ROW_KR2:ROW_KR2 + ROPE // 2, tok], rot[:, 0, :]).then_inc(misc_stored, 16)
                    n = 8
                    for m in range(V_PAIRS):
                        cols = slice(m // 2 * 2 * P, (m // 2 + 1) * 2 * P)
                        store(b, n, v_fox[bass.ds(b * TT + m % 2 * 4, 4), :, cols].rearrange("t p c -> p t c"), tokens=4)
                        n += 1
                    load_w(b, 18)
                    for m in range(QN_PAIRS):
                        store(b, n, feat[ROW_QN + m * P:ROW_QN + (m + 1) * P, tok])
                        n += 1
                    for m in range(KN_PAIRS):
                        store(b, n, feat[ROW_KN + m * P:ROW_KN + (m + 1) * P, tok])
                        n += 1
                    for m in range(V_PAIRS):
                        store(b, n, v_mla[bass.ds(b * TT + 2 * m, 2)].rearrange("t p c -> p t c"), tokens=2)
                        n += 1
                    sp.wait_ge(q_rope_done, AHEAD + b + 1)
                    sp.dma_start(feat[ROW_QR1:ROW_QR1 + P, tok], lat[:, 2, :]).then_inc(q_rope_stored, 16)
                    sp.dma_start(feat[ROW_QR2:ROW_QR2 + P, tok], lat[:, 0, :]).then_inc(q_rope_stored, 16)
                sp.dma_start(aug_q[:, 2:4, :], signs["minus"]).then_inc(ones_stored, 16)
                sp.dma_start(aug_k[:, 0:2, :], signs["plus"]).then_inc(ones_stored, 16)
                for s in range(2):
                    sp.wait_ge(stored[s], AHEAD + 16 * NB * (N_STAGED // 2))
                sp.wait_ge(misc_stored, AHEAD + 16 * 6 * NB)
                sp.wait_ge(q_rope_stored, AHEAD + 16 * 2 * NB)
                sp.wait_ge(ones_stored, 16 * 2)

            @block.gpsimd
            def _(pool):
                for count in (w_ready, q_rope_done):
                    pool.sem_inc(count, AHEAD)
                pool.wait_ge(consts_set, 1)
                with pool.Fori(0, NB) as b:
                    for i in range(PROJ_TILES):
                        raw, slot = i % RAW, i % RING
                        pool.wait_ge(w_landed[raw], b * (16 * SLOT_LOADS[raw]) + 16 * (i // RAW + 1))
                        pool.wait_ge(pair_done, AHEAD + b * N_PAIRS + (USED[i - RING] if i >= RING else LEFT[slot] - N_PAIRS))
                        nc.gpsimd.tensor_tensor(w_hi[:, slot, :], w_raw[:, raw, :], ones[:, 0:1].to_broadcast([P, BT]),
                                                ALU.mult).then_inc(w_half, 1)
                        pool.wait_ge(w_half, b * PROJ_TILES + i + 1)
                        nc.gpsimd.tensor_tensor(w_lo[:, slot, :], w_raw[:, raw, :], w_hi[:, slot, :].bitcast(F32),
                                                ALU.subtract).then_inc(w_ready, 1)
                    pool.wait_ge(pair_read, AHEAD + b * N_PAIRS + (V_DONE + QN_PAIRS + 2))
                    pool.wait_ge(trig_landed, b * 32 + 32)
                    link = Chain(pool, pool_step, b * 3, 3)
                    x1, x2, out = (lat[:, k, :] for k in range(3))
                    tmp, cos, sin = diag[:, :], trig[:, 0, :], trig[:, 1, :]
                    nc.gpsimd.tensor_tensor(out, x1, cos, ALU.mult)
                    link(nc.gpsimd.tensor_tensor(tmp, x2, sin, ALU.mult))
                    link(nc.gpsimd.tensor_tensor(out, out, tmp, ALU.subtract))
                    nc.gpsimd.tensor_tensor(tmp, x2, cos, ALU.mult)
                    link(nc.gpsimd.tensor_tensor(x1, x1, sin, ALU.mult))
                    nc.gpsimd.tensor_tensor(x1, x1, tmp, ALU.add).then_inc(q_rope_done, 1)
                    link.close()

            @block.scalar
            def _(act):
                for count in (rstd_done,):
                    act.sem_inc(count, AHEAD)
                def deviation(b, norm):
                    n = NORMS.index(norm)
                    act.wait_ge(var_done, b * 3 + n + 1)
                    nc.scalar.activation(small[:, 1, :], small[:, 0, :], ACT.Sqrt).then_inc(dev_done, 1)
                    act.wait_ge(row_done, AHEAD + b * 3 + n + 1)
                    nc.scalar.activation(rstd[:, RSTD_OF[norm], :], ps_row[:, :, :].rearrange("p a c -> p (a c)"),
                                         ACT.Copy).then_inc(rstd_done, 1)

                def squared(b, n, src):
                    act.wait_ge(sumsq_step, AHEAD + b * N_SQUARES + n)
                    nc.scalar.activation(square[:, :], src, ACT.Square).then_inc(square_done, 1)

                with act.Fori(0, NB) as b:
                    tok = bass.ds(b * BT, BT)

                    def load_x(c):
                        act.wait_ge(sumsq_step, AHEAD + b * N_SQUARES + max(c - XRING + 1, 0))
                        act.dma_start(x_sb[:, c % XRING, :], x_t[c * P:(c + 1) * P, tok]).then_inc(x_landed[c % XRING], 16)

                    act.wait_ge(w_ready, AHEAD + b * PROJ_TILES)
                    for slot in range(RAW):
                        act.dma_start(w_raw[:, slot, :], wproj[slot]).then_inc(w_landed[slot], 16)
                        load_x(slot)
                    for c in range(RAW, XRING):
                        load_x(c)
                    act.wait_ge(pair_done, AHEAD + b * N_PAIRS - (N_PAIRS - V_DONE))
                    act.wait_ge(gains_landed, 16)
                    for c in range(KC):
                        act.wait_ge(x_landed[c % XRING], b * (16 * KC // XRING) + 16 * (c // XRING + 1))
                        nc.scalar.activation(act_hi[:, c, :], x_sb[:, c % XRING, :], ACT.Identity,
                                             scale=gains_sb[:, c:c + 1]).then_inc(x_split, 1)
                        squared(b, c, x_sb[:, c % XRING, :])
                        if c + XRING - 1 in range(XRING, KC):
                            load_x(c + XRING - 1)
                    deviation(b, "x")
                    act.wait_ge(const_landed, 16 * 4)
                    for i in range(LATS):
                        act.wait_ge(pair_read, AHEAD + b * N_PAIRS + i + 1)
                        nc.scalar.activation(lat_hi[:, i, :], lat[:, i, :], ACT.Identity,
                                             scale=lat_gains_sb[:, i:i + 1]).then_inc(lat_split, 1)
                        squared(b, KC + i, lat[:, i, :])
                    act.wait_ge(gate_in, b + 1)
                    nc.scalar.activation(gate[:, 1, :], gate[:, 1, :], ACT.Exp).then_inc(act_step, 1)
                    act.wait_ge(act_step, b + 1)
                    nc.scalar.activation(gate[:, 1, :], gate[:, 1, :], ACT.Ln, bias=1.0).then_inc(gate_log, 1)
                    deviation(b, "q")
                    deviation(b, "kv")

            @block.vector
            def _(dve):
                for count in (sumsq_step, pair_read):
                    dve.sem_inc(count, AHEAD)
                STEPS = 3 * 5 + 1 + 3 + 3
                nc.vector.memset(carry[:, :], 0.0)
                nc.vector.memset(ones[:, :], 1.0).then_inc(consts_set, 1)
                dve.wait_ge(consts_set, 1)
                dve.wait_ge(gains_landed, 16)
                with dve.Fori(0, NB) as b:
                    link = Chain(dve, dve_step, b * STEPS, STEPS)

                    def add_square(n, first):
                        dve.wait_ge(square_done, b * N_SQUARES + n + 1)
                        if first:
                            op = nc.vector.tensor_copy(sumsq[:, :], square[:, :])
                        else:
                            dve.wait_ge(sumsq_step, AHEAD + b * N_SQUARES + n)
                            op = nc.vector.tensor_tensor(sumsq[:, :], sumsq[:, :], square[:, :], ALU.add)
                        op.then_inc(sumsq_step, 1)

                    def reciprocal_root(norm, width):
                        n = NORMS.index(norm)
                        dve.wait_ge(sums_done, b * 3 + n + 1)
                        var, dev, a = small[:, 0, :], small[:, 1, :], small[:, 2, :]
                        nc.vector.tensor_scalar(var, ps_sum[:, n * TT:(n + 1) * TT], 1.0 / width, EPS,
                                                ALU.mult, ALU.add).then_inc(var_done, 1)
                        dve.wait_ge(dev_done, b * 3 + n + 1)
                        r = rstd_t[:, n, :]
                        link(nc.vector.reciprocal(r, dev))
                        link(nc.vector.tensor_tensor(a, r, r, ALU.mult))
                        link(nc.vector.tensor_tensor(a, a, var, ALU.mult))
                        link(nc.vector.tensor_scalar(a, a, -0.5, 1.5, ALU.mult, ALU.add))
                        link(nc.vector.tensor_tensor(r, r, a, ALU.mult))
                        if norm == "x":
                            dve.wait_ge(q_rope_done, AHEAD + b)
                        dve.wait_ge(row_done, AHEAD + b * 3 + n)
                        nc.vector.tensor_tensor(
                            diag[:, :].rearrange("p (t c) -> p t c", t=TT),
                            ident_sb[:, :].unsqueeze(1).to_broadcast([P, TT, P]),
                            r.unsqueeze(2).to_broadcast([P, TT, P]), ALU.mult).then_inc(diag_done, 1)

                    def pair(n, j=0):
                        dve.wait_ge(pair_done, AHEAD + b * N_PAIRS + j * 4 + n + 1)
                        return pairs[:, n % 2, :, :].rearrange("p a c -> p (a c)")

                    def free_stage(n, j=0):
                        dve.wait_ge(stored[n % 2], AHEAD + b * (16 * N_STAGED // 2) + j * 32 + 16 * (n // 2))

                    for c in range(KC):
                        dve.wait_ge(x_split, b * KC + c + 1)
                        nc.vector.scalar_tensor_tensor(act_lo[:, c, :], x_sb[:, c % XRING, :], gains_sb[:, c:c + 1],
                                                       act_hi[:, c, :].bitcast(F32), ALU.mult,
                                                       ALU.subtract).then_inc(act_ready, 1)
                        add_square(c, c == 0)
                    dve.wait_ge(const_landed, 16 * 4)
                    reciprocal_root("x", D_MODEL)
                    dve.wait_ge(rstd_done, AHEAD + b * 3 + 1)
                    dve.wait_ge(q_rope_stored, AHEAD + b * 32)
                    dve.wait_ge(misc_stored, AHEAD + b * 96)
                    for i in range(LATS):
                        src = pair(i)
                        nc.vector.tensor_tensor(lat[:, i, :], src, rstd[:, 0, :], ALU.mult).then_inc(pair_read, 1)
                    src = pair(LATS)
                    nc.vector.tensor_tensor(gate[:, 0, :], src[0:HEADS], rstd[0:HEADS, 0, :], ALU.mult)
                    for plane, row in enumerate((MISC_KR1, MISC_KR2)):
                        end = row + ROPE // 2
                        last = nc.vector.tensor_tensor(rot[:, plane, :], src[row:end], rstd[row:end, 0, :], ALU.mult)
                    last.then_inc(pair_read, 1)
                    dve.wait_ge(pair_read, AHEAD + b * N_PAIRS + 4)
                    for i in range(LATS):
                        dve.wait_ge(lat_split, b * LATS + i + 1)
                        nc.vector.scalar_tensor_tensor(lat_lo[:, i, :], lat[:, i, :], lat_gains_sb[:, i:i + 1],
                                                       lat_hi[:, i, :].bitcast(F32), ALU.mult,
                                                       ALU.subtract).then_inc(lat_ready, 1)
                        if i < 2:
                            add_square(KC + i, i == 0)
                    link(nc.vector.tensor_scalar(gate[:, 0, :], gate[:, 0, :], bias_sb[:, 0:1], None, ALU.add))
                    nc.vector.scalar_tensor_tensor(gate[:, 1, :], gate[:, 0, :], -1.0, gate[:, 0, :], ALU.mult,
                                                   ALU.min).then_inc(gate_in, 1)
                    dve.wait_ge(trig_landed, b * 32 + 32)

                    kr = slice(MISC_KR1, MISC_KR1 + ROPE // 2)
                    x1, x2, out = (rot[:, k, :] for k in range(3))
                    tmp, cos, sin = diag[kr, :], trig[kr, 0, :], trig[kr, 1, :]
                    nc.vector.tensor_tensor(out, x1, cos, ALU.mult)
                    link(nc.vector.tensor_tensor(tmp, x2, sin, ALU.mult))
                    link(nc.vector.tensor_tensor(out, out, tmp, ALU.subtract))
                    nc.vector.tensor_tensor(tmp, x2, cos, ALU.mult)
                    link(nc.vector.tensor_tensor(x1, x1, sin, ALU.mult))
                    nc.vector.tensor_tensor(x1, x1, tmp, ALU.add).then_inc(rope_done, 1)
                    dve.wait_ge(gate_log, b + 1)
                    link(nc.vector.scalar_tensor_tensor(gate[:, 0, :], gate[:, 0, :], 0.0, gate[:, 1, :], ALU.min,
                                                        ALU.subtract))
                    link(nc.vector.tensor_tensor_scan(gate[:, 1, :], gate[:, 0, :], gate[:, 0, :], carry[:, 0:1],
                                                      ALU.add, ALU.bypass))
                    nc.vector.tensor_copy(carry[:, :], gate[:, 1, BT - 1:BT])
                    link(nc.vector.tensor_copy(gate[:, 2, :].bitcast(F32R), gate[:, 1, :]))
                    nc.vector.tensor_tensor(gate[:, 0, :], gate[:, 1, :], gate[:, 2, :],
                                            ALU.subtract).then_inc(gate_done, 1)

                    with dve.Fori(0, 2) as j:
                        for s in range(4):
                            src = pair(4 + s, j)
                            free_stage(s, j)
                            nc.vector.scalar_tensor_tensor(stage[:, s % 2, :], src, scale_sb[:, bass.ds(j, 1)],
                                                           rstd[:, 0, :], ALU.mult, ALU.mult).then_inc(pair_read, 1)

                    def values(n, norm, m):
                        src = pair(n)
                        staged = n - 4 if norm == 0 else n - 6
                        free_stage(staged)
                        first, tiles = (4 * (m % 2), 4) if norm == 0 else (2 * m, 2)
                        src = src.rearrange("p (t c) -> p t c", t=tiles)
                        dst = stage[:, staged % 2, :].rearrange("p (t c) -> p t c", t=tiles)
                        for h in range(tiles):
                            last = nc.vector.tensor_scalar(dst[:, h, :], src[:, h, :],
                                                           rstd_t[:, norm, first + h:first + h + 1], None, ALU.mult)
                        last.then_inc(pair_read, 1)

                    reciprocal_root("q", Q_LORA)
                    n = 12
                    for m in range(V_PAIRS):
                        if m == 1:
                            add_square(KC + 2, True)
                        if m == 2:
                            reciprocal_root("kv", KV_LORA)
                        values(n, 0, m)
                        n += 1
                    dve.wait_ge(rstd_done, AHEAD + b * 3 + 2)
                    for m in range(QN_PAIRS + 2):
                        src = pair(n)
                        if m < QN_PAIRS:
                            free_stage(n - 4)
                            dst = stage[:, n % 2, :]
                        else:
                            dst = lat[:, m - QN_PAIRS, :]
                        nc.vector.scalar_tensor_tensor(dst, src, MLA_K ** -0.5, rstd[:, 1, :], ALU.mult,
                                                       ALU.mult).then_inc(pair_read, 1)
                        n += 1
                    dve.wait_ge(rstd_done, AHEAD + b * 3 + 3)
                    for m in range(KN_PAIRS):
                        src = pair(n)
                        free_stage(n - 6)
                        nc.vector.tensor_tensor(stage[:, n % 2, :], src, rstd[:, 0, :], ALU.mult).then_inc(pair_read, 1)
                        n += 1
                    for m in range(V_PAIRS):
                        values(n, 2, m)
                        n += 1
                    assert n == N_PAIRS
                    link.close()

            @block.tensor
            def _(pe):
                for count in (pair_done, row_done):
                    pe.sem_inc(count, AHEAD)
                BEHIND = 3

                def tile_product(out, w_slot, w_cols, hi, lo, chunks, only=None):
                    for c in range(chunks) if only is None else [only]:
                        cols = w_cols(c)
                        for n in range(2):
                            for k, (w, a) in enumerate(((w_hi, hi), (w_hi, lo), (w_lo, hi))):
                                last = nc.tensor.matmul(out[:, n, :], w[:, w_slot, cols], a[:, c, half(n)],
                                                        start=c == 0 and k == 0, stop=c == chunks - 1 and k == 2)
                    return last

                def by_chunk(c):
                    return slice(c * P, (c + 1) * P)

                pe.wait_ge(consts_set, 1)
                with pe.Fori(0, NB) as b:
                    def wait_w(i, j=0):
                        pe.wait_ge(w_ready, AHEAD + b * PROJ_TILES + j * 4 + i + 1)

                    def out(n, j=0):
                        pe.wait_ge(pair_read, AHEAD + b * N_PAIRS + (j * 4 + n - 1 if n >= 2 else 0))
                        return pairs[:, n % 2, :, :]

                    def sums(norm):
                        n = NORMS.index(norm)
                        pe.wait_ge(sumsq_step, AHEAD + b * N_SQUARES + (KC, KC + 2, KC + 3)[n])
                        for t in range(TT):
                            last = nc.tensor.matmul(ps_sum[:, n * TT + t:n * TT + t + 1], sumsq[:, t * P:(t + 1) * P],
                                                    ones[:, 0:1], start=True, stop=True)
                        last.then_inc(sums_done, 1)

                    def row(norm):
                        n = NORMS.index(norm)
                        pe.wait_ge(diag_done, b * 3 + n + 1)
                        pe.wait_ge(rstd_done, AHEAD + b * 3 + n)
                        for h in range(2):
                            last = nc.tensor.matmul(ps_row[:, h, :], ones[:, :], diag[:, half(h)], start=True, stop=True)
                        last.then_inc(row_done, 1)

                    wait_w(0)
                    banks = [out(0), out(1)]
                    for c in range(KC + BEHIND):
                        if c < KC:
                            pe.wait_ge(act_ready, b * KC + c + 1)
                            last = tile_product(banks[0], 0, by_chunk, act_hi, act_lo, KC, only=c)
                            if c == KC - 1:
                                last.then_inc(pair_done, 1)
                        if c == BEHIND:
                            wait_w(1)
                        if c == KC:
                            sums("x")
                        if c >= BEHIND:
                            last = tile_product(banks[1], 1, by_chunk, act_hi, act_lo, KC, only=c - BEHIND)
                    last.then_inc(pair_done, 1)
                    row("x")
                    for i in range(2, 4):
                        wait_w(i)
                        tile_product(out(i), i, by_chunk, act_hi, act_lo, KC).then_inc(pair_done, 1)
                    with pe.Fori(0, 2) as j:
                        for s in range(4):
                            wait_w(4 + s, j)
                            tile_product(out(4 + s, j), s, by_chunk, act_hi, act_lo, KC).then_inc(pair_done, 1)
                    sums("q")
                    n = 12
                    for m in range(V_PAIRS):
                        s = 2 * (m // 2)
                        if m % 2 == 0:
                            wait_w(12 + s + 1)
                        banks = out(n)
                        for q in range(4):
                            tokens = slice((4 * (m % 2) + q) * P, (4 * (m % 2) + q + 1) * P)
                            for c in range(KC):
                                for k, (w, a) in enumerate(((w_hi, act_hi), (w_hi, act_lo), (w_lo, act_hi))):
                                    last = nc.tensor.matmul(banks[:, q // 2, q % 2 * 2 * P:(q % 2 + 1) * 2 * P],
                                                            a[:, c, tokens], w[:, s:s + 2, by_chunk(c)],
                                                            start=c == 0 and k == 0, stop=c == KC - 1 and k == 2)
                        last.then_inc(pair_done, 1)
                        n += 1
                        if m == 0:
                            row("q")
                        if m == 1:
                            sums("kv")
                        if m == 2:
                            row("kv")
                    pe.wait_ge(lat_ready, b * LATS + LATS)
                    for m in range(QN_PAIRS + 2):
                        i, at = (16, m) if m < QN_PAIRS else (17, m - QN_PAIRS)
                        if at == 0:
                            wait_w(i)
                        last = tile_product(out(n), i % RING, lambda c: slice((2 * at + c) * P, (2 * at + c + 1) * P),
                                            lat_hi, lat_lo, 2)
                        last.then_inc(pair_done, 1)
                        n += 1
                    wait_w(18)
                    for m in range(KN_PAIRS):
                        last = tile_product(out(n), 18 % RING, lambda c: slice(m * P, (m + 1) * P),
                                            lat_hi[:, 2:3, :], lat_lo[:, 2:3, :], 1)
                        last.then_inc(pair_done, 1)
                        n += 1
                    for m in range(V_PAIRS):
                        banks = out(n)
                        for h in range(2):
                            tokens = slice((2 * m + h) * P, (2 * m + h + 1) * P)
                            for k, (w, a) in enumerate(((w_hi, lat_hi), (w_hi, lat_lo), (w_lo, lat_hi))):
                                last = nc.tensor.matmul(banks[:, h, :], a[:, 2, tokens], w[:, 18 % RING, HALF:],
                                                        start=k == 0, stop=k == 2)
                        last.then_inc(pair_done, 1)
                        n += 1


def attend(nc, ident, ident_b, masks, masks_wide, feat, v_fox, v_mla, aug_q, aug_k, inv_rows, o_t):
    with ExitStack() as ctx:
        def sb(name, shape, dt=F32):
            return ctx.enter_context(nc.sbuf_tensor("a_" + name, shape, dt))

        def ps(name, shape):
            return ctx.enter_context(nc.psum_tensor("a_" + name, shape, F32))

        def sem(name):
            return ctx.enter_context(nc.semaphore("a_" + name))

        QT = SEQ // P
        KB = HALF // P
        GR = SEQ // HALF
        UNITS = [(g, 2 * j) for g in range(GR) for j in range(2 * (g + 1))]
        NU = len(UNITS)
        LAST_UNIT = [max(u for u in range(NU) if UNITS[u][0] == g) for g in range(GR)]
        CHUNKS = [(i, c) for i in range(QT) for c in range(i // KB + 1)]
        NX = len(CHUNKS) + 1
        SLOTS = 4
        LEAD = 2
        ROW_M = (HD + AUG, MLA_K)
        ROUND_STEPS, HALF_STEPS = 4, (6, 4)
        QK_LOADS, MORE_LOADS = (16 * 2, 16 * 5), (16 * 3, 16)
        per = 3
        BESIDE = [[x for x in range(NX - 1) if x * 13 // (NX - 1) == u - 1] for u in range(NU)]
        NEGATE_AT, INVERT_AT = 13+1, 6
        START = 64

        qa, qb = sb("qa", [P, 2, SEQ], F32R), sb("qb", [P, 2, SEQ], F32R)
        ka, kb = sb("ka", [P, 2, SEQ], F32R), sb("kb", [P, 2, SEQ], F32R)
        q_raw, k_raw = sb("q_raw", [P, SEQ]), sb("k_raw", [P, SEQ])
        v_raw = sb("v_raw", [P, QT, HD])
        v_ones = sb("v_ones", [P, 2, QT, 2, HD], F32R)
        v_lo = sb("v_lo", [P, 2, QT, HD], F32R)
        e_full = sb("e_full", [P, 2, 2, HALF])
        e_hi, e_lo = sb("e_hi", [P, SLOTS, 2, HALF], F32R), sb("e_lo", [P, SLOTS, 2, HALF], F32R)
        o_raw = sb("o_raw", [P, 2, SEQ])
        o_fin = sb("o_fin", [HD, SEQ])
        sums_t, inv_t = sb("sums_t", [P, QT]), sb("inv_t", [P, QT])
        part_max, neg_max = sb("part_max", [P, QT, GR]), sb("neg_max", [P, QT])
        m_rows = sb("m_rows", [QT, P], F32R)
        ident_sb, ident_b_sb = sb("ident", [P, P]), sb("ident_b", [P, P], BF16)
        masks_sb, wide_sb = sb("masks", [P, 2, P], BF16), sb("masks_wide", [P, 2, 2 * P], BF16)
        ones = sb("ones", [P, 1])

        s_ps = ps("s", [P, 2, 2, HALF])
        x_ps = ps("x", [P, 2, HALF])
        o_ps = ps("o", [P, 2, HALF])

        const_landed, consts_set, rows_set = sem("const_landed"), sem("consts_set"), sem("rows_set")
        qk_landed, more_landed, row_landed = sem("qk_landed"), sem("more_landed"), sem("row_landed")
        gates_landed = [sem(f"gates_landed{p}") for p in range(2)]
        rounded, halved = sem("rounded"), sem("halved")
        x_scored, x_read, max_done = sem("x_scored"), sem("x_read"), sem("max_done")
        scored, exped, split, weighed = sem("scored"), sem("exped"), sem("split"), sem("weighed")
        o_read, sums_landed, inverted = sem("o_read"), sem("sums_landed"), sem("inverted")
        last_inverted = sem("last_inverted")
        inv_landed, divided, stored = sem("inv_landed"), sem("divided"), sem("stored")

        def at(n, per, plus=0):
            it, heads = n
            if it is None:
                return START + heads * per + plus
            return it * (2 * per) + (START + heads * per + plus)

        def has_before(n):
            return n[0] is not None or n[1] > 0

        def has_before(n):
            return n[0] is not None or n[1] > 0

        LAST = (None, 2 * HEADS - 1)

        def is_last(n):
            return n[0] is None and n[1] == LAST[1]

        def later(n, heads):
            return n[0], n[1] + heads

        def every_head(eng, run):
            run((None, 0))
            with eng.Fori(0, 2) as it:
                run((it, 1))
                run((it, 2))
            for head in range(5, HEADS):
                run((None, head))
            with eng.Fori(0, 3) as it:
                run((it, HEADS))
                run((it, HEADS + 1))
            for head in range(2 * HEADS - 2, 2 * HEADS):
                run((None, head))

        def kind(n, heads=0):
            total = n[1] + heads
            if n[0] is None:
                return None if not 0 <= total < 2 * HEADS else int(total >= HEADS)
            return int(n[1] >= HEADS)

        def both(n, fox, mla, plus=0):
            return at(n, mla, HEADS * (fox - mla) + plus) if kind(n) else at(n, fox, plus)

        def of_kind(n):
            h = n[1] - HEADS * kind(n)
            return h if n[0] is None else n[0] * 2 + h

        def span(h, size, first=0):
            return slice(first + h * size, first + (h + 1) * size) if isinstance(h, int) else bass.ds(h * size + first, size)

        def group_cols(g):
            return slice(g * HALF, (g + 1) * HALF)

        def unit_cols(u):
            g, j = UNITS[u]
            return slice(HALF // 2 if j == g * KB + 2 else 0, HALF)

        def block_cols(u, b):
            g, j = UNITS[u]
            return slice(P, HALF) if (j, b) == (g * KB, 1) else unit_cols(u)

        with nc.Block() as block:
            @block.sync
            def _(sp):
                for count in (qk_landed, more_landed, *gates_landed, row_landed, sums_landed, inv_landed, stored):
                    sp.sem_inc(count, START)
                for dst, src in ((ident_sb[:, :], ident), (ident_b_sb[:, :], ident_b), (masks_sb[:, :, :], masks),
                                 (wide_sb[:, :, :], masks_wide)):
                    sp.dma_start(dst, src).then_inc(const_landed, 16)

                def rows(dst, row, h, size, count=qk_landed):
                    sp.dma_start(dst, feat[span(h, size, row), :]).then_inc(count, 16)

                def load(n, gates_between=False):
                    sp.wait_ge(halved, both(n, *HALF_STEPS))
                    h = of_kind(n)
                    if kind(n):
                        rows(q_raw[0:HD, :], ROW_QN, h, HD)
                        rows(k_raw[0:HD, :], ROW_KN, h, HD)
                        rows(q_raw[HD:HD + 16, :], ROW_QR1, h, 16)
                        rows(q_raw[HD + 16:MLA_K, :], ROW_QR2, h, 16)
                        sp.dma_start(k_raw[HD:MLA_K, :], feat[ROW_KR1:ROW_KR1 + ROPE, :]).then_inc(qk_landed, 16)
                    else:
                        rows(k_raw[0:HD, :], ROW_K, h, HD)
                        rows(q_raw[0:HD, :], ROW_Q, h, HD)
                        if gates_between:
                            sp.wait_ge(rows_set, 1)
                            gates(n)
                        rows(k_raw[HD:P, :], ROW_K, h, HD, more_landed)
                        rows(q_raw[HD:P, :], ROW_Q, h, HD, more_landed)
                    sp.dma_start(v_raw[:, :, :], (v_mla if kind(n) else v_fox)[:, :, span(h, HD)].rearrange("t p d -> p t d")
                                 ).then_inc(more_landed, 16)

                def gates(n):
                    par, h = n[1] % 2, of_kind(n)
                    sp.wait_ge(scored, at(n, NU, -NU))
                    for dst, src in ((qa, aug_q), (ka, aug_k)):
                        sp.dma_start(dst[HD:HD + AUG, par, :].bitcast(F32), src[span(h, 1)].rearrange("o r n -> (o r) n")
                                     ).then_inc(gates_landed[par], 16)

                def maximum_row(n):
                    sp.wait_ge(x_read, at(n, NX, NX))
                    row = ROW_M[kind(n)]
                    sp.dma_start(qa[row:row + 1, n[1] % 2, :].bitcast(F32), m_rows[:, :].bitcast(F32)).then_inc(row_landed, 16)

                def reciprocals(n):
                    sp.wait_ge(o_read, at(n, GR, GR))
                    sp.dma_start(sums_t[:, :], o_raw[HD:HD + 1, n[1] % 2, :]).then_inc(sums_landed, 16)
                    sp.wait_ge(inverted, at(n, 1, 1))
                    row = inv_rows[span(of_kind(n), 1, HEADS * kind(n)), :]
                    sp.dma_start(row.rearrange("o (p t) -> (o p) t", p=P), inv_t[:, :]).then_inc(stored, 16)
                    sp.wait_ge(stored, at(n, 32, 16))
                    sp.dma_start(o_fin[:, :], row.to_broadcast([HD, SEQ])).then_inc(inv_landed, 16)

                def store(n):
                    sp.wait_ge(divided, at(n, 1, 1))
                    sp.dma_start(o_t[span(of_kind(n), HD, HEADS * HD * kind(n)), :], o_fin[:, :]).then_inc(stored, 16)

                def beside(n):
                    if kind(n, 1) == 0:
                        gates(later(n, 1))
                    if has_before(n):
                        reciprocals(later(n, -1))
                    if kind(n, 2) is not None:
                        load(later(n, 2))
                    if has_before(n):
                        store(later(n, -1))
                    if kind(n, 1) is not None:
                        maximum_row(later(n, 1))

                first = (None, 0)
                load(first, gates_between=True)
                sp.wait_ge(rows_set, 2)
                load(later(first, 1))
                maximum_row(first)
                every_head(sp, beside)
                for g in range(GR):
                    sp.wait_ge(o_read, at(LAST, GR, g + 1))
                    sp.dma_start(o_t[LAST[1] * HD:(LAST[1] + 1) * HD, group_cols(g)], o_raw[0:HD, LAST[1] % 2, group_cols(g)]
                                 ).then_inc(stored, 16)
                sp.wait_ge(stored, at(LAST, 32, 16 * GR))

            @block.gpsimd
            def _(pool):
                pool.sem_inc(halved, START)
                pool.sem_inc(divided, START)
                pool.wait_ge(consts_set, 1)

                def copy(dst, src, first=0):
                    one = ones[first:first + src.shape[0], 0:1]
                    one = one.to_broadcast(src.shape) if len(src.shape) == 2 else one.unsqueeze(2).to_broadcast(src.shape)
                    return nc.gpsimd.tensor_tensor(dst, src, one, ALU.mult)

                def halve(n):
                    par, steps = n[1] % 2, 0
                    pool.wait_ge(qk_landed, both(n, *QK_LOADS, QK_LOADS[kind(n)]))
                    pool.wait_ge(more_landed, both(n, *MORE_LOADS, MORE_LOADS[kind(n)]))
                    pool.wait_ge(scored, at(n, NU, -NU))
                    if kind(n):
                        pool.wait_ge(rounded, at(n, ROUND_STEPS, ROUND_STEPS))
                        nc.gpsimd.tensor_tensor(kb[0:MLA_K, par, :], k_raw[0:MLA_K, :], ka[0:MLA_K, par, :].bitcast(F32),
                                                ALU.subtract).then_inc(halved, 1)
                        nc.gpsimd.tensor_tensor(qb[0:MLA_K, par, :], q_raw[0:MLA_K, :], qa[0:MLA_K, par, :].bitcast(F32),
                                                ALU.subtract).then_inc(halved, 1)
                        steps = 2
                    else:
                        copy(kb[:, par, :], k_raw[:, :]).then_inc(halved, 1)
                        pool.wait_ge(halved, both(n, *HALF_STEPS, 1))
                        nc.gpsimd.tensor_tensor(kb[HD:P, par, :], k_raw[HD:P, :], kb[HD:P, par, :].bitcast(F32),
                                                ALU.subtract).then_inc(halved, 1)
                        copy(qb[HD:P, par, :], q_raw[HD:P, :], HD).then_inc(halved, 1)
                        pool.wait_ge(halved, both(n, *HALF_STEPS, 3))
                        pool.wait_ge(rounded, at(n, ROUND_STEPS, ROUND_STEPS))
                        nc.gpsimd.tensor_tensor(qb[0:HD, par, :], q_raw[0:HD, :], qa[0:HD, par, :].bitcast(F32),
                                                ALU.subtract).then_inc(halved, 1)
                        steps = 4
                    pool.wait_ge(halved, both(n, *HALF_STEPS, steps))
                    pool.wait_ge(weighed, at(n, NU, -NU))
                    copy(v_ones[:, par, :, 0, :], v_raw[:, :, :]).then_inc(halved, 1)
                    pool.wait_ge(halved, both(n, *HALF_STEPS, steps + 1))
                    nc.gpsimd.tensor_tensor(v_lo[:, par, :, :], v_raw[:, :, :], v_ones[:, par, :, 0, :].bitcast(F32),
                                            ALU.subtract).then_inc(halved, 1)

                def divide(n):
                    pool.wait_ge(inv_landed, at(n, 16, 16))
                    nc.gpsimd.tensor_tensor(o_fin[:, :], o_raw[0:HD, n[1] % 2, :], o_fin[:, :], ALU.mult).then_inc(divided, 1)

                def beside(n):
                    if kind(n, 1) is not None:
                        halve(later(n, 1))
                    if has_before(n):
                        divide(later(n, -1))

                halve((None, 0))
                every_head(pool, beside)

            @block.scalar
            def _(act):
                for count in (rounded, exped, o_read):
                    act.sem_inc(count, START)
                nc.scalar.preload_act_table(ACT.Exp)

                def round_part(n, part):
                    width, tok = (MLA_K if kind(n) else HD), slice(part * SEQ // 2, (part + 1) * SEQ // 2)
                    if part == 0:
                        act.wait_ge(qk_landed, both(n, *QK_LOADS, QK_LOADS[kind(n)]))
                        act.wait_ge(scored, at(n, NU, -NU))
                        if kind(n):
                            act.wait_ge(rows_set, 2)
                    for dst, src in ((ka, k_raw), (qa, q_raw)):
                        nc.scalar.activation(dst[0:width, n[1] % 2, tok], src[0:width, tok], ACT.Copy).then_inc(rounded, 1)

                def exponentials(n, u):
                    act.wait_ge(scored, at(n, NU, u + 1))
                    act.wait_ge(weighed, at(n, NU, u + 1 - SLOTS))
                    src = s_ps[:, u % 2, :, unit_cols(u)]
                    nc.scalar.activation(e_hi[:, u % SLOTS, :, unit_cols(u)], src, ACT.Exp)
                    act.wait_ge(split, at(n, NU, u + 1 - 2))
                    nc.scalar.activation(e_full[:, u % 2, :, unit_cols(u)], src, ACT.Exp).then_inc(exped, 1)

                def read_output(n, g):
                    act.wait_ge(weighed, at(n, NU, LAST_UNIT[g] + 1))
                    if g == 0:
                        act.wait_ge(divided, at(n, 1, -1))
                    nc.scalar.activation(o_raw[:, n[1] % 2, group_cols(g)], o_ps[:, g % 2, :], ACT.Copy).then_inc(o_read, 1)

                def main(n):
                    for u in range(NU):
                        if kind(n, 1) is not None and u < 2:
                            round_part(later(n, 1), u)
                        if u + LEAD < NU:
                            exponentials(n, u + LEAD)
                        elif kind(n, 1) is not None:
                            exponentials(later(n, 1), u + LEAD - NU)
                        if u in LAST_UNIT and not is_last(n):
                            read_output(n, UNITS[u][0])

                first = (None, 0)
                for part in range(2):
                    round_part(first, part)
                for u in range(LEAD):
                    exponentials(first, u)
                every_head(act, main)

            @block.vector
            def _(dve):
                for count in (x_read, max_done, split, inverted):
                    dve.sem_inc(count, START)
                for par in range(2):
                    nc.vector.memset(ka[HD:P, par, :].bitcast(F32), 1.0).then_inc(rows_set, 1)
                nc.vector.memset(v_ones[:, :, :, 1, :].bitcast(F32), 1.0)
                nc.vector.memset(part_max[:, :, :], -3e38)
                nc.vector.memset(s_ps[:, :, 1, 0:P], 0.0)
                nc.vector.memset(ones[:, :], 1.0).then_inc(consts_set, 1)
                dve.wait_ge(consts_set, 1)

                def chunk_maximum(n, x):
                    i, c = CHUNKS[x]
                    w = min(HALF, (i + 1) * P - c * HALF)
                    dve.wait_ge(x_scored, at(n, NX, x + 1))
                    nc.vector.tensor_reduce(part_max[:, i, c:c + 1], x_ps[:, (n[1] + x) % 2, 0:w], AX_X, ALU.max
                                            ).then_inc(x_read, 1)

                def negate_maxima(n):
                    dve.wait_ge(x_read, at(n, NX, NX - 1))
                    nc.vector.tensor_reduce(neg_max[:, :], part_max[:, :, :], AX_X, ALU.max, negate=True).then_inc(max_done, 1)

                def maxima_rows(n):
                    dve.wait_ge(x_scored, at(n, NX, NX))
                    dve.wait_ge(row_landed, at(n, 16))
                    nc.vector.tensor_copy(m_rows[:, :], x_ps[0:QT, (n[1] + NX - 1) % 2, 0:P]).then_inc(x_read, 1)

                def low(n, u):
                    dve.wait_ge(exped, at(n, NU, u + 1))
                    cols = unit_cols(u)
                    nc.vector.tensor_tensor(e_lo[:, u % SLOTS, :, cols], e_full[:, u % 2, :, cols],
                                            e_hi[:, u % SLOTS, :, cols].bitcast(F32), ALU.subtract).then_inc(split, 1)

                def invert(n):
                    dve.wait_ge(sums_landed, at(n, 16, 16))
                    nc.vector.reciprocal(inv_t[:, :], sums_t[:, :]).then_inc(inverted, 1)

                def output(g):
                    dst = o_raw[0:HD, LAST[1] % 2, group_cols(g)]
                    if g == 0:
                        dve.wait_ge(divided, at(LAST, 1, -1))
                    dve.wait_ge(weighed, at(LAST, NU, LAST_UNIT[g] + 1))
                    nc.vector.reciprocal(dst, o_ps[HD:P, g % 2, :]).then_inc(last_inverted, 1)
                    dve.wait_ge(last_inverted, g + 1)
                    nc.vector.tensor_tensor(dst, o_ps[0:HD, g % 2, :], dst, ALU.mult).then_inc(o_read, 1)

                def main(n):
                    for u in range(NU):
                        if kind(n, 1) is not None:
                            for x in BESIDE[u][:2]:
                                chunk_maximum(later(n, 1), x)
                            if u == NEGATE_AT:
                                negate_maxima(later(n, 1))
                        if u + 1 < NU:
                            low(n, u + 1)
                        elif kind(n, 1) is not None:
                            low(later(n, 1), u + 1 - NU)
                        if kind(n, 1) is not None:
                            for x in BESIDE[u][2:]:
                                chunk_maximum(later(n, 1), x)
                        if kind(n, 1) is not None and u == NEGATE_AT:
                            maxima_rows(later(n, 1))
                        if u == INVERT_AT and has_before(n):
                            invert(later(n, -1))
                        if is_last(n) and u in LAST_UNIT:
                            output(UNITS[u][0])

                first = (None, 0)
                for x in range(NX - 1):
                    chunk_maximum(first, x)
                negate_maxima(first)
                maxima_rows(first)
                low(first, 0)
                every_head(dve, main)

            @block.tensor
            def _(pe):
                for count in (x_scored, scored, weighed):
                    pe.sem_inc(count, START)
                pe.wait_ge(const_landed, 16 * 4)
                pe.wait_ge(consts_set, 1)

                def chunk(n, x):
                    par, (i, c) = n[1] % 2, CHUNKS[x]
                    if x == 0:
                        if not kind(n):
                            pe.wait_ge(gates_landed[par], at(later(n, -par), 16, 32))
                        pe.wait_ge(rounded, at(n, ROUND_STEPS, ROUND_STEPS // 2))
                    if i == QT // 2 and c == 0:
                        pe.wait_ge(rounded, at(n, ROUND_STEPS, ROUND_STEPS))
                    pe.wait_ge(x_read, at(n, NX, x + 1 - 2))
                    width = MLA_K if kind(n) else HD + AUG
                    w = min(HALF, (i + 1) * P - c * HALF)
                    dst = x_ps[:, (n[1] + x) % 2, 0:w]
                    diagonal = c == i // KB
                    last = nc.tensor.matmul(dst, qa[0:width, par, i * P:(i + 1) * P], ka[0:width, par, c * HALF:c * HALF + w],
                                            start=True, stop=not diagonal)
                    if diagonal:
                        last = nc.tensor.matmul(dst[:, w - P:w], ident_b_sb[:, :], masks_sb[:, kind(n), :],
                                                start=False, stop=True)
                    last.then_inc(x_scored, 1)

                def turn_maxima(n):
                    pe.wait_ge(max_done, at(n, 1, 1))
                    nc.tensor.transpose(x_ps[0:QT, (n[1] + NX - 1) % 2, 0:P], neg_max[:, :], ident_sb[:, :]).then_inc(x_scored, 1)

                def scores(n, u):
                    par, latent, (g, j0) = n[1] % 2, kind(n), UNITS[u]
                    if u == 0:
                        pe.wait_ge(row_landed, at(n, 16, 16))
                        pe.wait_ge(halved, both(n, *HALF_STEPS, 2 if latent else 4))
                    pe.wait_ge(exped, at(n, NU, u + 1 - 2))
                    rows = ROW_M[latent] + 1
                    terms = [(ka[0:rows], qa[0:rows])]
                    if latent:
                        terms += [(ka[0:MLA_K], qb[0:MLA_K]), (kb[0:MLA_K], qa[0:MLA_K])]
                    else:
                        terms += [(kb, qb)]
                    for b in range(2):
                        j, cols = j0 + b, block_cols(u, b)
                        queries = slice(g * HALF + cols.start, (g + 1) * HALF)
                        diagonal = j0 >= g * KB
                        for m, (k, q) in enumerate(terms):
                            last = nc.tensor.matmul(s_ps[:, u % 2, b, cols], k[:, par, j * P:(j + 1) * P], q[:, par, queries],
                                                    start=m == 0, stop=m == len(terms) - 1 and not diagonal)
                        if diagonal:
                            own = (j - g * KB) * P
                            ahead = own - cols.start if b else 0
                            last = nc.tensor.matmul(s_ps[:, u % 2, b, own - ahead:own + P], ident_b_sb[:, :],
                                                    wide_sb[:, latent, P - ahead:2 * P], start=False, stop=True)
                    last.then_inc(scored, 1)

                def weigh(n, u, b):
                    par, (g, j0) = n[1] % 2, UNITS[u]
                    j, cols = j0 + b, block_cols(u, b)
                    if b == 0:
                        if u == 0:
                            pe.wait_ge(halved, both(n, *HALF_STEPS, HALF_STEPS[kind(n)]))
                        if j == 0:
                            pe.wait_ge(o_read, at(n, GR, g + 1 - 2))
                        pe.wait_ge(split, at(n, NU, u + 1))
                    dst = o_ps[:, g % 2, cols]
                    hi, lo = e_hi[:, u % SLOTS, b, cols], e_lo[:, u % SLOTS, b, cols]
                    nc.tensor.matmul(dst, v_ones[:, par, j, :, :], hi, start=j == 0, stop=False)
                    nc.tensor.matmul(dst[0:HD], v_lo[:, par, j, :], hi, start=False, stop=False)
                    last = nc.tensor.matmul(dst, v_ones[:, par, j, :, :], lo, start=False, stop=j == (g + 1) * KB - 1)
                    if b == 1:
                        last.then_inc(weighed, 1)

                def main(n):
                    for u in range(NU):
                        if u + LEAD < NU:
                            scores(n, u + LEAD)
                        elif kind(n, 1) is not None:
                            scores(later(n, 1), u + LEAD - NU)
                        more = BESIDE[u] if kind(n, 1) is not None else []
                        for x in more[:1]:
                            chunk(later(n, 1), x)
                        weigh(n, u, 0)
                        for x in more[1:2]:
                            chunk(later(n, 1), x)
                        weigh(n, u, 1)
                        for x in more[2:]:
                            chunk(later(n, 1), x)
                        if kind(n, 1) is not None and u == NEGATE_AT:
                            turn_maxima(later(n, 1))

                first = (None, 0)
                for x in range(NX - 1):
                    chunk(first, x)
                turn_maxima(first)
                for u in range(LEAD):
                    scores(first, u)
                every_head(pe, main)


def finish(nc, x_t, o_t, wfin, gains, ident, out_t):
    O_RING = 4
    with ExitStack() as ctx:
        def sb(name, shape, dt=F32):
            return ctx.enter_context(nc.sbuf_tensor("f_" + name, shape, dt))

        def ps(name, shape):
            return ctx.enter_context(nc.psum_tensor("f_" + name, shape, F32))

        def sem(name):
            return ctx.enter_context(nc.semaphore("f_" + name))

        x_sb = sb("x", [P, KC, BT])
        act_hi, act_lo = sb("act_hi", [P, KC, BT], F32R), sb("act_lo", [P, KC, BT], F32R)
        w_raw = sb("w_raw", [P, RAW, BT])
        w_hi, w_lo = sb("w_hi", [P, RING, BT], F32R), sb("w_lo", [P, RING, BT], F32R)
        r_hi, r_lo = sb("r_hi", [P, GROUP, BT], F32R), sb("r_lo", [P, GROUP, BT], F32R)
        hidden = sb("hidden", [P, 2, BT])
        o_raw = hidden[:, :, :].rearrange("p a (h n) -> p (a h) n", h=2)
        rstd = sb("rstd", [P, BT])
        square, sumsq, diag = sb("square", [P, BT]), sb("sumsq", [P, BT]), sb("diag", [P, BT])
        small = sb("small", [P, 4, TT])
        ones, ident_sb = sb("ones", [P, P]), sb("ident", [P, P])
        gains_sb = sb("gains", [P, 2, KC])

        pairs = ps("pairs", [P, 2, 2, HALF])
        ps_sum = ps("sum", [P, HALF])
        ps_row = ps("row", [P, 2, HALF])

        const_landed, consts_set = sem("const_landed"), sem("consts_set")
        x_landed = [sem(f"x_landed{c}") for c in range(KC)]
        o_landed = [sem(f"o_landed{i}") for i in range(O_RING)]
        o_half, o_ready, wo_done, wo_read = sem("o_half"), sem("o_ready"), sem("wo_done"), sem("wo_read")
        w_landed = [sem(f"w_landed{i}") for i in range(RAW)]
        w_half, w_ready = sem("w_half"), sem("w_ready")
        act_split, act_ready = sem("act_split"), sem("act_ready")
        square_done, sumsq_step = sem("square_done"), sem("sumsq_step")
        pair_done, pair_read = sem("pair_done"), sem("pair_read")
        sums_done, var_done, dev_done = sem("sums_done"), sem("var_done"), sem("dev_done")
        diag_done, row_done, rstd_done = sem("diag_done"), sem("row_done"), sem("rstd_done")
        hidden_squared, hidden_hi, hidden_ready = sem("hidden_squared"), sem("hidden_hi"), sem("hidden_ready")
        scaled, dve_step = sem("scaled"), sem("dve_step")
        stored = [sem(f"stored{i}") for i in range(2)]

        TILES = FIN_TILES
        G_PAIRS = GROUP + KC
        N_PAIRS = GROUPS * G_PAIRS
        LAST = GROUPS - 1
        NORMS = 2
        N_SQUARES = 3 * KC

        def w_slot(i):
            return (w_hi[:, i, :], w_lo[:, i, :]) if i < RING else (r_hi[:, i - RING, :], r_lo[:, i - RING, :])

        def w_half_bank(k):
            return pairs[:, k % 4 // 2, k % 2, :]

        with nc.Block() as block:
            @block.sync
            def _(sp):
                def load_w(b, i, g=0):
                    sp.wait_ge(w_ready, AHEAD + b * TILES + i - RAW + 1 + g * GROUP_TILES)
                    slot = i % RAW
                    src = wfin[i] if isinstance(g, int) else wfin[bass.ds(g * GROUP_TILES + i, 1)].rearrange("o p c -> p (o c)")
                    sp.dma_start(w_raw[:, slot, :], src).then_inc(w_landed[slot], 16)

                def tokens(b):
                    return slice(b * BT, (b + 1) * BT)

                def load_x(b, c):
                    sp.dma_start(x_sb[:, c, :], x_t[c * P:(c + 1) * P, tokens(b)]).then_inc(x_landed[c], 16)

                for dst, src in ((ident_sb[:, :], ident), (gains_sb[:, :, :], gains)):
                    sp.dma_start(dst, src).then_inc(const_landed, 16)
                for b in range(NB):
                    for i in range(WO_TILES):
                        if b == 0 and i == RING:
                            for c in range(KC):
                                load_x(b, c)
                        load_w(b, i)
                    if b > 0:
                        for c in range(KC + 1):
                            if c < KC:
                                sp.wait_ge(scaled, (b - 1) * KC + c + 1)
                                sp.dma_start(out_t[c * P:(c + 1) * P, tokens(b - 1)], x_sb[:, c, :]).then_inc(stored[c % 2], 16)
                            if c > 0:
                                sp.wait_ge(stored[(c - 1) % 2], 16 * ((b - 1) * (KC // 2) + (c - 1) // 2 + 1))
                                load_x(b, c - 1)
                    for i in range(WO_TILES, WO_TILES + RAW):
                        load_w(b, i)
                    with sp.Fori(0, GROUPS - 1) as g:
                        for k in range(GROUP_TILES):
                            load_w(b, WO_TILES + RAW + k, g)
                    for i in range(TILES - GROUP_TILES + RAW, TILES):
                        load_w(b, i)
                for c in range(KC):
                    sp.wait_ge(scaled, (NB - 1) * KC + c + 1)
                    sp.dma_start(out_t[c * P:(c + 1) * P, tokens(NB - 1)], x_sb[:, c, :]).then_inc(stored[c % 2], 16)
                for n in range(2):
                    sp.wait_ge(stored[n], NB * 16 * (KC // 2))

            @block.gpsimd
            def _(pool):
                for count in (w_ready,):
                    pool.sem_inc(count, AHEAD)
                pool.wait_ge(consts_set, 1)

                def split(b, i, dst, g=0):
                    raw = i % RAW
                    pool.wait_ge(w_landed[raw], b * (16 * TILES // RAW) + g * (16 * GROUP_TILES // RAW) + 16 * (i // RAW + 1))
                    hi, lo = dst
                    nc.gpsimd.tensor_tensor(hi, w_raw[:, raw, :], ones[:, 0:1].to_broadcast([P, BT]), ALU.mult).then_inc(w_half, 1)
                    pool.wait_ge(w_half, b * TILES + g * GROUP_TILES + i + 1)
                    nc.gpsimd.tensor_tensor(lo, w_raw[:, raw, :], hi.bitcast(F32), ALU.subtract).then_inc(w_ready, 1)

                def in_ring(slot):
                    return w_hi[:, slot, :], w_lo[:, slot, :]

                def second_tile(b, m, g=0):
                    pool.wait_ge(pair_done, AHEAD + b * N_PAIRS + g * G_PAIRS + m + 1)
                    split(b, WO_TILES + GROUP + m, in_ring(m), g)

                for b in range(NB):
                    for i in range(WO_TILES):
                        if b > 0:
                            pool.wait_ge(pair_done, AHEAD + b * N_PAIRS - (KC - 2 * (i + 1) if i < RING else 0))
                        split(b, i, w_slot(i))
                    for f in range(GROUP):
                        pool.wait_ge(wo_done, AHEAD + b * 2 * KC + KC + f + 1)
                        split(b, WO_TILES + f, in_ring(f))
                    with pool.Fori(0, GROUPS - 1) as g:
                        for m in range(GROUP):
                            second_tile(b, m, g)
                        for f in range(GROUP):
                            pool.wait_ge(pair_done, AHEAD + b * N_PAIRS + g * G_PAIRS + GROUP + 2 * (f + 1))
                            split(b, WO_TILES + GROUP_TILES + f, in_ring(f), g)
                    for m in range(GROUP):
                        second_tile(b, m, LAST)

            @block.scalar
            def _(act):
                for count in (rstd_done,):
                    act.sem_inc(count, AHEAD)
                def load_o(b, q):
                    h, c = divmod(q, KC)
                    if q >= O_RING:
                        act.wait_ge(o_ready, AHEAD + b * 2 * KC + q - O_RING + 1)
                    first = b * BT + h * HALF
                    act.dma_start(o_raw[:, q % O_RING, :], o_t[c * P:(c + 1) * P, first:first + HALF]).then_inc(o_landed[q % O_RING], 16)

                def load_first_o(b):
                    act.wait_ge(hidden_ready, AHEAD + b * (GROUPS * GROUP))
                    for q in range(O_RING):
                        load_o(b, q)

                def high_o(b, q):
                    h, c = divmod(q, KC)
                    if q == 0:
                        act.wait_ge(pair_done, AHEAD + b * N_PAIRS - KC)
                    act.wait_ge(o_landed[q % O_RING], (b * 2 * KC // O_RING + q // O_RING + 1) * 16)
                    nc.scalar.activation(act_hi[:, c, half(h)], o_raw[:, q % O_RING, :], ACT.Copy).then_inc(o_half, 1)
                    if q + O_RING - 1 in range(O_RING, 2 * KC):
                        load_o(b, q + O_RING - 1)

                def squared(b, n, dst, src):
                    act.wait_ge(sumsq_step, AHEAD + b * N_SQUARES + n)
                    nc.scalar.activation(dst, src, ACT.Square).then_inc(square_done, 1)

                def deviation(b, n):
                    act.wait_ge(var_done, b * NORMS + n + 1)
                    nc.scalar.activation(small[:, 1, :], small[:, 0, :], ACT.Sqrt).then_inc(dev_done, 1)
                    act.wait_ge(row_done, AHEAD + b * NORMS + n + 1)
                    nc.scalar.activation(rstd[:, :], ps_row[:, :, :].rearrange("p a c -> p (a c)"),
                                         ACT.Copy).then_inc(rstd_done, 1)

                def square_hidden(b, f, g):
                    act.wait_ge(pair_read, AHEAD + b * N_PAIRS + g * G_PAIRS + f + 1)
                    nc.scalar.activation(hidden[:, f % 2, :], hidden[:, f % 2, :], ACT.Square).then_inc(hidden_squared, 1)
                    act.wait_ge(hidden_squared, b * (GROUPS * GROUP) + g * GROUP + f + 1)
                    nc.scalar.activation(r_hi[:, f, :], hidden[:, f % 2, :], ACT.Copy).then_inc(hidden_hi, 1)

                def group(b, g):
                    act.wait_ge(pair_done, AHEAD + b * N_PAIRS + g * G_PAIRS)
                    for f in range(GROUP):
                        square_hidden(b, f, g)

                load_first_o(0)
                for q in range(KC):
                    high_o(0, q)
                act.wait_ge(const_landed, 32)
                for b in range(NB):
                    for h in range(2):
                        for c in range(KC):
                            if h == 0:
                                high_o(b, KC + c)
                            act.wait_ge(wo_read, AHEAD + b * 2 * KC + h * KC + c + 1)
                            squared(b, h * KC + c, square[:, half(h)], x_sb[:, c, half(h)])
                        act.wait_ge(wo_done, AHEAD + b * 2 * KC + (h + 1) * KC)
                        for c in range(KC):
                            nc.scalar.activation(act_hi[:, c, half(h)], x_sb[:, c, half(h)], ACT.Identity,
                                                 scale=gains_sb[:, 0, c:c + 1]).then_inc(act_split, 1)
                    deviation(b, 0)
                    with act.Fori(0, GROUPS - 1) as g:
                        group(b, g)
                    group(b, LAST)
                    if b + 1 < NB:
                        load_first_o(b + 1)
                    for c in range(KC):
                        if b + 1 < NB:
                            high_o(b + 1, c)
                        act.wait_ge(pair_read, AHEAD + b * N_PAIRS + (N_PAIRS - KC + c + 1))
                        squared(b, 2 * KC + c, square[:, :], x_sb[:, c, :])
                    deviation(b, 1)

            @block.vector
            def _(dve):
                for count in (hidden_ready, sumsq_step, pair_read, wo_read, o_ready):
                    dve.sem_inc(count, AHEAD)
                nc.vector.memset(ones[:, :], 1.0).then_inc(consts_set, 1)
                dve.wait_ge(consts_set, 1)
                link = Chain(dve, dve_step, 0, 5 * NORMS * NB)

                def low_o(b, q):
                    h, c = divmod(q, KC)
                    dve.wait_ge(o_half, b * 2 * KC + q + 1)
                    nc.vector.tensor_tensor(act_lo[:, c, half(h)], o_raw[:, q % O_RING, :],
                                            act_hi[:, c, half(h)].bitcast(F32), ALU.subtract).then_inc(o_ready, 1)

                def add_square(b, n, cols, first):
                    dve.wait_ge(square_done, b * N_SQUARES + n + 1)
                    if first:
                        op = nc.vector.tensor_copy(sumsq[:, cols], square[:, cols])
                    else:
                        dve.wait_ge(sumsq_step, AHEAD + b * N_SQUARES + n)
                        op = nc.vector.tensor_tensor(sumsq[:, cols], sumsq[:, cols], square[:, cols], ALU.add)
                    op.then_inc(sumsq_step, 1)

                def reciprocal_root(b, n):
                    dve.wait_ge(sums_done, b * NORMS + n + 1)
                    var, dev, a, r = (small[:, k, :] for k in range(4))
                    nc.vector.tensor_scalar(var, ps_sum[:, n * TT:(n + 1) * TT], 1.0 / D_MODEL, EPS,
                                            ALU.mult, ALU.add).then_inc(var_done, 1)
                    dve.wait_ge(dev_done, b * NORMS + n + 1)
                    link(nc.vector.reciprocal(r, dev))
                    link(nc.vector.tensor_tensor(a, r, r, ALU.mult))
                    link(nc.vector.tensor_tensor(a, a, var, ALU.mult))
                    link(nc.vector.tensor_scalar(a, a, -0.5, 1.5, ALU.mult, ALU.add))
                    link(nc.vector.tensor_tensor(r, r, a, ALU.mult))
                    dve.wait_ge(row_done, AHEAD + b * NORMS + n)
                    nc.vector.tensor_tensor(
                        diag[:, :].rearrange("p (t c) -> p t c", t=TT),
                        ident_sb[:, :].unsqueeze(1).to_broadcast([P, TT, P]),
                        r.unsqueeze(2).to_broadcast([P, TT, P]), ALU.mult).then_inc(diag_done, 1)

                def output_half(b, h, c):
                    k = h * KC + c
                    if h == 0:
                        dve.wait_ge(x_landed[c], 16 * (b + 1))
                    dve.wait_ge(wo_done, AHEAD + b * 2 * KC + k + 1)
                    x = x_sb[:, c, half(h)]
                    nc.vector.tensor_tensor(x, x, w_half_bank(k), ALU.add).then_inc(wo_read, 1)

                def pair(b, n, g):
                    dve.wait_ge(pair_done, AHEAD + b * N_PAIRS + g * G_PAIRS + n + 1)
                    return pairs[:, n % 2, :, :].rearrange("p a c -> p (a c)")

                def add_residual(b, c, g):
                    src = pair(b, GROUP + c, g)
                    nc.vector.tensor_tensor(x_sb[:, c, :], x_sb[:, c, :], src, ALU.add).then_inc(pair_read, 1)

                def hidden_tiles(b, g):
                    dve.wait_ge(rstd_done, AHEAD + b * NORMS + 1)
                    for f in range(GROUP):
                        n = b * (GROUPS * GROUP) + g * GROUP + f
                        src = pair(b, f, g)
                        nc.vector.scalar_tensor_tensor(hidden[:, f % 2, :], src, 0.0, rstd[:, :], ALU.max,
                                                       ALU.mult).then_inc(pair_read, 1)
                        dve.wait_ge(hidden_hi, n + 1)
                        nc.vector.tensor_tensor(r_lo[:, f, :], hidden[:, f % 2, :], r_hi[:, f, :].bitcast(F32),
                                                ALU.subtract).then_inc(hidden_ready, 1)

                for q in range(KC):
                    low_o(0, q)
                dve.wait_ge(const_landed, 32)
                for b in range(NB):
                    for h in range(2):
                        for c in range(KC):
                            output_half(b, h, c)
                            if h == 0:
                                low_o(b, KC + c)
                            if c > 0:
                                add_square(b, h * KC + c - 1, half(h), c == 1)
                        add_square(b, h * KC + KC - 1, half(h), False)
                        for c in range(KC):
                            dve.wait_ge(act_split, b * 2 * KC + h * KC + c + 1)
                            nc.vector.scalar_tensor_tensor(act_lo[:, c, half(h)], x_sb[:, c, half(h)], gains_sb[:, 0, c:c + 1],
                                                           act_hi[:, c, half(h)].bitcast(F32), ALU.mult,
                                                           ALU.subtract).then_inc(act_ready, 1)
                    reciprocal_root(b, 0)
                    with dve.Fori(0, GROUPS - 1) as g:
                        hidden_tiles(b, g)
                        for c in range(KC):
                            add_residual(b, c, g)
                    hidden_tiles(b, LAST)
                    for c in range(KC):
                        add_residual(b, c, LAST)
                        if b + 1 < NB:
                            low_o(b + 1, c)
                        if c > 0:
                            add_square(b, 2 * KC + c - 1, slice(0, BT), c == 1)
                    add_square(b, N_SQUARES - 1, slice(0, BT), False)
                    reciprocal_root(b, 1)
                    dve.wait_ge(rstd_done, AHEAD + b * NORMS + 2)
                    for c in range(KC):
                        nc.vector.scalar_tensor_tensor(x_sb[:, c, :], x_sb[:, c, :], gains_sb[:, 1, c:c + 1], rstd[:, :],
                                                       ALU.mult, ALU.mult).then_inc(scaled, 1)
                link.close()

            @block.tensor
            def _(pe):
                for count in (pair_done, row_done, wo_done):
                    pe.sem_inc(count, AHEAD)
                pe.wait_ge(consts_set, 1)

                def wait_w(b, i, g=0):
                    pe.wait_ge(w_ready, AHEAD + b * TILES + g * GROUP_TILES + i + 1)

                def product(dst, w, cols, a, c, n, first, last):
                    for k, (wk, ak) in enumerate(((0, 0), (0, 1), (1, 0))):
                        op = nc.tensor.matmul(dst, w[wk][:, cols], a[ak][:, c, half(n)],
                                              start=first and k == 0, stop=last and k == 2)
                    return op

                def by_chunk(c):
                    return slice(c * P, (c + 1) * P)

                acts, hiddens = (act_hi, act_lo), (r_hi, r_lo)

                def ring(slot):
                    return w_hi[:, slot, :], w_lo[:, slot, :]

                def sums(b, n):
                    pe.wait_ge(sumsq_step, AHEAD + b * N_SQUARES + (2 + n) * KC)
                    for t in range(TT):
                        last = nc.tensor.matmul(ps_sum[:, n * TT + t:n * TT + t + 1], sumsq[:, t * P:(t + 1) * P],
                                                ones[:, 0:1], start=True, stop=True)
                    last.then_inc(sums_done, 1)

                def row(b, n):
                    pe.wait_ge(diag_done, b * NORMS + n + 1)
                    pe.wait_ge(rstd_done, AHEAD + b * NORMS + n)
                    for h in range(2):
                        last = nc.tensor.matmul(ps_row[:, h, :], ones[:, :], diag[:, half(h)], start=True, stop=True)
                    last.then_inc(row_done, 1)

                def output_projection(b):
                    for h in range(2):
                        for i in range(WO_TILES):
                            k = h * KC + i
                            if h == 0:
                                wait_w(b, i)
                            if k >= 4:
                                pe.wait_ge(wo_read, AHEAD + b * 2 * KC + k - 3)
                            elif k == 0:
                                pe.wait_ge(pair_read, AHEAD + b * N_PAIRS)
                            for c in range(KC):
                                if i == 0:
                                    pe.wait_ge(o_ready, AHEAD + b * 2 * KC + h * KC + c + 1)
                                if b > 0 and k == 0 and c == KC // 2:
                                    sums(b - 1, 1)
                                last = product(w_half_bank(k), w_slot(i), by_chunk(c), acts, c, h, c == 0, c == KC - 1)
                            last.then_inc(wo_done, 1)
                            if b > 0 and k == 0:
                                row(b - 1, 1)

                def group(b, g):
                    def out(n):
                        pe.wait_ge(pair_read, AHEAD + b * N_PAIRS + g * G_PAIRS + n - 1)
                        return pairs[:, n % 2, :, :]

                    def second(banks, m, d, tiles):
                        for f in tiles:
                            for n in range(2):
                                last = product(banks[:, n, :], ring(m), by_chunk(f * 2 + d), hiddens, f, n,
                                               f == 0, f == GROUP - 1)
                        return last

                    first_group = isinstance(g, int) and g == 0
                    for f in range(GROUP):
                        wait_w(b, WO_TILES + f, g)
                        banks = out(f)
                        if first_group and f == 0:
                            for n in range(2):
                                if n == 1:
                                    sums(b, 0)
                                for c in range(KC):
                                    pe.wait_ge(act_ready, b * 2 * KC + n * KC + c + 1)
                                    last = product(banks[:, n, :], ring(f), by_chunk(c), acts, c, n, c == 0, c == KC - 1)
                        else:
                            for c in range(KC):
                                for n in range(2):
                                    last = product(banks[:, n, :], ring(f), by_chunk(c), acts, c, n, c == 0, c == KC - 1)
                        last.then_inc(pair_done, 1)
                        if first_group and f == 0:
                            row(b, 0)
                    for m in range(GROUP):
                        wait_w(b, WO_TILES + GROUP + m, g)
                        ready = b * (GROUPS * GROUP) + g * GROUP
                        if m == 0:
                            pe.wait_ge(hidden_ready, AHEAD + ready + GROUP - 1)
                        n = GROUP + 2 * m
                        banks = [out(n), None]
                        second(banks[0], m, 0, range(GROUP - 1))
                        banks[1] = out(n + 1)
                        second(banks[1], m, 1, range(GROUP - 1))
                        if m == 0:
                            pe.wait_ge(hidden_ready, AHEAD + ready + GROUP)
                        for d in range(2):
                            second(banks[d], m, d, [GROUP - 1]).then_inc(pair_done, 1)

                for b in range(NB):
                    output_projection(b)
                    pe.wait_ge(wo_read, AHEAD + (b + 1) * 2 * KC)
                    group(b, 0)
                    with pe.Fori(1, GROUPS) as g:
                        group(b, g)
                sums(NB - 1, 1)
                row(NB - 1, 1)


def weight_tile(w, cols):
    rows = w.shape[0] // P
    tile = w[:, cols].reshape(rows, P, len(cols)).transpose(1, 0, 2).reshape(P, -1)
    return np.pad(tile, ((0, 0), (0, BT - tile.shape[1])))


def projection_stream(w_in, w_q_up, w_kv_up):
    w = HEADS * HD
    gate0 = 3 * w
    lat0 = gate0 + HEADS
    kr0 = lat0 + Q_LORA + KV_LORA
    padded = np.pad(w_in, ((0, 0), (0, 1)))
    pad = w_in.shape[1]
    misc = np.full(P, pad)
    misc[0:HEADS] = gate0 + np.arange(HEADS)
    misc[MISC_KR1:MISC_KR1 + 16] = kr0 + np.arange(16)
    misc[MISC_KR2:MISC_KR2 + 16] = kr0 + 16 + np.arange(16)
    tiles = [weight_tile(padded, lat0 + i * P + np.arange(P)) for i in range(LATS)]
    tiles.append(weight_tile(padded, misc))
    for i in range(12):
        tiles.append(weight_tile(padded, i * P + np.arange(P)))
    heads = np.arange(HEADS)[:, None] * MLA_K
    plain = (heads + np.arange(HD)).reshape(-1, P)
    r1 = (heads + HD + np.arange(16)).reshape(-1)
    r2 = (heads + HD + 16 + np.arange(16)).reshape(-1)
    parts = [weight_tile(w_q_up, c)[:, :2 * P] for c in (*plain, r1, r2)]
    tiles.append(np.concatenate(parts[0:4], axis=1))
    tiles.append(np.pad(np.concatenate(parts[4:6], axis=1), ((0, 0), (0, BT - 4 * P))))
    heads = np.arange(HEADS)[:, None] * 2 * HD
    tiles.append(w_kv_up[:, np.concatenate([(heads + np.arange(HD)).reshape(-1), (heads + HD + np.arange(HD)).reshape(-1)])])
    return np.ascontiguousarray(np.stack(tiles))


def finish_stream(w_o, w_ff1, w_ff2):
    tiles = [weight_tile(w_o, i * P + np.arange(P)) for i in range(WO_TILES)]
    for g in range(GROUPS):
        tiles += [weight_tile(w_ff1, (g * GROUP + f) * P + np.arange(P)) for f in range(GROUP)]
        rows = w_ff2[g * GROUP * P:(g + 1) * GROUP * P]
        tiles += [weight_tile(rows, m * 2 * P + np.arange(2 * P)) for m in range(GROUP)]
    return np.ascontiguousarray(np.stack(tiles))


def program(nc, x_t, wproj, wfin, gain_mix, gain_lat, gains_fin, gate_bias, cos_t, sin_t, ident, ident_b, masks,
            masks_wide, scale, minus, plus, out_t):
    feat = nc.dram_tensor("feat", [ROWS, SEQ], F32).ap()
    v_fox = nc.dram_tensor("v_fox", [SEQ // P, P, HEADS * HD], F32).ap()
    v_mla = nc.dram_tensor("v_mla", [SEQ // P, P, HEADS * HD], F32).ap()
    aug_q = nc.dram_tensor("aug_q", [HEADS, AUG, SEQ], F32).ap()
    aug_k = nc.dram_tensor("aug_k", [HEADS, AUG, SEQ], F32).ap()
    inv_rows = nc.dram_tensor("inv_rows", [2 * HEADS, SEQ], F32).ap()
    o_t = nc.dram_tensor("o_t", [D_MODEL, SEQ], F32).ap()
    project(nc, x_t, wproj, gain_mix, gain_lat, gate_bias, cos_t, sin_t, ident,
            {"scale": scale, "minus": minus, "plus": plus}, feat, v_fox, v_mla, aug_q, aug_k)
    attend(nc, ident, ident_b, masks, masks_wide, feat, v_fox, v_mla, aug_q, aug_k, inv_rows, o_t)
    finish(nc, x_t, o_t, wfin, gains_fin, ident, out_t)


def shape_constants():
    bf16 = np.dtype(mybir.dt.np(BF16))
    half_rope = ROPE // 2
    inv = (np.float32(ROPE_THETA) ** (-np.arange(half_rope, dtype=np.float32) / np.float32(half_rope))).astype(np.float32)
    ang = inv[:, None] * np.arange(SEQ, dtype=np.float32)[None, :]
    i = np.arange(P)
    causal = i[None, :] <= i[:, None]
    chunked = (i // CHUNK)[None, :] <= (i // CHUNK)[:, None]
    masks = [np.where(m, 0.0, -1e30) for m in (causal, chunked)]
    wide = [np.concatenate([np.full((P, P), -1e30), m.T], axis=1) for m in masks]
    return {
        "cos_t": np.tile(np.cos(ang), (HEADS, 1)).astype(np.float32),
        "sin_t": np.tile(np.sin(ang), (HEADS, 1)).astype(np.float32),
        "ident": np.eye(P, dtype=np.float32),
        "ident_b": np.eye(P).astype(bf16),
        "masks": np.stack(masks, axis=1).astype(bf16),
        "masks_wide": np.stack(wide, axis=1).astype(bf16),
        "scale": np.tile(np.array([[HD ** -0.5, 1.0]], np.float32), (P, 1)),
        "minus": -np.ones((HEADS, 2, SEQ), np.float32),
        "plus": np.ones((HEADS, 2, SEQ), np.float32),
    }


def kernel(**inputs):
    import concourse.bacc as bacc
    from concourse.bass_utils import run_bass_kernel_spmd

    a = {k: np.asarray(v) for k, v in inputs.items()}
    arrays = {
        "x_t": a["x"][0].T,
        "wproj": projection_stream(a["w_in"][0], a["w_q_up"][0], a["w_kv_up"][0]),
        "wfin": finish_stream(a["w_o"][0], a["w_ff1"][0], a["w_ff2"][0]),
        "gain_mix": a["g_mix"][0].reshape(KC, P).T,
        "gain_lat": np.concatenate([a["g_q"][0], a["g_kv"][0]]).reshape(LATS, P).T,
        "gains_fin": np.stack([a["g_mlp"][0].reshape(KC, P), a["g_final"].reshape(KC, P)]).transpose(2, 0, 1),
        "gate_bias": a["b_f"][0][:, None],
        **shape_constants(),
    }
    arrays = {k: np.ascontiguousarray(v) for k, v in arrays.items()}
    nc = bacc.Bacc("TRN2", target_bir_lowering=False, num_devices=1)
    args = {k: nc.dram_tensor(k, v.shape, mybir.dt.from_np(v.dtype), kind="ExternalInput").ap() for k, v in arrays.items()}
    out_t = nc.dram_tensor("out_t", [D_MODEL, SEQ], F32, kind="ExternalOutput").ap()
    program(nc, **args, out_t=out_t)
    got = run_bass_kernel_spmd(nc, [arrays], core_ids=[0]).results[0]["out_t"]
    return np.ascontiguousarray(got.T)[None]
```
